# Optimizing a Trainium2 kernel written in Bass

```python
import jax, jax.numpy as jnp
from jax import lax
import numpy as np

D_MODEL = 1024
BATCH = 1
SEQ = 128
DEPTH = 2
DEC_BATCH = 1
DEC_SEQ = 256
PAST_LEN = 128

GRID_W = 64
D_FOURIER = 256
N_FOURIER_GROUPS = 4
FOURIER_GROUP_DIM = D_FOURIER // N_FOURIER_GROUPS
NA_HEADS = 8
NA_HEAD_DIM = 64
D_NA = NA_HEADS * NA_HEAD_DIM
NA_MAX_ROWS = 8
NA_COLS = 16
NA_COL_BLOCK = 16
NA_BAND = 32
POOL_WINDOWS = (2, 4, 8, 16)
N_POOL_GROUPS = 4
D_POOL = 256
POOL_GROUP_DIM = D_POOL // N_POOL_GROUPS
D_IN = D_FOURIER + 3 * D_NA + D_POOL
IN_SPLITS = (D_FOURIER, D_FOURIER + D_NA, D_FOURIER + 2 * D_NA, D_FOURIER + 3 * D_NA)
N_BRANCHES = 3
PEER_HEADS = 8
PEER_N_KEYS = 128
PEER_N_EXPERTS = PEER_N_KEYS * PEER_N_KEYS
PEER_D_KEY = 256
PEER_TOPK = 16
TOKEN_BLOCK = 128
DENSE_BLOCK_THRESHOLD = 2048
EPS = 1e-6
NEG_INF = -1e30

kernel_name = "hybrid_dit_fnet_natten_pool_peer_step"

def rmsnorm(x, g):
    xf = x.astype(jnp.float32)
    y = xf * lax.rsqrt(jnp.mean(xf * xf, axis=-1, keepdims=True) + EPS)
    return (y * g.astype(jnp.float32)).astype(x.dtype)

def adaln(cvec, w_ada, b_ada):
    m = jax.nn.silu(cvec) @ w_ada + b_ada
    return [t[:, None, :] for t in jnp.split(m, 6, axis=-1)]

def fourier_mix(zf):
    B, L, _ = zf.shape
    z = zf.astype(jnp.float32).reshape(B, L, N_FOURIER_GROUPS, FOURIER_GROUP_DIM)
    r = jnp.fft.fft2(z, axes=(1, 3), norm="ortho").real
    return r.reshape(B, L, D_FOURIER).astype(zf.dtype)

def pool_mix(zp, w_pool_grp, pool_scale):
    B, L, _ = zp.shape
    z = zp.astype(jnp.float32).reshape(B, L, N_POOL_GROUPS, POOL_GROUP_DIM)
    cs = jnp.concatenate([jnp.zeros((B, 1, N_POOL_GROUPS, POOL_GROUP_DIM), jnp.float32),
                          jnp.cumsum(z, axis=1)], axis=1)
    t = jnp.arange(L)[:, None]
    half = jnp.array([w // 2 for w in POOL_WINDOWS], dtype=jnp.int32)[None, :]
    lo = jnp.clip(t - half, 0, L)
    hi = jnp.clip(t + half, 0, L)
    gi = jnp.arange(N_POOL_GROUPS)[None, :]
    win_sum = cs[:, hi, gi] - cs[:, lo, gi]
    mean = win_sum / (hi - lo).astype(jnp.float32)[None, :, :, None]
    d = (mean - z).astype(zp.dtype)
    y = jnp.einsum('blgc,gce->blge', d, w_pool_grp) * pool_scale.reshape(N_POOL_GROUPS, POOL_GROUP_DIM)
    return y.reshape(B, L, D_POOL)

def _attend(q, k, v):
    s = jnp.einsum('bqhd,bhkd->bhqk', q, k).astype(jnp.float32)
    p = jax.nn.softmax(s, axis=-1).astype(v.dtype)
    return jnp.einsum('bhqk,bhkd->bqhd', p, v)

def dense_attention(q, k, v):
    B, L, H, dh = q.shape
    if k.shape[2] < DENSE_BLOCK_THRESHOLD:
        return _attend(q, k, v)
    qb = q.reshape(B, L // TOKEN_BLOCK, TOKEN_BLOCK, H, dh).transpose(1, 0, 2, 3, 4)
    ob = lax.map(lambda qq: _attend(qq, k, v), qb)
    return ob.transpose(1, 0, 2, 3, 4).reshape(B, L, H, dh)

def neighbourhood_attention(q, k, v, ck, cv, rel_bias):
    B, N, H, dh = q.shape
    rows = N // GRID_W
    wr = min(NA_MAX_ROWS, rows)
    ncb = GRID_W // NA_COL_BLOCK
    r = jnp.arange(rows)
    kr = jnp.clip(r - wr // 2, 0, rows - wr)[:, None] + jnp.arange(wr)[None, :]
    qc = jnp.arange(ncb)[:, None] * NA_COL_BLOCK + jnp.arange(NA_COL_BLOCK)[None, :]
    kcb = (jnp.clip(jnp.arange(ncb) * NA_COL_BLOCK - NA_COL_BLOCK // 2, 0, GRID_W - NA_BAND)[:, None]
           + jnp.arange(NA_BAND)[None, :])
    cstart = jnp.clip(qc - NA_COLS // 2, 0, GRID_W - NA_COLS)
    valid = (kcb[:, None, :] >= cstart[:, :, None]) & (kcb[:, None, :] < cstart[:, :, None] + NA_COLS)
    nl = wr * NA_BAND
    valid = jnp.broadcast_to(valid[:, :, None, :], (ncb, NA_COL_BLOCK, wr, NA_BAND)).reshape(
        ncb, 1, NA_COL_BLOCK, nl)
    dr = kr - r[:, None] + (NA_MAX_ROWS - 1)
    dc = jnp.clip(kcb[:, None, :] - qc[:, :, None], -(NA_COLS - 1), NA_COLS - 1) + (NA_COLS - 1)
    bias = rel_bias[:, dr[:, None, None, :, None], dc[None, :, :, None, :]]
    bias = bias.transpose(1, 2, 0, 3, 4, 5).reshape(rows, ncb, H, NA_COL_BLOCK, nl)
    qg = q.reshape(B, rows, ncb, NA_COL_BLOCK, H, dh)
    ridx = kr[:, None, :, None]
    cidx = kcb[None, :, None, :]
    kg = k.reshape(B, rows, GRID_W, H, dh)[:, ridx, cidx].reshape(B, rows, ncb, nl, H, dh)
    vg = v.reshape(B, rows, GRID_W, H, dh)[:, ridx, cidx].reshape(B, rows, ncb, nl, H, dh)
    s_loc = jnp.einsum('brjqhd,brjkhd->brjhqk', qg, kg).astype(jnp.float32) + bias.astype(jnp.float32)
    s_loc = jnp.where(valid, s_loc, NEG_INF)
    s_ctx = jnp.einsum('brjqhd,bhkd->brjhqk', qg, ck).astype(jnp.float32)
    p = jax.nn.softmax(jnp.concatenate([s_loc, s_ctx], axis=-1), axis=-1).astype(v.dtype)
    o = (jnp.einsum('brjhqk,brjkhd->brjqhd', p[..., :nl], vg)
         + jnp.einsum('brjhqk,bhkd->brjqhd', p[..., nl:], cv))
    return o.reshape(B, N, H * dh)

def peer_ffn(h, peer_wq, peer_keys, peer_u, peer_v):
    B, L, D = h.shape
    q = (h @ peer_wq).reshape(B, L, PEER_HEADS, 2, PEER_D_KEY // 2)
    s = jnp.einsum('blhpc,hpnc->blhpn', q, peer_keys).astype(jnp.float32)
    sv, si = lax.top_k(s, PEER_TOPK)
    cand = (sv[..., 0, :, None] + sv[..., 1, None, :]).reshape(B, L, PEER_HEADS, PEER_TOPK * PEER_TOPK)
    cid = (si[..., 0, :, None] * PEER_N_KEYS + si[..., 1, None, :]).reshape(
        B, L, PEER_HEADS, PEER_TOPK * PEER_TOPK)
    top, pos = lax.top_k(cand, PEER_TOPK)
    eid = jnp.take_along_axis(cid, pos, axis=-1)
    g = jax.nn.softmax(top, axis=-1).astype(h.dtype)
    nb = (B * L) // TOKEN_BLOCK
    hb = h.reshape(nb, TOKEN_BLOCK, D)
    eb = eid.reshape(nb, TOKEN_BLOCK, PEER_HEADS * PEER_TOPK)
    gb = g.reshape(nb, TOKEN_BLOCK, PEER_HEADS * PEER_TOPK)

    def expert_block(args):
        hh, ee, gg = args
        act = jax.nn.gelu(jnp.einsum('tkd,td->tk', peer_u[ee], hh))
        return jnp.einsum('tk,tkd->td', gg * act, peer_v[ee])

    out = lax.map(expert_block, (hb, eb, gb))
    return out.reshape(B, L, D)

def trunk_layer(x, cvec, ctx_kv, w_ada, b_ada, g_attn, g_ffn, w_in, w_fourier, w_pool_grp, pool_scale,
                w_pool, rel_bias, w_attn, w_gate, b_gate, w_out, peer_wq, peer_keys, peer_u, peer_v):
    shift1, scale1, gate1, shift2, scale2, gate2 = adaln(cvec, w_ada, b_ada)
    B, L, _ = x.shape
    h = rmsnorm(x, g_attn) * (1 + scale1) + shift1
    zf, zq, zk, zv, zp = jnp.split(h @ w_in, IN_SPLITS, axis=-1)
    q = zq.reshape(B, L, NA_HEADS, NA_HEAD_DIM) * (NA_HEAD_DIM ** -0.5)
    k = zk.reshape(B, L, NA_HEADS, NA_HEAD_DIM)
    v = zv.reshape(B, L, NA_HEADS, NA_HEAD_DIM)
    if ctx_kv is None:
        kc = k.transpose(0, 2, 1, 3)
        vc = v.transpose(0, 2, 1, 3)
        attn = dense_attention(q, kc, vc).reshape(B, L, D_NA)
        state = (kc, vc)
    else:
        attn = neighbourhood_attention(q, k, v, ctx_kv[0], ctx_kv[1], rel_bias)
        state = None
    branch_f = fourier_mix(zf) @ w_fourier
    branch_a = attn @ w_attn
    branch_p = pool_mix(zp, w_pool_grp, pool_scale) @ w_pool
    gf, ga, gp = jnp.split(jax.nn.sigmoid(h @ w_gate + b_gate), N_BRANCHES, axis=-1)
    x = x + gate1 * ((gf * branch_f + ga * branch_a + gp * branch_p) @ w_out)
    h2 = rmsnorm(x, g_ffn) * (1 + scale2) + shift2
    x = x + gate2 * peer_ffn(h2, peer_wq, peer_keys, peer_u, peer_v)
    return x, state

def setup_inputs(seed: int = 0) -> dict:
    key = jax.random.key(seed)
    ks = jax.random.split(key, 32)

    def nrm(k, shape, scale):
        return jax.random.normal(k, shape, jnp.float32) * scale

    return {
        "x_prompt": nrm(ks[0], (BATCH, SEQ, D_MODEL), 1.0),
        "x_sample": nrm(ks[1], (DEC_BATCH, DEC_SEQ, D_MODEL), 1.0),
        "cache_k": nrm(ks[2], (DEC_BATCH, DEPTH, NA_HEADS, PAST_LEN, NA_HEAD_DIM), 1.0),
        "cache_v": nrm(ks[3], (DEC_BATCH, DEPTH, NA_HEADS, PAST_LEN, NA_HEAD_DIM), 1.0),
        "c": nrm(ks[4], (DEC_BATCH, D_MODEL), 1.0),
        "c_ctx": nrm(ks[5], (D_MODEL,), 1.0),
        "w_ada": nrm(ks[6], (DEPTH, D_MODEL, 6 * D_MODEL), D_MODEL ** -0.5),
        "b_ada": nrm(ks[7], (DEPTH, 6 * D_MODEL), 0.02),
        "g_attn": 1.0 + nrm(ks[8], (DEPTH, D_MODEL), 0.02),
        "g_ffn": 1.0 + nrm(ks[9], (DEPTH, D_MODEL), 0.02),
        "w_in": nrm(ks[10], (DEPTH, D_MODEL, D_IN), D_MODEL ** -0.5),
        "w_fourier": nrm(ks[11], (DEPTH, D_FOURIER, D_MODEL), D_FOURIER ** -0.5),
        "w_pool_grp": nrm(ks[12], (DEPTH, N_POOL_GROUPS, POOL_GROUP_DIM, POOL_GROUP_DIM), POOL_GROUP_DIM ** -0.5),
        "pool_scale": 1.0 + nrm(ks[13], (DEPTH, D_POOL), 0.02),
        "w_pool": nrm(ks[14], (DEPTH, D_POOL, D_MODEL), D_POOL ** -0.5),
        "rel_bias": nrm(ks[15], (DEPTH, NA_HEADS, 2 * NA_MAX_ROWS - 1, 2 * NA_COLS - 1), 0.1),
        "w_attn": nrm(ks[16], (DEPTH, D_NA, D_MODEL), D_NA ** -0.5),
        "w_gate": nrm(ks[17], (DEPTH, D_MODEL, N_BRANCHES * D_MODEL), D_MODEL ** -0.5),
        "b_gate": nrm(ks[18], (DEPTH, N_BRANCHES * D_MODEL), 0.02),
        "w_out": nrm(ks[19], (DEPTH, D_MODEL, D_MODEL), D_MODEL ** -0.5),
        "peer_wq": nrm(ks[20], (DEPTH, D_MODEL, PEER_HEADS * PEER_D_KEY), D_MODEL ** -0.5),
        "peer_keys": nrm(ks[21], (DEPTH, PEER_HEADS, 2, PEER_N_KEYS, PEER_D_KEY // 2), (PEER_D_KEY // 2) ** -0.5),
        "peer_u": nrm(ks[22], (DEPTH, PEER_N_EXPERTS, D_MODEL), D_MODEL ** -0.5),
        "peer_v": nrm(ks[23], (DEPTH, PEER_N_EXPERTS, D_MODEL), PEER_HEADS ** -0.5),
        "g_final": 1.0 + nrm(ks[24], (D_MODEL,), 0.02),
    }

def reference(x_prompt, x_sample, cache_k, cache_v, c, c_ctx, w_ada, b_ada, g_attn, g_ffn, w_in,
              w_fourier, w_pool_grp, pool_scale, w_pool, rel_bias, w_attn, w_gate, b_gate, w_out,
              peer_wq, peer_keys, peer_u, peer_v, g_final):
    cctx = c_ctx[None, :]
    xp = x_prompt
    xs = x_sample
    new_ks = []
    new_vs = []
    for l in range(DEPTH):
        lw = (w_ada[l], b_ada[l], g_attn[l], g_ffn[l], w_in[l], w_fourier[l], w_pool_grp[l],
              pool_scale[l], w_pool[l], rel_bias[l], w_attn[l], w_gate[l], b_gate[l], w_out[l],
              peer_wq[l], peer_keys[l], peer_u[l], peer_v[l])
        xp, (kl, vl) = trunk_layer(xp, cctx, None, *lw)
        new_ks.append(kl)
        new_vs.append(vl)
        xs, _ = trunk_layer(xs, c, (cache_k[:, l], cache_v[:, l]), *lw)
    y_prompt = rmsnorm(xp, g_final)
    y_sample = rmsnorm(xs, g_final)
    new_k = jnp.stack(new_ks, axis=1)
    new_v = jnp.stack(new_vs, axis=1)
    return (y_prompt, y_sample, new_k, new_v)


_drawn_inputs = setup_inputs


def setup_inputs(seed=0):
    import zlib

    import numpy as np

    out = dict(_drawn_inputs(seed))
    spreads = {}
    factors = {'pool_scale': 3.218, 'rel_bias': 4.103, 'b_gate': 4.513, 'g_final': 7.979, 'g_ffn': 3.432}
    for name, (base, spread) in spreads.items():
        noise = np.random.default_rng([zlib.crc32(name.encode()), seed]).standard_normal(out[name].shape)
        drawn = base * np.exp(spread * noise) if base else spread * noise
        out[name] = __import__('jax').numpy.asarray(drawn.astype(out[name].dtype))
    for name, factor in factors.items():
        out[name] = (out[name] * factor).astype(out[name].dtype)
    return out
```

```python
from contextlib import ExitStack

import concourse.bass as bass
from concourse import mybir
from concourse.alu_op_type import AluOpType as ALU

F32 = mybir.dt.float32
F32R = mybir.dt.float32r
U32 = mybir.dt.uint32
ACT = mybir.ActivationFunctionType
AX = mybir.AxisListType.X

P = 128
D = 1024
DEPTH = 2
TB = 3
T = TB * P
KC = D // P
HEADS = 8
DH = 64
GRID = 64
RB = 15 * 31
KEYS = 128
TOPK = 16
EPS = 1e-6
UW = 1024
HB = 512
SLOTS = 4

U_ADA = 0
U_IN = U_ADA + 6 * KC
U_GF = U_IN + 2 * KC
U_WF = U_GF + KC
U_GP = U_WF + 2
U_WP = U_GP + KC
U_GA = U_WP + 2
U_WA = U_GA + KC
U_OUT = U_WA + 4
U_Q = U_OUT + KC
U_PEER = U_Q + 2 * KC
UNITS = U_PEER + 2 * KEYS
PAIRS = UNITS // 2
assert UNITS % SLOTS == 0

C_ADA = 0
C_IN = C_ADA + 12
C_GF = C_IN + 12
C_WF = C_GF + 6
C_GP = C_WF + 6
C_WP = C_GP + 6
C_GA = C_WP + 6
C_WA = C_GA + 6
C_OUT = C_WA + 6
C_Q = C_OUT + 6
C_V = C_Q + 12
ACCS = C_V + 6
assert ACCS % 6 == 0

STEPS = HEADS * TB
X_MOD = 0
X_HT = X_MOD + 8
X_ZT = X_HT + KC
X_FC = X_ZT + 10
X_FP = X_FC + TB
X_PD = X_FP + 2
X_PY = X_PD + 2
X_ATT = X_PY + 2
X_MT = X_ATT + 3 * STEPS
X_H2 = X_MT + KC
X_QT = X_H2 + KC
X_SC = X_QT + 16
X_IT = X_SC + 12
X_G = X_IT + TB
X_U = X_G + T // 4
AUXS = X_U + KEYS
assert AUXS % 2 == 0

GT = 16
GN = 8
GGROUPS = KEYS // GN
BODY = 2 * GN


def att_order():
    order = []
    for i in range(STEPS + 2):
        order.append([(kind, j) for kind, j in (("s", i), ("t", i - 1), ("v", i - 2)) if 0 <= j < STEPS])
    return order


ATT = att_order()
ATT_USE = {}
for _step in ATT:
    for _u in _step:
        ATT_USE[_u] = X_ATT + len(ATT_USE)


def build(nc, a, o):
    with ExitStack() as ctx:
        def sb(name, shape, dt=F32):
            return ctx.enter_context(nc.sbuf_tensor(name, shape, dt))

        def sem(name):
            return ctx.enter_context(nc.semaphore(name))

        X = sb("x", [P, TB, D])
        Z = sb("z", [P, TB, 2 * D])
        Zf = Z[:].rearrange("p t n -> p (t n)")
        XN = Zf[:, 0:TB * D].rearrange("p (t n) -> p t n", t=TB)
        HRAW = Zf[:, TB * D:2 * TB * D].rearrange("p (k t) -> p k t", k=KC)
        M = Z[:, :, 0:D]
        GCH = Zf.rearrange("p (s t n) -> p s t n", s=2, n=GN)
        LTh = sb("lt_hi", [P, KC, T], F32R)
        LTl = sb("lt_lo", [P, KC, T], F32R)
        BTh = sb("bt_hi", [P, 8, T], F32R)
        BTl = sb("bt_lo", [P, 8, T], F32R)
        raw = sb("raw", [P, SLOTS, UW])
        whi = sb("whi", [P, SLOTS, UW], F32R)
        wlo = sb("wlo", [P, SLOTS, UW], F32R)
        U = sb("u", [P, 13568])

        def part(at, n, **k):
            v = U[:, at:at + n]
            return v.rearrange(*k["r"][:1], **k["r"][1]) if "r" in k else v

        BADA = part(0, 6 * D)
        MODR = part(6 * D, 6 * D)
        GTB = part(0, TB * D, r=("p (t n) -> p t n", dict(t=TB)))
        ZFT = part(0, 2 * T, r=("p (c t) -> p c t", dict(c=2)))
        ZCS = part(768, TB * 512, r=("p (t c n) -> p t c n", dict(t=TB, c=2)))
        DT = part(2304, 2 * T, r=("p (c t) -> p c t", dict(c=2)))
        XTMP = part(0, 512)
        QT = part(3072, 4 * T, r=("p (c t) -> p c t", dict(c=4)))
        KT = part(4608, 4 * T, r=("p (c t) -> p c t", dict(c=4)))
        BIAS = part(6144, 4096, r=("p (b h n) -> p b h n", dict(b=2, h=HEADS)))
        S = part(10240, 768, r=("p (s n) -> p s n", dict(s=2)))
        PR = part(11008, 768, r=("p (s n) -> p s n", dict(s=2)))
        PT = part(11776, 768, r=("p (s k q) -> p s k q", dict(s=2, k=3)))
        KCT = part(12544, 512, r=("p (c n) -> p c n", dict(c=4)))
        VC = part(13056, 512)
        KEYT = part(0, 16 * KEYS, r=("p (h n) -> p h n", dict(h=16)))
        PQT = part(2048, 16 * T, r=("p (h t) -> p h t", dict(h=16)))
        CAND = part(2048, 2048, r=("p (h a b) -> p h a b", dict(h=HEADS, a=TOPK)))
        OH = part(4096, 2048, r=("p (h k a) -> p h k a", dict(h=HEADS, k=TOPK)))
        STG = part(4096, 4096, r=("p (s g t n) -> p s g t n", dict(s=2, g=GGROUPS, t=GT)))
        GATE2 = part(2048, 2048, r=("p (c n) -> p c n", dict(c=2)))
        SV = part(8192, 256, r=("p (h k) -> p h k", dict(h=16)))
        SI = part(8448, 256, r=("p (h k) -> p h k", dict(h=16))).bitcast(U32)
        SIF = part(8704, 256, r=("p (h q k) -> p h q k", dict(h=HEADS, q=2)))
        TOP = part(8960, 128, r=("p (h k) -> p h k", dict(h=HEADS)))
        POS = part(9088, 128, r=("p (h k) -> p h k", dict(h=HEADS))).bitcast(U32)
        PA = part(9216, 128, r=("p (h k) -> p h k", dict(h=HEADS))).bitcast(U32)
        PB = part(9344, 128, r=("p (h k) -> p h k", dict(h=HEADS))).bitcast(U32)
        PAB = part(9472, 256, r=("p (q h k) -> p q h k", dict(q=2, h=HEADS)))
        SEL = part(9728, 384, r=("p (q h k) -> p q h k", dict(q=3, h=HEADS)))
        SELf = part(9728, 384, r=("p (q m) -> p q m", dict(q=3)))
        SELT = part(10112, 3 * T, r=("p (q t) -> p q t", dict(q=3)))
        HOT = part(11264, 1024, r=("p (s q n) -> p s q n", dict(s=4, q=2)))
        ACTB = part(12288, 768, r=("p (s t) -> p s t", dict(s=2)))
        GFIN = part(0, D)

        ident = sb("ident", [P, P])
        iota = sb("iota", [P, P])
        mask = sb("mask", [P, GRID])
        dft_c = sb("dft_c", [P, 256])
        dft_p = sb("dft_p", [P, 2, P])
        dft_s = sb("dft_s", [P, 2, 2, 256])
        pool_p = sb("pool_p", [P, 4, P])
        pool_s = sb("pool_s", [P, 2, 4, 256])
        wpg = sb("wpg", [P, 2, P])
        cond = sb("cond", [P, 2, KC])
        gcol = sb("gcol", [P, 2, KC])
        pscale = sb("pscale", [P, 2])
        modc = sb("modc", [P, 4, 2, KC])
        ms = sb("ms", [P, TB])
        rstd = sb("rstd", [P, TB])
        nhalf = sb("nhalf", [P, TB])
        nmax = sb("nmax", [P, 2])
        rsum = sb("rsum", [P, 2])
        hsum = sb("hsum", [P, HEADS])
        acc = [ctx.enter_context(nc.psum_tensor(f"acc{i}", [P, HB], F32)) for i in range(6)]
        aux = [ctx.enter_context(nc.psum_tensor(f"aux{i}", [P, HB], F32)) for i in range(2)]

        gate_rows = nc.dram_tensor("gate_rows", (2, 2, D), F32, kind="Internal").ap()
        gmat = nc.dram_tensor("gmat", (GGROUPS, P, T * GN), F32, kind="Internal").ap()

        bias_rows = nc.dram_tensor("bias_rows", (DEPTH * HEADS, GRID, RB), F32, kind="Internal").ap()
        toeplitz = nc.dram_tensor("toeplitz", (DEPTH, GRID, HEADS, 7 * GRID), F32, kind="Internal").ap()

        pair_landed = [sem("pair_landed0"), sem("pair_landed1")]
        hi_ready = sem("hi_ready")
        lo_ready = sem("lo_ready")
        unit_used = sem("unit_used")
        acc_done = sem("acc_done")
        acc_free = sem("acc_free")
        aux_done = sem("aux_done")
        aux_free = sem("aux_free")
        const_landed = sem("const_landed")
        x_landed = sem("x_landed")
        start_ready = sem("start_ready")
        bias_rows_stored = sem("bias_rows_stored")
        toeplitz_stored = sem("toeplitz_stored")
        silu_ready = sem("silu_ready")
        layer_free = sem("layer_free")
        bada_landed = sem("bada_landed")
        cols_landed = sem("cols_landed")
        cond_ready = sem("cond_ready")
        modr_ready = sem("modr_ready")
        rows_stored = sem("rows_stored")
        mods_done = sem("mods_done")
        ms_ready = sem("ms_ready")
        rstd_ready = sem("rstd_ready")
        xn_ready = sem("xn_ready")
        ht_ready = sem("ht_ready")
        z_ready = sem("z_ready")
        kv_stored = sem("kv_stored")
        att_landed = sem("att_landed")
        zt_ready = sem("zt_ready")
        zcs_ready = sem("zcs_ready")
        dt_ready = sem("dt_ready")
        four_done = sem("four_done")
        bgate_landed = sem("bgate_landed")
        gate_sum = sem("gate_sum")
        gate_ready = sem("gate_ready")
        gtb_free = sem("gtb_free")
        s_ready = sem("s_ready")
        p_ready = sem("p_ready")
        pn_ready = sem("pn_ready")
        pt_ready = sem("pt_ready")
        att_done = sem("att_done")
        m_ready = sem("m_ready")
        gate1_landed = sem("gate1_landed")
        out_done = sem("out_done")
        keys_landed = sem("keys_landed")
        pq_ready = sem("pq_ready")
        pqt_ready = sem("pqt_ready")
        top_ready = sem("top_ready")
        exp_ready = sem("exp_ready")
        sel_ready = sem("sel_ready")
        selt_ready = sem("selt_ready")
        hot_ready = sem("hot_ready")
        stage_ready = sem("stage_ready")
        stage_stored = [sem("stage_stored0"), sem("stage_stored1")]
        gate2_landed = sem("gate2_landed")
        group_landed = [sem("group_landed0"), sem("group_landed1")]
        act_ready = sem("act_ready")
        w_ready = sem("w_ready")
        gfin_landed = sem("gfin_landed")
        y_ready = sem("y_ready")
        y_stored = sem("y_stored")

        NSTG = T // GT
        block = ctx.enter_context(nc.Block())

        def accum(use):
            return acc[use % 6]

        @block.sync
        def _(sp):
            for t, src in ((ident, "ident"), (iota, "iota"), (mask, "mask"), (dft_c, "dft_c"), (dft_p, "dft_p"),
                           (dft_s, "dft_s"), (pool_p, "pool_p"), (pool_s, "pool_s"), (cond, "cond")):
                sp.dma_start(t[:], a[src]).then_inc(const_landed, 16)
            sp.dma_start(X[:, 0, :], a["x_prompt"]).then_inc(x_landed, 16)
            sp.dma_start(X[:, 1:3, :], a["x_sample"].rearrange("(b p) n -> p b n", p=P)).then_inc(x_landed, 16)
            with sp.Fori(0, DEPTH) as l:
                def pairs(u0, u1, source):
                    for i, u in enumerate(range(u0, u1, 2)):
                        q = u // 2
                        sp.wait_ge(lo_ready, l * UNITS + u + 2)
                        sp.dma_start(raw[:, u % SLOTS:u % SLOTS + 2, :], source(i)).then_inc(pair_landed[q % 2], 16)

                def rows(w, n0):
                    v = w[bass.ds(l, 1)].rearrange("o (k s p) n -> p (o k) s n", p=P, s=2)
                    return lambda i: v[:, i, :, n0:n0 + UW]

                sp.wait_ge(layer_free, l + 1)
                sp.dma_start(BADA, a["b_ada"][bass.ds(l, 1)].to_broadcast([P, 6 * D])).then_inc(bada_landed, 16)
                sp.dma_start(gcol[:], a["gcol"][bass.ds(l, 1)].rearrange("o p s k -> (o p) s k")).then_inc(cols_landed, 16)
                sp.dma_start(pscale[:], a["pool_scale"][bass.ds(l, 1)].rearrange("o p s -> (o p) s")).then_inc(cols_landed, 16)
                for g in range(4):
                    sp.dma_start(wpg[64 * (g % 2):64 * (g % 2) + 64, g // 2, 64 * (g % 2):64 * (g % 2) + 64],
                                 a["w_pool_grp"][bass.ds(l, 1), g].rearrange("o c e -> (o c) e")).then_inc(cols_landed, 16)
                for p in range(6):
                    pairs(U_ADA + p * KC, U_ADA + (p + 1) * KC, rows(a["w_ada"], p * D))
                    if p == 3:
                        sp.wait_ge(modr_ready, l * 6 + 3)
                        for s in range(2):
                            sp.dma_start(gate_rows[0, s:s + 1, :], MODR[64 * s:64 * s + 1, 2 * D:3 * D]).then_inc(rows_stored, 16)
                pairs(U_IN, U_IN + 4, rows(a["w_in"], 0))
                sp.wait_ge(modr_ready, l * 6 + 6)
                for s in range(2):
                    sp.dma_start(gate_rows[1, s:s + 1, :], MODR[64 * s:64 * s + 1, 5 * D:6 * D]).then_inc(rows_stored, 16)
                sp.wait_ge(mods_done, l + 1)
                sp.wait_ge(rows_stored, l * 64 + 64)
                sp.wait_ge(toeplitz_stored, 16 * DEPTH * HEADS)
                for b in range(2):
                    for r2 in range(2):
                        r = 2 * b + r2
                        sp.dma_start(BIAS[64 * r2:64 * r2 + 64, b],
                                     toeplitz[bass.ds(l, 1), :, :, (3 - r) * GRID:(7 - r) * GRID]
                                     .rearrange("o q h n -> (o q) h n")).then_inc(att_landed, 16)
                sp.dma_start(KCT, a["cache_k"][bass.ds(l, 1)].rearrange("o p c n -> (o p) c n")).then_inc(att_landed, 16)
                sp.dma_start(VC.rearrange("p (h d) -> p h d", h=HEADS),
                             a["cache_v"][bass.ds(l, 1)].rearrange("o h k d -> (o k) h d")).then_inc(att_landed, 16)
                v = a["w_in"][bass.ds(l, 1)].rearrange("o (k s p) n -> p (o k) s n", p=P, s=2)
                pairs(U_IN + 4, U_IN + 8, lambda i: v[:, i + 2, :, 0:UW])
                pairs(U_IN + 8, U_IN + 16, rows(a["w_in"], UW))
                pairs(U_GF, U_GF + 4, rows(a["w_gate"], 0))
                sp.wait_ge(z_ready, l + 1)
                for n0, out in ((768, o["new_k"]), (1280, o["new_v"])):
                    sp.dma_start(out[bass.ds(l, 1)].rearrange("o h t d -> (o t) h d"),
                                 Z[:, 0, n0:n0 + 512].rearrange("p (h d) -> p h d", h=HEADS)).then_inc(kv_stored, 16)
                sp.wait_ge(four_done, l + 1)
                sp.dma_start(GTB, a["b_gate"][bass.ds(l, 1), 0:1, :].to_broadcast([P, TB, D])).then_inc(bgate_landed, 16)
                wg = a["w_gate"][bass.ds(l, 1)].rearrange("o (k s p) n -> p (o k) s n", p=P, s=2)
                pairs(U_GF + 4, U_WF, lambda i: wg[:, i + 2, :, 0:UW])
                pairs(U_WF, U_GP, rows(a["w_fourier"], 0))
                pairs(U_GP, U_GP + 4, rows(a["w_gate"], 2 * UW))
                sp.wait_ge(gtb_free, l * 3 + 1)
                sp.dma_start(GTB, a["b_gate"][bass.ds(l, 1), 2:3, :].to_broadcast([P, TB, D])).then_inc(bgate_landed, 16)
                pairs(U_GP + 4, U_WP, lambda i: wg[:, i + 2, :, 2 * UW:3 * UW])
                pairs(U_WP, U_GA, rows(a["w_pool"], 0))
                pairs(U_GA, U_GA + 4, rows(a["w_gate"], UW))
                sp.wait_ge(gtb_free, l * 3 + 2)
                sp.dma_start(GTB, a["b_gate"][bass.ds(l, 1), 1:2, :].to_broadcast([P, TB, D])).then_inc(bgate_landed, 16)
                pairs(U_GA + 4, U_WA, lambda i: wg[:, i + 2, :, UW:2 * UW])
                pairs(U_WA, U_OUT, rows(a["w_attn"], 0))
                sp.wait_ge(att_done, l + 1)
                for s in range(2):
                    sp.dma_start(Z[:, s, D:2 * D], gate_rows[0, s:s + 1, :].to_broadcast([P, D])).then_inc(gate1_landed, 16)
                pairs(U_OUT, U_Q, rows(a["w_out"], 0))
                pairs(U_Q, U_Q + 4, rows(a["peer_wq"], 0))
                sp.wait_ge(out_done, l + 1)
                sp.dma_start(KEYT, a["keys"][bass.ds(l, 1)].rearrange("o p h n -> (o p) h n")).then_inc(keys_landed, 16)
                wq = a["peer_wq"][bass.ds(l, 1)].rearrange("o (k s p) n -> p (o k) s n", p=P, s=2)
                pairs(U_Q + 4, U_Q + 8, lambda i: wq[:, i + 2, :, 0:UW])
                pairs(U_Q + 8, U_PEER, rows(a["peer_wq"], UW))
                with sp.Fori(0, NSTG // 2) as g:
                    for s in range(2):
                        sp.wait_ge(stage_ready, l * NSTG + g * 2 + s + 1)
                        sp.dma_start(gmat.rearrange("g p (t n) -> p g t n", n=GN)[:, :, bass.ds(g * (2 * GT) + s * GT, GT), :]
                                     .rearrange("p g t n -> p g (t n)"),
                                     STG[:, s].rearrange("p g t n -> p g (t n)")).then_inc(stage_stored[s], 16)
                for s in range(2):
                    sp.wait_ge(stage_stored[s], l * (8 * NSTG) + 8 * NSTG)
                for s in range(2):
                    sp.dma_start(GATE2[:, s, :], gate_rows[1, s:s + 1, :].to_broadcast([P, D])).then_inc(gate2_landed, 16)
                with sp.Fori(0, KEYS // BODY) as i:
                    for k in range(BODY // 2):
                        n = 2 * k
                        if n % GN == 0:
                            s = n // GN
                            sp.wait_ge(w_ready, l * KEYS + i * BODY + n - (GN if s else 0) + 1)
                            sp.dma_start(GCH[:, s].rearrange("p t n -> p (t n)"),
                                         gmat[bass.ds(i * 2 + s, 1)].rearrange("o p n -> (o p) n")).then_inc(group_landed[s], 16)
                        q = U_PEER + 4 * k
                        sp.wait_ge(lo_ready, l * UNITS + i * (2 * BODY) + q + 2)
                        sp.dma_start(raw[:, 0:2, :], a["ut"][bass.ds(l * KEYS + i * BODY + n, 2)].rearrange("s p n -> p s n")).then_inc(pair_landed[0], 16)
                        sp.wait_ge(lo_ready, l * UNITS + i * (2 * BODY) + q + 4)
                        sp.dma_start(raw[:, 2:4, :], a["peer_v"][bass.ds(l * P, P), bass.ds(i * BODY + n, 2), :]).then_inc(pair_landed[1], 16)
            sp.wait_ge(layer_free, DEPTH + 1)
            sp.dma_start(GFIN, a["g_final"].to_broadcast([P, D])).then_inc(gfin_landed, 16)
            sp.wait_ge(y_ready, 1)
            sp.dma_start(o["y_prompt"], X[:, 0, :]).then_inc(y_stored, 16)
            sp.dma_start(o["y_sample"].rearrange("(b p) n -> p b n", p=P), X[:, 1:3, :]).then_inc(y_stored, 16)
            sp.wait_ge(kv_stored, 32 * DEPTH)
            sp.wait_ge(y_stored, 32)

        @block.gpsimd
        def _(pool):
            pool.sem_inc(lo_ready, SLOTS)
            pool.wait_ge(start_ready, 1)

            def root(n):
                pool.wait_ge(ms_ready, n)
                pool.tensor_tensor(rstd[:], ms[:], nhalf[:], ALU.pow).then_inc(rstd_ready, 1)

            def lo(value, slot):
                pool.wait_ge(hi_ready, value)
                pool.tensor_tensor(wlo[:, slot], raw[:, slot], whi[:, slot].bitcast(F32), ALU.subtract).then_inc(lo_ready, 1)

            with pool.Fori(0, DEPTH) as l:
                root(l * 2 + 1)
                with pool.Fori(0, (U_Q + 4) // 4) as i:
                    for s in range(SLOTS):
                        lo(l * UNITS + i * 4 + s + 1, s)
                root(l * 2 + 2)
                with pool.Fori(0, (UNITS - U_Q - 4) // 4) as i:
                    for s in range(SLOTS):
                        lo(l * UNITS + i * 4 + U_Q + 4 + s + 1, s)
            root(2 * DEPTH + 1)

        @block.scalar
        def _(act):
            rb = a["rel_bias"].rearrange("l h r c -> (l h) (r c)")
            act.dma_start(bias_rows, rb.rearrange("n (o c) -> n o c", o=1).to_broadcast([DEPTH * HEADS, GRID, RB]))\
               .then_inc(bias_rows_stored, 16)
            act.wait_ge(bias_rows_stored, 16)
            for n in range(DEPTH):
                for h in range(HEADS):
                    src = bass.AP(tensor=bias_rows.tensor, offset=(n * HEADS + h) * GRID * RB + 4 * 31 + 15,
                                  ap=[[RB - 1, GRID], [31, 7], [1, GRID]])
                    act.dma_start(toeplitz[n, :, h, :].rearrange("q (r k) -> q r k", r=7), src).then_inc(toeplitz_stored, 16)
            act.wait_ge(const_landed, 16 * 9)
            act.activation(cond[:], cond[:], ACT.Silu).then_inc(silu_ready, 1)
            with act.Fori(0, DEPTH) as l:
                def hi(u):
                    q = u // 2
                    act.wait_ge(pair_landed[q % 2], l * (8 * PAIRS) + 16 * (q // 2 + 1))
                    act.wait_ge(unit_used, l * UNITS + u + 1)
                    act.activation(whi[:, u % SLOTS], raw[:, u % SLOTS], ACT.Copy).then_inc(hi_ready, 1)

                for u in range(0, U_GF):
                    hi(u)

                def exps(i):
                    n = P if i % TB == 0 else T
                    act.wait_ge(s_ready, l * STEPS + i + 1)
                    if i >= 2:
                        act.wait_ge(pt_ready, l * STEPS + i - 1)
                    act.activation(PR[:, i % 2, 0:n], S[:, i % 2, 0:n], ACT.Exp, bias=nmax[:, i % 2:i % 2 + 1],
                                   accum_out=rsum[:, i % 2:i % 2 + 1]).then_inc(p_ready, 1)

                def sigmoid(g):
                    for t in range(TB):
                        act.wait_ge(gate_sum, l * 9 + 3 * g + t + 1)
                        act.activation(GTB[:, t], GTB[:, t], ACT.Sigmoid).then_inc(gate_ready, 1)

                for u in range(U_GF, U_OUT):
                    i = u - U_GF
                    hi(u)
                    if i < STEPS:
                        exps(i)
                    if u + 1 in (U_GP, U_GA):
                        sigmoid((U_GP, U_GA).index(u + 1))
                sigmoid(2)
                for u in range(U_OUT, U_PEER):
                    hi(u)
                for t in range(TB):
                    act.wait_ge(top_ready, l * TB + t + 1)
                    act.activation(SEL[:, 2], SEL[:, 2], ACT.Exp).then_inc(exp_ready, 1)
                def stages(g, first):
                    for s in range(2):
                        if not first:
                            act.wait_ge(stage_stored[s], l * (8 * NSTG) + g * 16)
                        for j in range(4):
                            use = X_G + 4 * s + j
                            act.wait_ge(aux_done, l * AUXS + g * 8 + use + 1)
                            act.activation(STG[:, s, :, 4 * j:4 * j + 4, :].rearrange("p g t n -> p t g n"),
                                           aux[use % 2][:].rearrange("p (t g n) -> p t g n", t=4, n=GN), ACT.Copy)\
                               .then_inc(aux_free, 1)
                        act.drain().then_inc(stage_ready, 1)

                stages(0, True)
                with act.Fori(1, NSTG // 2) as g:
                    stages(g, False)
                with act.Fori(0, KEYS // 2) as k:
                    for j in range(4):
                        act.wait_ge(pair_landed[j // 2], l * (8 * PAIRS) + k * 16 + (4 * U_PEER + 16))
                        act.wait_ge(unit_used, l * UNITS + k * 4 + U_PEER + j + 1)
                        act.activation(whi[:, j], raw[:, j], ACT.Copy).then_inc(hi_ready, 1)
                    for j in range(2):
                        use = X_U + j
                        act.wait_ge(aux_done, l * AUXS + k * 2 + use + 1)
                        act.wait_ge(w_ready, l * KEYS + k * 2 + j + 1)
                        act.activation(ACTB[:, j], aux[use % 2][:, 0:T], ACT.Gelu_apprx_tanh).then_inc(act_ready, 1)
                        act.wait_ge(act_ready, l * KEYS + k * 2 + j + 1)
                        act.sem_inc(aux_free, 1)

        @block.tensor
        def _(pe):
            pe.sem_inc(unit_used, SLOTS)
            pe.wait_ge(const_landed, 16 * 9)
            with pe.Fori(0, DEPTH) as l:
                def unit(u, lt, chunk, use, first, last):
                    pe.wait_ge(lo_ready, l * UNITS + u + 1 + SLOTS)
                    s = u % SLOTS
                    for t in range(TB):
                        if first:
                            for h in range(2):
                                pe.wait_ge(acc_free, l * ACCS + use + 2 * t + h + 1)
                        lh, ll = (x[:, chunk, t * P:(t + 1) * P] for x in lt)
                        for n, (x, w) in enumerate(((lh, whi), (lh, wlo), (ll, whi))):
                            for h in range(2):
                                mm = pe.matmul(accum(use + 2 * t + h)[:], x, w[:, s, h * HB:(h + 1) * HB],
                                               start=first and n == 0, stop=last and n == 2)
                                if last and n == 2:
                                    mm.then_inc(acc_done, 1)
                    pe.drain().then_inc(unit_used, 1)

                def bank(use):
                    pe.wait_ge(aux_free, l * AUXS + use + 1)
                    return aux[use % 2]

                pe.wait_ge(cond_ready, l + 1)
                for p in range(6):
                    for k in range(KC):
                        u = U_ADA + p * KC + k
                        pe.wait_ge(lo_ready, l * UNITS + u + 1 + SLOTS)
                        for h in range(2):
                            use = C_ADA + 2 * p + h
                            if k == 0:
                                pe.wait_ge(acc_free, l * ACCS + use + 1)
                            for n, (x, w) in enumerate(((LTh, whi), (LTh, wlo), (LTl, whi))):
                                mm = pe.matmul(accum(use)[:], x[:, k, 0:P], w[:, u % SLOTS, h * HB:(h + 1) * HB],
                                               start=(k == 0 and n == 0), stop=(k == KC - 1 and n == 2))
                            if k == KC - 1:
                                mm.then_inc(acc_done, 1)
                        pe.drain().then_inc(unit_used, 1)
                pe.wait_ge(modr_ready, l * 6 + 6)
                for n, p in enumerate((0, 1, 3, 4)):
                    for q in range(2):
                        b = bank(X_MOD + 2 * n + q)
                        for j in range(4):
                            at = p * D + (4 * q + j) * P
                            mm = pe.transpose(b[:, j * P:(j + 1) * P], MODR[:, at:at + P], ident[:])
                        mm.then_inc(aux_done, 1)

                def turn(src, base):
                    for k in range(KC):
                        b = bank(base + k)
                        for t in range(TB):
                            mm = pe.transpose(b[:, t * P:(t + 1) * P], src[:, t, k * P:(k + 1) * P], ident[:])
                        mm.then_inc(aux_done, 1)

                pe.wait_ge(xn_ready, l * 2 + 1)
                turn(XN, X_HT)
                pe.wait_ge(ht_ready, l * 3 + 1)
                for p in range(2):
                    for k in range(KC):
                        unit(U_IN + p * KC + k, (LTh, LTl), k, C_IN + 6 * p, k == 0, k == KC - 1)
                pe.wait_ge(z_ready, l + 1)
                for k in range(10):
                    b = bank(X_ZT + k)
                    for t in range(TB):
                        mm = pe.transpose(b[:, t * P:(t + 1) * P], Z[:, t, k * P:(k + 1) * P], ident[:])
                    mm.then_inc(aux_done, 1)
                pe.wait_ge(zt_ready, l + 1)
                for t in range(TB):
                    b = bank(X_FC + t)
                    for c in range(2):
                        mm = pe.matmul(b[:, c * 256:(c + 1) * 256], ZFT[:, c, t * P:(t + 1) * P], dft_c[:], start=True, stop=True)
                    mm.then_inc(aux_done, 1)
                pe.wait_ge(zcs_ready, l + 1)
                for c in range(2):
                    b = bank(X_FP + c)
                    for q in range(2):
                        pe.matmul(b[:, 0:P], ZCS[:, 0, c, q * P:(q + 1) * P], dft_p[:, q, :], start=(q == 0), stop=(q == 1))
                    for n in range(4):
                        t, q = n // 2, n % 2
                        mm = pe.matmul(b[:, P:T], ZCS[:, 1 + t, c, q * P:(q + 1) * P], dft_s[:, t, q, :], start=(n == 0), stop=(n == 3))
                    mm.then_inc(aux_done, 1)
                for c in range(2):
                    b = bank(X_PD + c)
                    for g2 in range(2):
                        g = 2 * c + g2
                        out = b[64 * g2:64 * g2 + 64, :]
                        pe.matmul(out[:, 0:P], Z[:, 0, 1792 + 64 * g:1856 + 64 * g], pool_p[:, g, :], start=True, stop=True)
                        for t in range(2):
                            mm = pe.matmul(out[:, P:T], Z[:, 1 + t, 1792 + 64 * g:1856 + 64 * g], pool_s[:, t, g, :],
                                           start=(t == 0), stop=(t == 1))
                    mm.then_inc(aux_done, 1)
                pe.wait_ge(dt_ready, l + 1)
                pe.wait_ge(cols_landed, l * 96 + 96)
                for c in range(2):
                    pe.matmul(bank(X_PY + c)[:, 0:T], wpg[:, c, :], DT[:, c, :], start=True, stop=True).then_inc(aux_done, 1)

                pe.wait_ge(att_landed, l * (16 * 6) + 16 * 6)

                def attend(kind, i):
                    h, t = i // TB, i % TB
                    r = 64 * (h % 2)
                    b = bank(ATT_USE[kind, i])
                    if kind == "s":
                        q = QT[r:r + 64, h // 2, t * P:(t + 1) * P]
                        if t == 0:
                            mm = pe.matmul(b[:, 0:P], q, KT[r:r + 64, h // 2, 0:P], start=True, stop=True)
                        else:
                            pe.matmul(b[:, 0:256], q, KT[r:r + 64, h // 2, P:T], start=True, stop=True)
                            mm = pe.matmul(b[:, 256:T], q, KCT[r:r + 64, h // 2, :], start=True, stop=True)
                    elif kind == "t":
                        pe.wait_ge(pn_ready, l * STEPS + i + 1)
                        for n in range(1 if t == 0 else 3):
                            mm = pe.transpose(b[:, n * P:(n + 1) * P], PR[:, i % 2, n * P:(n + 1) * P], ident[:])
                    else:
                        pe.wait_ge(pt_ready, l * STEPS + i + 1)
                        v = 1280 + DH * h
                        vs = [Z[:, 0, v:v + DH]] if t == 0 else [Z[:, 1, v:v + DH], Z[:, 2, v:v + DH], VC[:, DH * h:DH * h + DH]]
                        for n, x in enumerate(vs):
                            mm = pe.matmul(b[r:r + 64, 0:P], x, PT[:, i % 2, n, :], start=(n == 0), stop=(n == len(vs) - 1))
                    mm.then_inc(aux_done, 1)

                passes = [(U_GF, KC, (LTh, LTl), 0, C_GF), (U_WF, 2, (BTh, BTl), 0, C_WF),
                          (U_GP, KC, (LTh, LTl), 0, C_GP), (U_WP, 2, (BTh, BTl), 6, C_WP),
                          (U_GA, KC, (LTh, LTl), 0, C_GA), (U_WA, 4, (BTh, BTl), 2, C_WA)]
                for u0, n, lt, c0, use in passes:
                    if u0 == U_WF:
                        pe.wait_ge(four_done, l + 1)
                    if u0 == U_WA:
                        pe.wait_ge(att_done, l + 1)
                    for k in range(n):
                        i = u0 + k - U_GF
                        if i < len(ATT):
                            for kind, j in ATT[i]:
                                attend(kind, j)
                        unit(u0 + k, lt, c0 + k, use, k == 0, k == n - 1)
                pe.wait_ge(m_ready, l + 1)
                turn(M, X_MT)
                pe.wait_ge(ht_ready, l * 3 + 2)
                for k in range(KC):
                    unit(U_OUT + k, (LTh, LTl), k, C_OUT, k == 0, k == KC - 1)
                pe.wait_ge(xn_ready, l * 2 + 2)
                turn(XN, X_H2)
                pe.wait_ge(ht_ready, l * 3 + 3)
                for p in range(2):
                    for k in range(KC):
                        unit(U_Q + p * KC + k, (LTh, LTl), k, C_Q + 6 * p, k == 0, k == KC - 1)
                pe.wait_ge(pq_ready, l + 1)
                for k in range(16):
                    b = bank(X_QT + k)
                    for t in range(TB):
                        mm = pe.transpose(b[:, t * P:(t + 1) * P], Z[:, t, k * P:(k + 1) * P], ident[:])
                    mm.then_inc(aux_done, 1)
                pe.wait_ge(pqt_ready, l + 1)
                pe.wait_ge(keys_landed, l * 16 + 16)
                for t in range(TB):
                    for q in range(4):
                        b = bank(X_SC + 4 * t + q)
                        for j in range(4):
                            mm = pe.matmul(b[:, j * P:(j + 1) * P], PQT[:, 4 * q + j, t * P:(t + 1) * P], KEYT[:, 4 * q + j, :],
                                           start=True, stop=True)
                        mm.then_inc(aux_done, 1)
                for t in range(TB):
                    pe.wait_ge(sel_ready, l * TB + t + 1)
                    b = bank(X_IT + t)
                    for q in range(3):
                        mm = pe.transpose(b[:, q * P:(q + 1) * P], SELf[:, q, :], ident[:])
                    mm.then_inc(aux_done, 1)
                with pe.Fori(0, T // GT) as g:
                    for j in range(GT):
                        use = X_G + j // 4
                        if j % 4 == 0:
                            pe.wait_ge(aux_free, l * AUXS + g * (GT // 4) + use + 1)
                        pe.wait_ge(hot_ready, l * T + g * GT + j + 1)
                        mm = pe.matmul(aux[use % 2][:, (j % 4) * P:(j % 4 + 1) * P], HOT[:, j % 4, 0, :], HOT[:, j % 4, 1, :],
                                       start=True, stop=True)
                        if j % 4 == 3:
                            mm.then_inc(aux_done, 1)
                for b in range(6):
                    pe.wait_ge(acc_free, l * ACCS + C_V + b + 1)

                def experts(k, first, last):
                    for j in range(2):
                        pe.wait_ge(lo_ready, l * UNITS + k * 4 + U_PEER + j + 1 + SLOTS)
                        pe.wait_ge(aux_free, l * AUXS + k * 2 + X_U + j + 1)
                        b = aux[(X_U + j) % 2]
                        for c in range(KC):
                            for n, (w, x) in enumerate(((whi, LTh), (whi, LTl), (wlo, LTh))):
                                mm = pe.matmul(b[:, 0:T], w[:, j, c * P:(c + 1) * P], x[:, c, :],
                                               start=(c == 0 and n == 0), stop=(c == KC - 1 and n == 2))
                        mm.then_inc(aux_done, 1)
                        pe.drain().then_inc(unit_used, 1)
                    for j in range(2):
                        pe.wait_ge(lo_ready, l * UNITS + k * 4 + U_PEER + 2 + j + 1 + SLOTS)
                        pe.wait_ge(w_ready, l * KEYS + k * 2 + j + 1 + 2)
                        for t in range(TB):
                            wh, wl = (x[:, j, t * P:(t + 1) * P] for x in (BTh, BTl))
                            for n, (x, w) in enumerate(((wh, whi), (wh, wlo), (wl, whi))):
                                for h in range(2):
                                    mm = pe.matmul(accum(C_V + 2 * t + h)[:], x, w[:, 2 + j, h * HB:(h + 1) * HB],
                                                   start=(first and j == 0 and n == 0), stop=(last and j == 1 and n == 2),
                                                   skip_group_check=True)
                                    if last and j == 1 and n == 2:
                                        mm.then_inc(acc_done, 1)
                        pe.drain().then_inc(unit_used, 1)

                experts(0, True, False)
                with pe.Fori(1, KEYS // 2 - 1) as k:
                    experts(k, False, False)
                experts(KEYS // 2 - 1, False, True)

        @block.vector
        def _(dve):
            dve.memset(nhalf[:], -0.5)
            dve.memset(wpg[:], 0.0)
            dve.drain().then_inc(start_ready, 1)
            dve.sem_inc(acc_free, 6)
            dve.sem_inc(aux_free, 2)
            dve.sem_inc(layer_free, 1)
            dve.sem_inc(w_ready, 2)
            dve.wait_ge(const_landed, 16 * 9)
            dve.wait_ge(x_landed, 32)
            dve.wait_ge(silu_ready, 1)

            def mean_square():
                for t in range(TB):
                    dve.tensor_tensor_reduce(XN[:, t], X[:, t], X[:, t], 1.0, 0.0, ALU.mult, ALU.add, ms[:, t:t + 1])
                dve.drain()
                dve.tensor_scalar(ms[:], ms[:], 1.0 / D, EPS, ALU.mult, ALU.add).then_inc(ms_ready, 1)

            def normalise(n):
                dve.wait_ge(rstd_ready, n)
                for t in range(TB):
                    dve.tensor_scalar(XN[:, t], X[:, t], rstd[:, t:t + 1], None, ALU.mult)

            with dve.Fori(0, DEPTH) as l:
                def bank(use):
                    dve.wait_ge(aux_done, l * AUXS + use + 1)
                    return aux[use % 2]

                def accu(use):
                    dve.wait_ge(acc_done, l * ACCS + use + 1)
                    return accum(use)

                def split(h, lo, src):
                    dve.tensor_copy(h, src)
                    dve.drain()
                    return dve.tensor_tensor(lo, src, h.bitcast(F32), ALU.subtract)

                for s in range(2):
                    src = cond[:, s, :].rearrange("p (k o) -> p k o", o=1).to_broadcast([P, KC, 64])
                    h, lo = (x[:, :, 64 * s:64 * s + 64] for x in (LTh, LTl))
                    split(h, lo, src)
                dve.drain().then_inc(cond_ready, 1)
                mean_square()
                dve.wait_ge(bada_landed, l * 16 + 16)
                for p in range(6):
                    for h in range(2):
                        at = p * D + h * HB
                        dve.tensor_tensor(MODR[:, at:at + HB], accu(C_ADA + 2 * p + h)[:], BADA[:, at:at + HB],
                                          ALU.add).then_inc(acc_free, 1)
                    dve.drain().then_inc(modr_ready, 1)
                normalise(l * 2 + 1)
                dve.drain().then_inc(xn_ready, 1)
                for n in range(4):
                    for q in range(2):
                        b = bank(X_MOD + 2 * n + q)
                        dve.tensor_copy(modc[:, n, :, 4 * q:4 * q + 4],
                                        b[:].rearrange("p (k s c) -> p s k c", k=4, s=2)[:, :, :, 0]).then_inc(aux_free, 1)
                dve.drain().then_inc(mods_done, 1)
                dve.wait_ge(cols_landed, l * 96 + 96)
                for n in range(2):
                    for s in range(2):
                        dve.scalar_tensor_tensor(modc[:, 2 * n + 1, s, :], modc[:, 2 * n + 1, s, :], 1.0, gcol[:, n, :],
                                                 ALU.add, ALU.mult)
                dve.drain()

                def modulated(base, n):
                    for k in range(KC):
                        b = bank(base + k)
                        for s, (c0, c1) in enumerate(((0, P), (P, T))):
                            x = dve.tensor_scalar(HRAW[:, k, c0:c1], b[:, c0:c1], modc[:, 2 * n + 1, s, k:k + 1],
                                                  modc[:, 2 * n, s, k:k + 1], ALU.mult, ALU.add)
                        x.then_inc(aux_free, 1)
                    dve.drain()
                    split(LTh[:], LTl[:], HRAW[:])
                    dve.drain().then_inc(ht_ready, 1)

                modulated(X_HT, 0)
                for p in range(2):
                    for t in range(TB):
                        for h in range(2):
                            at = p * D + h * HB
                            dve.tensor_copy(Z[:, t, at:at + HB], accu(C_IN + 6 * p + 2 * t + h)[:]).then_inc(acc_free, 1)
                dve.drain().then_inc(z_ready, 1)
                for k in range(10):
                    b = bank(X_ZT + k)
                    if k < 2:
                        x = dve.tensor_copy(ZFT[:, k], b[:, 0:T])
                    elif k < 6:
                        x = dve.tensor_scalar(QT[:, k - 2], b[:, 0:T], DH ** -0.5, None, ALU.mult)
                    else:
                        x = dve.tensor_copy(KT[:, k - 6], b[:, 0:T])
                    x.then_inc(aux_free, 1)
                dve.drain().then_inc(zt_ready, 1)
                for t in range(TB):
                    dve.tensor_copy(ZCS[:, t].rearrange("p c n -> p (c n)"), bank(X_FC + t)[:]).then_inc(aux_free, 1)
                dve.drain().then_inc(zcs_ready, 1)
                for c in range(2):
                    split(BTh[:, c], BTl[:, c], bank(X_FP + c)[:, 0:T]).then_inc(aux_free, 1)
                for c in range(2):
                    dve.tensor_copy(DT[:, c], bank(X_PD + c)[:, 0:T]).then_inc(aux_free, 1)
                dve.drain().then_inc(dt_ready, 1)
                for c in range(2):
                    dve.tensor_scalar(ZFT[:, c], bank(X_PY + c)[:, 0:T], pscale[:, c:c + 1], None, ALU.mult).then_inc(aux_free, 1)
                dve.drain()
                split(BTh[:, 6:8], BTl[:, 6:8], ZFT)
                dve.drain().then_inc(four_done, 1)
                dve.wait_ge(att_landed, l * (16 * 6) + 16 * 6)
                bv = BIAS.rearrange("p b h (r n) -> p (b h r) n", r=4)
                dve.tensor_tensor(bv, bv, mask[:].rearrange("p (o n) -> p o n", o=1).to_broadcast([P, 2 * HEADS * 4, GRID]), ALU.add)
                dve.drain()

                def evacuate(kind, i):
                    h, t = i // TB, i % TB
                    s, r = i % 2, 64 * (i // TB % 2)
                    b = bank(ATT_USE[kind, i])
                    if kind == "s":
                        if t == 0:
                            dve.tensor_copy(S[:, s, 0:P], b[:, 0:P]).then_inc(aux_free, 1)
                        else:
                            dve.tensor_tensor(S[:, s, 0:256], b[:, 0:256], BIAS[:, t - 1, h, :], ALU.add)
                            dve.tensor_copy(S[:, s, 256:T], b[:, 256:T]).then_inc(aux_free, 1)
                        dve.drain()
                        dve.tensor_reduce(nmax[:, s:s + 1], S[:, s, 0:P if t == 0 else T], AX, ALU.max, negate=True).then_inc(s_ready, 1)
                    elif kind == "t":
                        n = 1 if t == 0 else 3
                        dve.tensor_copy(PT[:, s, 0:n, :].rearrange("p k q -> p (k q)"), b[:, 0:n * P]).then_inc(aux_free, 1)
                        dve.drain().then_inc(pt_ready, 1)
                    else:
                        at = (slice(r, r + 64), 2 + h // 2, slice(t * P, (t + 1) * P))
                        split(BTh[at], BTl[at], b[r:r + 64, 0:P]).then_inc(aux_free, 1)

                def probabilities(i):
                    s, n = i % 2, P if i % TB == 0 else T
                    dve.wait_ge(p_ready, l * STEPS + i + 1)
                    dve.reciprocal(rsum[:, s:s + 1], rsum[:, s:s + 1])
                    dve.drain()
                    dve.tensor_scalar(PR[:, s, 0:n], PR[:, s, 0:n], rsum[:, s:s + 1], None, ALU.mult).then_inc(pn_ready, 1)

                def gate(n, use):
                    dve.wait_ge(bgate_landed, l * 48 + 16 * (n + 1))
                    for t in range(TB):
                        for h in range(2):
                            g = GTB[:, t, h * HB:(h + 1) * HB]
                            dve.tensor_tensor(g, g, accu(use + 2 * t + h)[:], ALU.add).then_inc(acc_free, 1)
                        dve.drain().then_inc(gate_sum, 1)

                def merge(n, use):
                    if n == 0:
                        dve.wait_ge(kv_stored, l * 32 + 32)
                    for t in range(TB):
                        dve.wait_ge(gate_ready, l * 9 + 3 * n + t + 1)
                        for h in range(2):
                            g, m = GTB[:, t, h * HB:(h + 1) * HB], M[:, t, h * HB:(h + 1) * HB]
                            dve.tensor_tensor(g if n else m, g, accu(use + 2 * t + h)[:], ALU.mult).then_inc(acc_free, 1)
                            if n:
                                dve.drain()
                                dve.tensor_tensor(m, m, g, ALU.add)
                    x = dve.drain()
                    x.then_inc(gtb_free, 1)

                for i in range(U_OUT - U_GF):
                    u = U_GF + i
                    if i < len(ATT):
                        for kind, j in ATT[i]:
                            evacuate(kind, j)
                        if i < STEPS:
                            probabilities(i)
                    if i == len(ATT) - 1:
                        dve.drain().then_inc(att_done, 1)
                    for u1, what, n, use in ((U_WF, gate, 0, C_GF), (U_GP, merge, 0, C_WF), (U_WP, gate, 1, C_GP),
                                             (U_GA, merge, 1, C_WP), (U_WA, gate, 2, C_GA), (U_OUT, merge, 2, C_WA)):
                        if u + 1 == u1:
                            what(n, use)
                dve.sem_inc(m_ready, 1)
                for k in range(KC):
                    split(LTh[:, k], LTl[:, k], bank(X_MT + k)[:, 0:T]).then_inc(aux_free, 1)
                dve.drain().then_inc(ht_ready, 1)

                def residual(use, gates):
                    for t in range(TB):
                        for h in range(2):
                            at = slice(h * HB, (h + 1) * HB)
                            dve.tensor_tensor(XTMP, accu(use + 2 * t + h)[:], gates[:, min(t, 1), at], ALU.mult).then_inc(acc_free, 1)
                            dve.drain()
                            dve.tensor_tensor(X[:, t, at], X[:, t, at], XTMP, ALU.add)
                            dve.drain()

                dve.wait_ge(gate1_landed, l * 32 + 32)
                residual(C_OUT, Z[:, 0:2, D:2 * D])
                dve.sem_inc(out_done, 1)
                mean_square()
                normalise(l * 2 + 2)
                dve.drain().then_inc(xn_ready, 1)
                modulated(X_H2, 1)
                for p in range(2):
                    for t in range(TB):
                        for h in range(2):
                            at = p * D + h * HB
                            dve.tensor_copy(Z[:, t, at:at + HB], accu(C_Q + 6 * p + 2 * t + h)[:]).then_inc(acc_free, 1)
                dve.drain().then_inc(pq_ready, 1)
                for k in range(16):
                    dve.tensor_copy(PQT[:, k], bank(X_QT + k)[:, 0:T]).then_inc(aux_free, 1)
                dve.drain().then_inc(pqt_ready, 1)
                for t in range(TB):
                    for q in range(4):
                        dve.tensor_copy(Z[:, t, q * HB:(q + 1) * HB], bank(X_SC + 4 * t + q)[:]).then_inc(aux_free, 1)
                dve.drain()

                def top16(rows):
                    for r in range(2):
                        for v, m, i in rows:
                            dve.max(m[:, 8 * r:8 * r + 8], v)
                        dve.drain()
                        for v, m, i in rows:
                            dve.max_index(i[:, 8 * r:8 * r + 8], m[:, 8 * r:8 * r + 8], v)
                        if r == 0:
                            dve.drain()
                            for v, m, i in rows:
                                dve.match_replace(v, m[:, 0:8], v, -3.0e38)
                            dve.drain()

                for t in range(TB):
                    top16([(Z[:, t, k * P:(k + 1) * P], SV[:, k, :], SI[:, k, :]) for k in range(16)])
                    dve.drain()
                    dve.tensor_copy(SIF.rearrange("p h q k -> p (h q) k"), SI)
                    sv = SV.rearrange("p (h q) k -> p h q k", q=2)
                    for h in range(HEADS):
                        dve.tensor_tensor(CAND[:, h], sv[:, h, 0].rearrange("p (a o) -> p a o", o=1).to_broadcast([P, TOPK, TOPK]),
                                          sv[:, h, 1].rearrange("p (o b) -> p o b", o=1).to_broadcast([P, TOPK, TOPK]), ALU.add)
                    dve.drain()
                    top16([(CAND[:, h].rearrange("p a b -> p (a b)"), TOP[:, h, :], POS[:, h, :]) for h in range(HEADS)])
                    dve.drain()
                    if t:
                        dve.wait_ge(selt_ready, l * TB + t)
                    dve.tensor_tensor(SEL[:, 2], TOP, TOP[:, :, 0:1].to_broadcast([P, HEADS, TOPK]), ALU.subtract)
                    dve.drain().then_inc(top_ready, 1)
                    dve.tensor_scalar(PA, POS, 4, None, ALU.logical_shift_right)
                    dve.tensor_scalar(PB, POS, TOPK - 1, None, ALU.bitwise_and)
                    dve.drain()
                    dve.tensor_copy(PAB[:, 0], PA)
                    dve.tensor_copy(PAB[:, 1], PB)
                    dve.drain()
                    for q in range(2):
                        for h in range(HEADS):
                            dve.tensor_tensor(OH[:, h], PAB[:, q, h].rearrange("p (k o) -> p k o", o=1).to_broadcast([P, TOPK, TOPK]),
                                              iota[:, 0:TOPK].rearrange("p (o a) -> p o a", o=1).to_broadcast([P, TOPK, TOPK]), ALU.is_equal)
                        dve.drain()
                        for h in range(HEADS):
                            dve.tensor_tensor(OH[:, h], OH[:, h], SIF[:, h, q].rearrange("p (o a) -> p o a", o=1).to_broadcast([P, TOPK, TOPK]),
                                              ALU.mult)
                        dve.drain()
                        dve.tensor_reduce(SEL[:, q].rearrange("p h k -> p (h k)"), OH.rearrange("p h k a -> p (h k) a"), AX, ALU.add)
                        dve.drain()
                    dve.wait_ge(exp_ready, l * TB + t + 1)
                    dve.tensor_reduce(hsum[:], SEL[:, 2], AX, ALU.add)
                    dve.drain()
                    dve.reciprocal(hsum[:], hsum[:])
                    dve.drain()
                    dve.tensor_tensor(SEL[:, 2], SEL[:, 2], hsum[:].rearrange("p (h o) -> p h o", o=1).to_broadcast([P, HEADS, TOPK]), ALU.mult)
                    dve.drain().then_inc(sel_ready, 1)
                    b = bank(X_IT + t)
                    dve.tensor_copy(SELT[:, :, t * P:(t + 1) * P], b[:, 0:3 * P].rearrange("p (q t) -> p q t", q=3)).then_inc(aux_free, 1)
                    dve.drain().then_inc(selt_ready, 1)
                with dve.Fori(0, T // 4) as g:
                    for j in range(4):
                        dve.wait_ge(aux_done, l * AUXS + g + X_G)
                        i1, i2, gg = (SELT[:, q, bass.ds(g * 4 + j, 1)] for q in range(3))
                        dve.tensor_scalar(HOT[:, j, 0, :], iota[:], i1, gg, ALU.is_equal, ALU.mult)
                        dve.tensor_scalar(HOT[:, j, 1, :], iota[:], i2, None, ALU.is_equal)
                        dve.drain().then_inc(hot_ready, 1)
                with dve.Fori(0, KEYS // BODY) as i:
                    for n in range(BODY):
                        j, s = n % 2, n // GN
                        if n % GN == 0:
                            dve.wait_ge(group_landed[s], l * (8 * GGROUPS) + i * 16 + 16)
                        dve.wait_ge(act_ready, l * KEYS + i * BODY + n + 1)
                        dve.tensor_tensor(ACTB[:, j], ACTB[:, j], GCH[:, s, :, n % GN], ALU.mult)
                        dve.drain()
                        dve.wait_ge(unit_used, l * UNITS + i * (2 * BODY) + U_PEER + 4 * (n // 2) - 2 + j + 1 + SLOTS)
                        split(BTh[:, j], BTl[:, j], ACTB[:, j]).then_inc(w_ready, 1)
                dve.wait_ge(gate2_landed, l * 32 + 32)
                residual(C_V, GATE2)
                dve.drain().then_inc(layer_free, 1)
            mean_square()
            normalise(2 * DEPTH + 1)
            dve.drain()
            dve.wait_ge(gfin_landed, 16)
            for t in range(TB):
                dve.tensor_tensor(X[:, t], XN[:, t], GFIN, ALU.mult)
            dve.drain().then_inc(y_ready, 1)


def _constants():
    import numpy as np

    ident = np.eye(P, dtype=np.float32)
    iota = np.tile(np.arange(P, dtype=np.float32), (P, 1))
    qc = np.arange(P)[:, None] % GRID
    kc = np.arange(GRID)[None, :]
    start = np.clip(qc - 8, 0, GRID - 16)
    mask = np.where((kc >= start) & (kc < start + 16), 0.0, -1e30).astype(np.float32)

    def dft(n):
        angle = 2 * np.pi * (np.outer(np.arange(n), np.arange(n)) % n) / n
        return np.cos(angle) / np.sqrt(n), np.sin(angle) / np.sqrt(n)

    c64, s64 = dft(64)
    dft_c = np.zeros((P, 256))
    for g in range(2):
        dft_c[64 * g:64 * g + 64, 64 * g:64 * g + 64] = c64
        dft_c[64 * g:64 * g + 64, P + 64 * g:P + 64 * g + 64] = s64
    c, s = dft(128)
    dft_p = np.stack([c, -s], axis=1)
    c, s = dft(256)
    dft_s = np.stack([c, -s], axis=1).reshape(2, P, 2, 256).transpose(1, 0, 2, 3)

    def pool(n):
        out = np.zeros((n, 4, n))
        for g, w in enumerate((2, 4, 8, 16)):
            for t in range(n):
                a, b = max(t - w // 2, 0), min(t + w // 2, n)
                out[a:b, g, t] = 1.0 / (b - a)
                out[t, g, t] -= 1.0
        return out

    pool_p = pool(128)
    pool_s = pool(256).reshape(2, P, 4, 256).transpose(1, 0, 2, 3)
    tables = dict(ident=ident, iota=iota, mask=mask, dft_c=dft_c, dft_p=dft_p, dft_s=dft_s, pool_p=pool_p, pool_s=pool_s)
    return {k: np.ascontiguousarray(v, dtype=np.float32) for k, v in tables.items()}


_OUTS = {"y_prompt": (128, D), "y_sample": (256, D), "new_k": (DEPTH, HEADS, 128, DH), "new_v": (DEPTH, HEADS, 128, DH)}


def kernel(**inputs):
    import numpy as np
    import concourse.bacc as bacc
    from concourse.bass_utils import run_bass_kernel_spmd as run

    x = {k: np.asarray(v) for k, v in inputs.items()}
    arrays = dict(_constants())
    arrays["x_prompt"] = x["x_prompt"].reshape(128, D)
    arrays["x_sample"] = x["x_sample"].reshape(256, D)
    arrays["cond"] = np.stack([x["c_ctx"].reshape(KC, P), x["c"].reshape(KC, P)]).transpose(2, 0, 1)
    arrays["gcol"] = np.stack([x["g_attn"].reshape(DEPTH, KC, P), x["g_ffn"].reshape(DEPTH, KC, P)], axis=1).transpose(0, 3, 1, 2)
    arrays["pool_scale"] = x["pool_scale"].reshape(DEPTH, 2, P).transpose(0, 2, 1)
    arrays["b_gate"] = x["b_gate"].reshape(DEPTH, 3, D)
    for name in ("b_ada", "w_ada", "w_in", "w_fourier", "w_pool_grp", "w_pool", "w_attn", "w_gate", "w_out", "peer_wq", "rel_bias"):
        arrays[name] = x[name]
    arrays["cache_k"] = x["cache_k"][0].reshape(DEPTH, 4, 2, 128, DH).transpose(0, 2, 4, 1, 3).reshape(DEPTH, P, 4, 128)
    arrays["cache_v"] = x["cache_v"][0]
    arrays["keys"] = x["peer_keys"].transpose(0, 4, 1, 2, 3).reshape(DEPTH, P, 16, KEYS)
    arrays["ut"] = x["peer_u"].reshape(DEPTH, KEYS, KEYS, KC, P).transpose(0, 2, 4, 3, 1).reshape(DEPTH * KEYS, P, KC * KEYS)
    arrays["peer_v"] = x["peer_v"].reshape(DEPTH * KEYS, KEYS, D)
    arrays["g_final"] = x["g_final"].reshape(1, D)
    arrays = {k: np.ascontiguousarray(v) for k, v in arrays.items()}

    nc = bacc.Bacc("TRN2", target_bir_lowering=False, num_devices=1)
    a = {k: nc.dram_tensor("in_" + k, v.shape, F32, kind="ExternalInput").ap() for k, v in arrays.items()}
    o = {k: nc.dram_tensor("out_" + k, shape, F32, kind="ExternalOutput").ap() for k, shape in _OUTS.items()}
    build(nc, a, o)
    r = run(nc, [{"in_" + k: v for k, v in arrays.items()}], core_ids=[0]).results[0]
    return (r["out_y_prompt"].reshape(1, 128, D), r["out_y_sample"].reshape(1, 256, D),
            r["out_new_k"].reshape(1, DEPTH, HEADS, 128, DH), r["out_new_v"].reshape(1, DEPTH, HEADS, 128, DH))
```

```python
from contextlib import ExitStack

import concourse.bass as bass
from concourse import mybir
from concourse.alu_op_type import AluOpType as ALU

F32 = mybir.dt.float32
F32R = mybir.dt.float32r
U32 = mybir.dt.uint32
ACT = mybir.ActivationFunctionType
AX = mybir.AxisListType.X

P = 128
D = 1024
DEPTH = 2
TB = 3
T = TB * P
KC = D // P
HEADS = 8
DH = 64
GRID = 64
RB = 15 * 31
KEYS = 128
TOPK = 16
EPS = 1e-6
UW = 1024
HB = 512
SLOTS = 4

U_IN = 0
U_GF = U_IN + 2 * KC
U_WF = U_GF + KC
U_GP = U_WF + 2
U_WP = U_GP + KC
U_GA = U_WP + 2
U_WA = U_GA + KC
U_OUT = U_WA + 4
U_Q = U_OUT + KC
U_PEER = U_Q + 2 * KC
UNITS = U_PEER + 2 * KEYS
PAIRS = UNITS // 2
USED = U_PEER + KEYS
assert UNITS % SLOTS == 0

C_ADA = 0
C_IN = C_ADA + 12
C_GF = C_IN + 12
C_WF = C_GF + 6
C_GP = C_WF + 6
C_WP = C_GP + 6
C_GA = C_WP + 6
C_WA = C_GA + 6
C_OUT = C_WA + 6
C_Q = C_OUT + 6
C_V = C_Q + 12
ACCS = C_V + 6
assert ACCS % 6 == 0

STEPS = HEADS * TB
BESIDE = [[("z", 2), ("z", 3)], [], [("z", 4), ("z", 5), ("z", 0)], [], [("z", 1), ("z", 6), ("z", 7)], [],
          [("f", 0), ("f", 1), ("f", 2)], [], [("z", 8), ("p", 0), ("p", 1)], [], [("z", 9), ("d", 0), ("d", 1)], [],
          [("y", 0), ("y", 1)], []]
_step = 0
for _i in range(len(BESIDE), 2 * (U_WA - U_GF)):
    BESIDE.append([])
    if _i % 2 == 0 or _i // 2 in (12, 14, 16, 22, 24):
        BESIDE[-1] += [(_k, _j) for _k, _j in (("s", _step), ("t", _step - 1), ("v", _step - 2)) if 0 <= _j < STEPS]
        _step += 1
BESIDE += [[]] * (2 * (U_OUT - U_WA))
assert _step == STEPS + 2
X_MOD = 0
X_HT = X_MOD + 8
X_BES = X_HT + KC
USE = {}
for _i in BESIDE:
    for _u in _i:
        USE[_u] = X_BES + len(USE)
X_MT = X_BES + len(USE)
X_H2 = X_MT + KC
X_QA = X_H2 + KC
X_SA = X_QA + 8
X_QB = X_SA + 6
X_SB = X_QB + 8
X_IT = X_SB + 6
X_G = X_IT + TB
X_U = X_G + T // 4
AUXS = X_U + KEYS
assert X_U % 2 == 0

GT = 16
BY_POOL = (0, 2, 3, 5, 6)
GN = 8
GGROUPS = KEYS // GN
BODY = 2 * GN


def build(nc, a, o):
    with ExitStack() as ctx:
        def sb(name, shape, dt=F32):
            return ctx.enter_context(nc.sbuf_tensor(name, shape, dt))

        def sem(name):
            return ctx.enter_context(nc.semaphore(name))

        X = sb("x", [P, TB, D])
        Z = sb("z", [P, TB, 2 * D])
        Zf = Z[:].rearrange("p t n -> p (t n)")
        XN = Zf[:, 0:TB * D].rearrange("p (t n) -> p t n", t=TB)
        HRAW = Zf[:, TB * D:2 * TB * D].rearrange("p (k t) -> p k t", k=KC)
        M = Z[:, :, 0:D]
        GCH = Zf.rearrange("p (s t n) -> p s t n", s=2, n=GN)
        LTh = sb("lt_hi", [P, KC, T], F32R)
        LTl = sb("lt_lo", [P, KC, T], F32R)
        BTh = sb("bt_hi", [P, 8, T], F32R)
        BTl = sb("bt_lo", [P, 8, T], F32R)
        raw = sb("raw", [P, SLOTS, UW])
        whi = sb("whi", [P, SLOTS, UW], F32R)
        wlo = sb("wlo", [P, SLOTS, UW], F32R)
        U = sb("u", [P, 13568])

        def part(at, n, **k):
            v = U[:, at:at + n]
            return v.rearrange(*k["r"][:1], **k["r"][1]) if "r" in k else v

        BADA = part(0, 6 * D)
        MODR = part(6 * D, 6 * D)
        CB = part(12 * D, KC * P, r=("p (k c) -> p k c", dict(k=KC)))
        GTB = part(0, TB * D, r=("p (t n) -> p t n", dict(t=TB)))
        ZFT = Z[:, 0:2, 256:256 + T]
        ZCS = part(10240, TB * 512, r=("p (t c n) -> p t c n", dict(t=TB, c=2)))
        DT = part(11776, 2 * T, r=("p (c t) -> p c t", dict(c=2)))
        XTMP = part(0, 1024, r=("p (s n) -> p s n", dict(s=2)))
        QT = part(3072, 4 * T, r=("p (c t) -> p c t", dict(c=4)))
        KT = part(4608, 4 * T, r=("p (c t) -> p c t", dict(c=4)))
        BIAS = part(6144, 4096, r=("p (b h n) -> p b h n", dict(b=2, h=HEADS)))
        MRAW = part(6144, KC * T, r=("p (k t) -> p k t", dict(k=KC)))
        S = part(10240, 768, r=("p (s n) -> p s n", dict(s=2)))
        PR = part(11008, 768, r=("p (s n) -> p s n", dict(s=2)))
        PT = part(11776, 768, r=("p (s k q) -> p s k q", dict(s=2, k=3)))
        KCT = part(12544, 512, r=("p (c n) -> p c n", dict(c=4)))
        VC = part(13056, 512)
        KEYT = part(0, 16 * KEYS, r=("p (h n) -> p h n", dict(h=16)))
        PQT = part(2048, 16 * T, r=("p (h t) -> p h t", dict(h=16)))
        CAND = part(2048, 2048, r=("p (h a b) -> p h a b", dict(h=HEADS, a=TOPK)))
        OH = [part(at, 2048, r=("p (h k a) -> p h k a", dict(h=HEADS, k=TOPK))) for at in (4096, 11488)]
        STG = part(4096, 4096, r=("p (s g t n) -> p s g t n", dict(s=2, g=GGROUPS, t=GT)))
        GATE2 = part(2048, 2048, r=("p (c n) -> p c n", dict(c=2)))
        SV = part(8192, 768, r=("p (t h k) -> p t h k", dict(t=TB, h=16)))
        SI = part(8960, 768, r=("p (t h k) -> p t h k", dict(t=TB, h=16))).bitcast(U32)
        SIF = part(6144, 512, r=("p (s h q k) -> p s h q k", dict(s=2, h=HEADS, q=2)))
        TOP = part(9728, 128, r=("p (h k) -> p h k", dict(h=HEADS)))
        POS = part(9856, 128, r=("p (h k) -> p h k", dict(h=HEADS))).bitcast(U32)
        PA = part(9984, 128, r=("p (h k) -> p h k", dict(h=HEADS))).bitcast(U32)
        PB = part(10112, 128, r=("p (h k) -> p h k", dict(h=HEADS))).bitcast(U32)
        PAB = part(6656, 512, r=("p (s q h k) -> p s q h k", dict(s=2, q=2, h=HEADS)))
        SEL = part(7168, 768, r=("p (s q h k) -> p s q h k", dict(s=2, q=3, h=HEADS)))
        SELf = part(7168, 768, r=("p (s q m) -> p s q m", dict(s=2, q=3)))
        SELT = part(10336, 3 * T, r=("p (q t) -> p q t", dict(q=3)))
        SELC = part(10240, 96, r=("p (s q t) -> p s q t", dict(s=2, q=3)))
        HOT1 = part(2048, 2048, r=("p (s n) -> p s n", dict(s=16)))
        HOT2 = part(11488, 2048, r=("p (s n) -> p s n", dict(s=16)))
        ACTB = part(0, 768, r=("p (s t) -> p s t", dict(s=2)))
        GFIN = part(0, D)

        ident = sb("ident", [P, P])
        iota = sb("iota", [P, P])
        mask = sb("mask", [P, GRID])
        dft_c = sb("dft_c", [P, 256])
        dft_p = sb("dft_p", [P, 2, P])
        dft_s = sb("dft_s", [P, 2, 2, 256])
        pool_p = sb("pool_p", [P, 4, P])
        pool_s = sb("pool_s", [P, 2, 4, 256])
        wpg = sb("wpg", [P, 2, P])
        cond = sb("cond", [P, 2, KC])
        gcol = sb("gcol", [P, 2, KC])
        pscale = sb("pscale", [P, 2])
        modc = sb("modc", [P, 4, 2, KC])
        ms = sb("ms", [P, TB])
        rstd = sb("rstd", [P, TB])
        nhalf = sb("nhalf", [P, TB])
        nmax = sb("nmax", [P, 2])
        rsum = sb("rsum", [P, 2])
        hsum = sb("hsum", [P, HEADS])
        acc = [ctx.enter_context(nc.psum_tensor(f"acc{i}", [P, HB], F32)) for i in range(6)]
        aux = [ctx.enter_context(nc.psum_tensor(f"aux{i}", [P, HB], F32)) for i in range(2)]

        gate_rows = nc.dram_tensor("gate_rows", (2, 2, D), F32, kind="Internal").ap()
        gmat = nc.dram_tensor("gmat", (GGROUPS, P, T * GN), F32, kind="Internal").ap()

        bias_rows = nc.dram_tensor("bias_rows", (DEPTH * HEADS, GRID, RB), F32, kind="Internal").ap()
        toeplitz = nc.dram_tensor("toeplitz", (DEPTH, GRID, HEADS, 7 * GRID), F32, kind="Internal").ap()

        pair_landed = [sem("pair_landed0"), sem("pair_landed1")]
        hi_ready = sem("hi_ready")
        lo_ready = sem("lo_ready")
        unit_used = sem("unit_used")
        acc_done = sem("acc_done")
        acc_free = sem("acc_free")
        aux_done = sem("aux_done")
        aux_free = sem("aux_free")
        first_landed = sem("first_landed")
        const_landed = sem("const_landed")
        x_landed = sem("x_landed")
        start_ready = sem("start_ready")
        bias_rows_stored = sem("bias_rows_stored")
        toeplitz_stored = sem("toeplitz_stored")
        silu_ready = sem("silu_ready")
        layer_free = sem("layer_free")
        ada_landed = [sem("ada_landed0"), sem("ada_landed1")]
        ada_used = sem("ada_used")
        bada_landed = sem("bada_landed")
        cols_landed = sem("cols_landed")
        cond_ready = sem("cond_ready")
        modr_ready = sem("modr_ready")
        rows_stored = sem("rows_stored")
        mods_done = sem("mods_done")
        ms_ready = sem("ms_ready")
        rstd_ready = sem("rstd_ready")
        xn_ready = sem("xn_ready")
        ht_ready = sem("ht_ready")
        z_ready = sem("z_ready")
        kv_stored = sem("kv_stored")
        att_landed = sem("att_landed")
        zf_ready = sem("zf_ready")
        qk_ready = sem("qk_ready")
        zcs_ready = sem("zcs_ready")
        dt_ready = sem("dt_ready")
        four_done = sem("four_done")
        bgate_landed = sem("bgate_landed")
        gate_sum = sem("gate_sum")
        gate_ready = sem("gate_ready")
        gtb_free = sem("gtb_free")
        s_ready = sem("s_ready")
        p_ready = sem("p_ready")
        pn_ready = sem("pn_ready")
        pt_ready = sem("pt_ready")
        att_done = sem("att_done")
        m_ready = sem("m_ready")
        gate1_landed = sem("gate1_landed")
        out_done = sem("out_done")
        keys_landed = sem("keys_landed")
        pq_ready = sem("pq_ready")
        pqt_ready = sem("pqt_ready")
        top_ready = sem("top_ready")
        exp_ready = sem("exp_ready")
        place_ready = sem("place_ready")
        index_ready = sem("index_ready")
        sel_ready = sem("sel_ready")
        selc_ready = sem("selc_ready")
        hot1_ready = sem("hot1_ready")
        hot2_ready = sem("hot2_ready")
        hot2_open = sem("hot2_open")
        stage_ready = sem("stage_ready")
        stage_stored = [sem("stage_stored0"), sem("stage_stored1")]
        gate2_landed = sem("gate2_landed")
        group_landed = [sem("group_landed0"), sem("group_landed1")]
        act_ready = sem("act_ready")
        w_ready = sem("w_ready")
        gfin_landed = sem("gfin_landed")
        y_ready = sem("y_ready")
        y_stored = sem("y_stored")

        NSTG = T // GT
        block = ctx.enter_context(nc.Block())

        def accum(use):
            return acc[use % 6]

        @block.sync
        def _(sp):
            with sp.Fori(0, DEPTH) as l:
                def pairs(u0, u1, source):
                    for i, u in enumerate(range(u0, u1, 2)):
                        q = u // 2
                        sp.wait_ge(lo_ready, l * UNITS + u + 2)
                        sp.dma_start(raw[:, u % SLOTS:u % SLOTS + 2, :], source(i)).then_inc(pair_landed[q % 2], 16)

                def rows(w, n0):
                    v = w[bass.ds(l, 1)].rearrange("o (k s p) n -> p (o k) s n", p=P, s=2)
                    return lambda i: v[:, i, :, n0:n0 + UW]

                for p in range(6):
                    source = rows(a["w_ada"], p * D)
                    for i in range(KC // 2):
                        n = p * (KC // 2) + i
                        if n < 2:
                            sp.wait_ge(lo_ready, l * UNITS + SLOTS)
                        else:
                            sp.wait_ge(ada_used, l * 6 * KC + 2 * n - 2)
                        sp.dma_start(raw[:, 2 * (n % 2):2 * (n % 2) + 2, :], source(i)).then_inc(ada_landed[n % 2], 16)
                    if p == 3:
                        sp.wait_ge(modr_ready, l * 6 + 3)
                        for s in range(2):
                            sp.dma_start(gate_rows[0, s:s + 1, :], MODR[64 * s:64 * s + 1, 2 * D:3 * D]).then_inc(rows_stored, 16)
                source = rows(a["w_in"], 0)
                for i in range(2):
                    sp.wait_ge(ada_used, l * 6 * KC + 6 * KC - 2 + 2 * i)
                    sp.dma_start(raw[:, 2 * i:2 * i + 2, :], source(i)).then_inc(pair_landed[i], 16)
                sp.wait_ge(modr_ready, l * 6 + 6)
                for s in range(2):
                    sp.dma_start(gate_rows[1, s:s + 1, :], MODR[64 * s:64 * s + 1, 5 * D:6 * D]).then_inc(rows_stored, 16)
                sp.wait_ge(mods_done, l + 1)
                sp.wait_ge(rows_stored, l * 64 + 64)
                sp.wait_ge(toeplitz_stored, 16 * DEPTH * HEADS)
                for b in range(2):
                    for r2 in range(2):
                        r = 2 * b + r2
                        sp.dma_start(BIAS[64 * r2:64 * r2 + 64, b],
                                     toeplitz[bass.ds(l, 1), :, :, (3 - r) * GRID:(7 - r) * GRID]
                                     .rearrange("o q h n -> (o q) h n")).then_inc(att_landed, 16)
                sp.dma_start(GTB, a["b_gate"][bass.ds(l, 1), 0:1, :].to_broadcast([P, TB, D])).then_inc(bgate_landed, 16)
                sp.dma_start(KCT, a["cache_k"][bass.ds(l, 1)].rearrange("o p c n -> (o p) c n")).then_inc(att_landed, 16)
                sp.dma_start(VC.rearrange("p (h d) -> p h d", h=HEADS),
                             a["cache_v"][bass.ds(l, 1)].rearrange("o h k d -> (o k) h d")).then_inc(att_landed, 16)
                v = a["w_in"][bass.ds(l, 1)].rearrange("o (k s p) n -> p (o k) s n", p=P, s=2)
                pairs(U_IN + 4, U_IN + 8, lambda i: v[:, i + 2, :, 0:UW])
                pairs(U_IN + 8, U_IN + 16, rows(a["w_in"], UW))
                pairs(U_GF, U_GF + 4, rows(a["w_gate"], 0))
                sp.wait_ge(z_ready, l + 1)
                for n0, out in ((768, o["new_k"]), (1280, o["new_v"])):
                    sp.dma_start(out[bass.ds(l, 1)].rearrange("o h t d -> (o t) h d"),
                                 Z[:, 0, n0:n0 + 512].rearrange("p (h d) -> p h d", h=HEADS)).then_inc(kv_stored, 16)
                wg = a["w_gate"][bass.ds(l, 1)].rearrange("o (k s p) n -> p (o k) s n", p=P, s=2)
                pairs(U_GF + 4, U_WF, lambda i: wg[:, i + 2, :, 0:UW])
                pairs(U_WF, U_GP, rows(a["w_fourier"], 0))
                pairs(U_GP, U_GP + 4, rows(a["w_gate"], 2 * UW))
                sp.wait_ge(gtb_free, l * 2 + 1)
                sp.dma_start(GTB, a["b_gate"][bass.ds(l, 1), 2:3, :].to_broadcast([P, TB, D])).then_inc(bgate_landed, 16)
                pairs(U_GP + 4, U_WP, lambda i: wg[:, i + 2, :, 2 * UW:3 * UW])
                pairs(U_WP, U_GA, rows(a["w_pool"], 0))
                pairs(U_GA, U_GA + 4, rows(a["w_gate"], UW))
                sp.wait_ge(gtb_free, l * 2 + 2)
                sp.dma_start(GTB, a["b_gate"][bass.ds(l, 1), 1:2, :].to_broadcast([P, TB, D])).then_inc(bgate_landed, 16)
                pairs(U_GA + 4, U_WA, lambda i: wg[:, i + 2, :, UW:2 * UW])
                pairs(U_WA, U_OUT, rows(a["w_attn"], 0))
                sp.wait_ge(att_done, l + 1)
                for s in range(2):
                    sp.dma_start(Z[:, s, D:2 * D], gate_rows[0, s:s + 1, :].to_broadcast([P, D])).then_inc(gate1_landed, 16)
                pairs(U_OUT, U_Q, rows(a["w_out"], 0))
                pairs(U_Q, U_Q + 4, rows(a["peer_wq"], 0))
                sp.wait_ge(out_done, l + 1)
                sp.dma_start(KEYT, a["keys"][bass.ds(l, 1)].rearrange("o p h n -> (o p) h n")).then_inc(keys_landed, 16)
                wq = a["peer_wq"][bass.ds(l, 1)].rearrange("o (k s p) n -> p (o k) s n", p=P, s=2)
                pairs(U_Q + 4, U_Q + 8, lambda i: wq[:, i + 2, :, 0:UW])
                pairs(U_Q + 8, U_PEER, rows(a["peer_wq"], UW))
                def group(g, s, used):
                    if used is not None:
                        sp.wait_ge(w_ready, l * KEYS + used + GN + 1)
                    sp.dma_start(GCH[:, s].rearrange("p t n -> p (t n)"),
                                 gmat[bass.ds(g, 1)].rearrange("o p n -> (o p) n")).then_inc(group_landed[s], 16)

                def expert_pair(i, n):
                    sp.wait_ge(lo_ready, l * UNITS + i * (2 * BODY) + 2 * n + (U_PEER + 2))
                    sp.dma_start(raw[:, 0:2, :], a["ut"][bass.ds(l * KEYS + i * BODY + n, 2)].rearrange("s p n -> p s n")).then_inc(pair_landed[0], 16)
                    sp.wait_ge(lo_ready, l * UNITS + i * (2 * BODY) + 2 * n + (U_PEER + 4))
                    sp.dma_start(raw[:, 2:4, :], a["peer_v"][bass.ds(l * P, P), bass.ds(i * BODY + n, 2), :]).then_inc(pair_landed[1], 16)

                expert_pair(0, 0)
                with sp.Fori(0, NSTG // 2) as g:
                    for s in range(2):
                        sp.wait_ge(stage_ready, l * NSTG + g * 2 + s + 1)
                        sp.dma_start(gmat.rearrange("g p (t n) -> p g t n", n=GN)[:, :, bass.ds(g * (2 * GT) + s * GT, GT), :]
                                     .rearrange("p g t n -> p g (t n)"),
                                     STG[:, s].rearrange("p g t n -> p g (t n)")).then_inc(stage_stored[s], 16)
                for s in range(2):
                    sp.wait_ge(stage_stored[s], l * (8 * NSTG) + 8 * NSTG)
                group(0, 0, None)
                for s in range(2):
                    sp.dma_start(GATE2[:, s, :], gate_rows[1, s:s + 1, :].to_broadcast([P, D])).then_inc(gate2_landed, 16)
                def experts(i, last):
                    for k in range(BODY // 2):
                        n = 2 * k
                        if not (last and n == BODY - 2):
                            expert_pair(i, n + 2)
                        if n == GN // 2:
                            group(i * 2 + 1, 1, i * BODY)
                        if n == BODY - GN // 2 and not last:
                            group(i * 2 + 2, 0, i * BODY + GN)

                with sp.Fori(0, KEYS // BODY - 1) as i:
                    experts(i, False)
                experts(KEYS // BODY - 1, True)
            sp.wait_ge(layer_free, DEPTH + 1)
            sp.dma_start(GFIN, a["g_final"].to_broadcast([P, D])).then_inc(gfin_landed, 16)
            sp.wait_ge(y_ready, 1)
            sp.dma_start(o["y_prompt"], X[:, 0, :]).then_inc(y_stored, 16)
            sp.dma_start(o["y_sample"].rearrange("(b p) n -> p b n", p=P), X[:, 1:3, :]).then_inc(y_stored, 16)
            sp.wait_ge(kv_stored, 32 * DEPTH)
            sp.wait_ge(y_stored, 32)

        @block.gpsimd
        def _(pool):
            pool.sem_inc(lo_ready, SLOTS)
            pool.wait_ge(start_ready, 1)

            def root(n):
                pool.wait_ge(ms_ready, n)
                pool.tensor_tensor(rstd[:], ms[:], nhalf[:], ALU.pow).then_inc(rstd_ready, 1)

            def lo(value, slot):
                pool.wait_ge(hi_ready, value)
                pool.tensor_tensor(wlo[:, slot], raw[:, slot], whi[:, slot].bitcast(F32), ALU.subtract).then_inc(lo_ready, 1)

            with pool.Fori(0, DEPTH) as l:
                root(l * 2 + 1)
                with pool.Fori(0, (U_Q + 4) // 4) as i:
                    for s in range(SLOTS):
                        lo(l * UNITS + i * 4 + s + 1, s)
                root(l * 2 + 2)
                with pool.Fori(0, (U_PEER - U_Q) // 4) as i:
                    for s in range(SLOTS):
                        lo(l * UNITS + i * 4 + U_Q + 4 + s + 1, s)
                for t in range(TB):
                    s = t % 2
                    pool.wait_ge(place_ready, l * TB + t + 1)
                    if t >= 2:
                        pool.wait_ge(aux_done, l * AUXS + X_IT + t - 1)
                    for q in range(2):
                        index = SIF[:, s, :, q, :].rearrange("p h (o a) -> p h o a", o=1).to_broadcast([P, HEADS, TOPK, TOPK])
                        pool.tensor_tensor(OH[q], OH[q], index, ALU.mult)
                    pool.drain()
                    for w in (8, 4, 2, 1):
                        for q in range(2):
                            out = OH[q][:, :, :, 0:w] if w > 1 else SEL[:, s, q].rearrange("p h (k o) -> p h k o", o=1)
                            pool.tensor_tensor(out, OH[q][:, :, :, 0:w], OH[q][:, :, :, w:2 * w], ALU.add)
                        x = pool.drain()
                    x.then_inc(index_ready, 1)
                with pool.Fori(0, T // (2 * GT)) as g:
                    for n in range(8):
                        if n not in BY_POOL:
                            continue
                        if n in (BY_POOL[0], min(x for x in BY_POOL if x > 3)):
                            pool.wait_ge(selc_ready, l * (T // GT) + g * 2 + n // 4 + 1)
                        pool.wait_ge(aux_done, l * AUXS + g * 8 + X_G + n - 3)
                        pool.sem_inc(hot2_open, 1)
                        for j in range(4 * n, 4 * n + 4):
                            i2 = SELC[:, n // 4, 1, j % GT:j % GT + 1]
                            x = pool.tensor_scalar(HOT2[:, j % 16, :], iota[:], i2, None, ALU.is_equal)
                        x.then_inc(hot2_ready, 1)
                with pool.Fori(1, 2 * KEYS // 4) as i:
                    for s in range(SLOTS):
                        lo(l * UNITS + i * 4 + U_PEER + s + 1, s)
            root(2 * DEPTH + 1)

        @block.scalar
        def _(act):
            for t, src in ((cond, "cond"), (ident, "ident")):
                act.dma_start(t[:], a[src]).then_inc(first_landed, 16)
            act.dma_start(X[:, 0, :], a["x_prompt"]).then_inc(x_landed, 16)
            act.dma_start(X[:, 1:3, :], a["x_sample"].rearrange("(b p) n -> p b n", p=P)).then_inc(x_landed, 16)
            act.wait_ge(first_landed, 32)
            act.activation(cond[:], cond[:], ACT.Silu).then_inc(silu_ready, 1)
            for t, src in ((iota, "iota"), (mask, "mask"), (dft_c, "dft_c"), (dft_p, "dft_p"),
                           (dft_s, "dft_s"), (pool_p, "pool_p"), (pool_s, "pool_s")):
                act.dma_start(t[:], a[src]).then_inc(const_landed, 16)
            rb = a["rel_bias"].rearrange("l h r c -> (l h) (r c)")
            act.dma_start(bias_rows, rb.rearrange("n (o c) -> n o c", o=1).to_broadcast([DEPTH * HEADS, GRID, RB]))\
               .then_inc(bias_rows_stored, 16)
            act.wait_ge(bias_rows_stored, 16)
            for n in range(DEPTH):
                for h in range(HEADS):
                    src = bass.AP(tensor=bias_rows.tensor, offset=(n * HEADS + h) * GRID * RB + 4 * 31 + 15,
                                  ap=[[RB - 1, GRID], [31, 7], [1, GRID]])
                    act.dma_start(toeplitz[n, :, h, :].rearrange("q (r k) -> q r k", r=7), src).then_inc(toeplitz_stored, 16)
            with act.Fori(0, DEPTH) as l:
                act.wait_ge(layer_free, l + 1)
                act.dma_start(BADA, a["b_ada"][bass.ds(l, 1)].to_broadcast([P, 6 * D])).then_inc(bada_landed, 16)
                act.dma_start(gcol[:], a["gcol"][bass.ds(l, 1)].rearrange("o p s k -> (o p) s k")).then_inc(cols_landed, 16)
                act.dma_start(pscale[:], a["pool_scale"][bass.ds(l, 1)].rearrange("o p s -> (o p) s")).then_inc(cols_landed, 16)
                for g in range(4):
                    act.dma_start(wpg[64 * (g % 2):64 * (g % 2) + 64, g // 2, 64 * (g % 2):64 * (g % 2) + 64],
                                  a["w_pool_grp"][bass.ds(l, 1), g].rearrange("o c e -> (o c) e")).then_inc(cols_landed, 16)

                def hi(u):
                    q = u // 2
                    act.wait_ge(pair_landed[q % 2], l * (8 * PAIRS) + 16 * (q // 2 + 1))
                    act.wait_ge(unit_used, l * USED + max(u + 1, 3))
                    act.activation(whi[:, u % SLOTS], raw[:, u % SLOTS], ACT.Copy).then_inc(hi_ready, 1)

                for u in range(U_IN, U_GF + 2):
                    hi(u)

                def exps(i):
                    n = P if i % TB == 0 else T
                    act.wait_ge(s_ready, l * STEPS + i + 1)
                    if i >= 2:
                        act.wait_ge(pt_ready, l * STEPS + i - 1)
                    act.activation(PR[:, i % 2, 0:n], S[:, i % 2, 0:n], ACT.Exp, bias=nmax[:, i % 2:i % 2 + 1],
                                   accum_out=rsum[:, i % 2:i % 2 + 1]).then_inc(p_ready, 1)

                def sigmoid(g):
                    for h in range(2):
                        act.wait_ge(gate_sum, l * 6 + 2 * g + h + 1)
                        v = GTB[:, :, h * HB:(h + 1) * HB]
                        act.activation(v, v, ACT.Sigmoid).then_inc(gate_ready, 1)

                for u in range(U_GF, U_OUT):
                    i = 2 * (u - U_GF)
                    hi(u + 2)
                    for kind, j in BESIDE[i] + BESIDE[i + 1]:
                        if kind == "s":
                            exps(j)
                    if u + 1 in (U_GP, U_GA):
                        sigmoid((U_GP, U_GA).index(u + 1))
                sigmoid(2)
                for u in range(U_OUT + 2, U_PEER + SLOTS):
                    hi(u)
                for t in range(TB):
                    act.wait_ge(top_ready, l * TB + t + 1)
                    act.activation(SEL[:, t % 2, 2], SEL[:, t % 2, 2], ACT.Exp).then_inc(exp_ready, 1)

                def stages(g, first):
                    for s in range(2):
                        if not first:
                            act.wait_ge(stage_stored[s], l * (8 * NSTG) + g * 16)
                        for j in range(4):
                            use = X_G + 4 * s + j
                            act.wait_ge(aux_done, l * AUXS + g * 8 + use + 1)
                            act.activation(STG[:, s, :, 4 * j:4 * j + 4, :].rearrange("p g t n -> p t g n"),
                                           aux[use % 2][:].rearrange("p (t g n) -> p t g n", t=4, n=GN), ACT.Copy)\
                               .then_inc(aux_free, 1)
                        act.drain().then_inc(stage_ready, 1)

                stages(0, True)
                with act.Fori(1, NSTG // 2) as g:
                    stages(g, False)

                def gelus(k):
                    for j in range(2):
                        use = X_U + j
                        act.wait_ge(aux_done, l * AUXS + k * 2 + use + 1)
                        act.wait_ge(w_ready, l * KEYS + k * 2 + j - 1 + GN + 1)
                        act.activation(ACTB[:, j], aux[use % 2][:, 0:T], ACT.Gelu_apprx_tanh).then_inc(act_ready, 1)

                with act.Fori(1, KEYS // 2) as k:
                    gelus(k - 1)
                    for j in range(4):
                        act.wait_ge(pair_landed[j // 2], l * (8 * PAIRS) + k * 16 + (4 * U_PEER + 16))
                        if j < 2:
                            act.wait_ge(aux_done, l * AUXS + k * 2 + X_U + j - 1)
                        else:
                            act.wait_ge(unit_used, l * USED + k * 2 + U_PEER + j - 3 + SLOTS)
                        act.activation(whi[:, j], raw[:, j], ACT.Copy).then_inc(hi_ready, 1)
                gelus(KEYS // 2 - 1)

        @block.tensor
        def _(pe):
            pe.sem_inc(unit_used, SLOTS)
            pe.wait_ge(first_landed, 32)
            with pe.Fori(0, DEPTH) as l:
                def unit(u, lt, chunk, use, first, last, beside=None):
                    pe.wait_ge(lo_ready, l * UNITS + u + 1 + SLOTS)
                    s = u % SLOTS
                    for h in range(2):
                        if beside and h:
                            beside()
                        for t in range(TB):
                            if first:
                                pe.wait_ge(acc_free, l * ACCS + use + TB * h + t + 1)
                            lh, ll = (x[:, chunk, t * P:(t + 1) * P] for x in lt)
                            for n, (x, w) in enumerate(((lh, whi), (lh, wlo), (ll, whi))):
                                mm = pe.matmul(accum(use + TB * h + t)[:], x, w[:, s, h * HB:(h + 1) * HB],
                                               start=first and n == 0, stop=last and n == 2)
                            if last:
                                mm.then_inc(acc_done, 1)
                    (pe.drain() if last else mm).then_inc(unit_used, 1)

                def bank(use):
                    pe.wait_ge(aux_free, l * X_U + use + 1)
                    return aux[use % 2]

                pe.wait_ge(cond_ready, l + 1)
                for p in range(6):
                    for k in range(KC):
                        n = p * KC + k
                        q = n // 2
                        if k % 2 == 0:
                            pe.wait_ge(ada_landed[q % 2], l * (8 * 24) + 16 * (q // 2 + 1))
                        for h in range(2):
                            use = C_ADA + 2 * p + h
                            if k == 0:
                                pe.wait_ge(acc_free, l * ACCS + use + 1)
                            mm = pe.matmul(accum(use)[:], CB[:, k, :], raw[:, n % SLOTS, h * HB:(h + 1) * HB],
                                           start=(k == 0), stop=(k == KC - 1))
                            if k == KC - 1:
                                mm.then_inc(acc_done, 1)
                        (mm if k < KC - 1 else pe.drain()).then_inc(ada_used, 1)
                pe.wait_ge(modr_ready, l * 6 + 6)
                for n, p in enumerate((0, 1, 3, 4)):
                    for q in range(2):
                        b = bank(X_MOD + 2 * n + q)
                        for j in range(4):
                            at = p * D + (4 * q + j) * P
                            mm = pe.transpose(b[:, j * P:(j + 1) * P], MODR[:, at:at + P], ident[:])
                        mm.then_inc(aux_done, 1)

                def turn(src, base, k):
                    b = bank(base + k)
                    for t in range(TB):
                        mm = pe.transpose(b[:, t * P:(t + 1) * P], src[:, t, k * P:(k + 1) * P], ident[:])
                    mm.then_inc(aux_done, 1)

                def turned_pass(src, base, ready, u0, use, ht0):
                    for k in range(KC + 2):
                        if k < KC:
                            ready(k)
                            turn(src, base, k)
                        if k >= 2:
                            pe.wait_ge(ht_ready, l * (3 * KC) + ht0 + k - 1)
                            unit(u0 + k - 2, (LTh, LTl), k - 2, use, k == 2, k == KC + 1)

                def xn(n):
                    return lambda k: pe.wait_ge(xn_ready, l * 2 + n) if k == 0 else None

                turned_pass(XN, X_HT, xn(1), U_IN, C_IN, 0)
                for k in range(KC):
                    unit(U_IN + KC + k, (LTh, LTl), k, C_IN + 6, k == 0, k == KC - 1)

                def small(kind, i):
                    if (kind, i) == ("z", 2):
                        pe.wait_ge(z_ready, l + 1)
                    if (kind, i) == ("f", 0):
                        pe.wait_ge(zf_ready, l + 1)
                        pe.wait_ge(const_landed, 16 * 7)
                    if (kind, i) == ("p", 0):
                        pe.wait_ge(zcs_ready, l + 1)
                    if (kind, i) == ("y", 0):
                        pe.wait_ge(dt_ready, l + 1)
                        pe.wait_ge(cols_landed, l * 96 + 96)
                    if (kind, i) == ("s", 0):
                        pe.wait_ge(qk_ready, l + 1)
                        pe.wait_ge(att_landed, l * (16 * 6) + 16 * 6)
                    b = bank(USE[kind, i])
                    h, t = i // TB, i % TB
                    r = 64 * (h % 2)
                    if kind == "z":
                        for t in range(TB):
                            mm = pe.transpose(b[:, t * P:(t + 1) * P], Z[:, t, i * P:(i + 1) * P], ident[:])
                    elif kind == "f":
                        for c in range(2):
                            mm = pe.matmul(b[:, c * 256:(c + 1) * 256], ZFT[:, c, i * P:(i + 1) * P], dft_c[:], start=True, stop=True)
                    elif kind == "p":
                        for q in range(2):
                            pe.matmul(b[:, 0:P], ZCS[:, 0, i, q * P:(q + 1) * P], dft_p[:, q, :], start=(q == 0), stop=(q == 1))
                        for n in range(4):
                            t, q = n // 2, n % 2
                            mm = pe.matmul(b[:, P:T], ZCS[:, 1 + t, i, q * P:(q + 1) * P], dft_s[:, t, q, :], start=(n == 0), stop=(n == 3))
                    elif kind == "d":
                        for g2 in range(2):
                            g = 2 * i + g2
                            out = b[64 * g2:64 * g2 + 64, :]
                            pe.matmul(out[:, 0:P], Z[:, 0, 1792 + 64 * g:1856 + 64 * g], pool_p[:, g, :], start=True, stop=True)
                            for t in range(2):
                                mm = pe.matmul(out[:, P:T], Z[:, 1 + t, 1792 + 64 * g:1856 + 64 * g], pool_s[:, t, g, :],
                                               start=(t == 0), stop=(t == 1))
                    elif kind == "y":
                        mm = pe.matmul(b[:, 0:T], wpg[:, i, :], DT[:, i, :], start=True, stop=True)
                    elif kind == "s":
                        q = QT[r:r + 64, h // 2, t * P:(t + 1) * P]
                        if t == 0:
                            mm = pe.matmul(b[:, 0:P], q, KT[r:r + 64, h // 2, 0:P], start=True, stop=True)
                        else:
                            pe.matmul(b[:, 0:256], q, KT[r:r + 64, h // 2, P:T], start=True, stop=True)
                            mm = pe.matmul(b[:, 256:T], q, KCT[r:r + 64, h // 2, :], start=True, stop=True)
                    elif kind == "t":
                        pe.wait_ge(pn_ready, l * STEPS + i + 1)
                        for n in range(1 if t == 0 else 3):
                            mm = pe.transpose(b[:, n * P:(n + 1) * P], PR[:, i % 2, n * P:(n + 1) * P], ident[:])
                    else:
                        pe.wait_ge(pt_ready, l * STEPS + i + 1)
                        v = 1280 + DH * h
                        vs = [Z[:, 0, v:v + DH]] if t == 0 else [Z[:, 1, v:v + DH], Z[:, 2, v:v + DH], VC[:, DH * h:DH * h + DH]]
                        for n, x in enumerate(vs):
                            mm = pe.matmul(b[r:r + 64, 0:P], x, PT[:, i % 2, n, :], start=(n == 0), stop=(n == len(vs) - 1))
                    mm.then_inc(aux_done, 1)

                passes = [(U_GF, KC, (LTh, LTl), 0, C_GF), (U_WF, 2, (BTh, BTl), 0, C_WF),
                          (U_GP, KC, (LTh, LTl), 0, C_GP), (U_WP, 2, (BTh, BTl), 6, C_WP),
                          (U_GA, KC, (LTh, LTl), 0, C_GA), (U_WA, 4, (BTh, BTl), 2, C_WA)]
                for u0, n, lt, c0, use in passes:
                    if u0 == U_WF:
                        pe.wait_ge(four_done, l + 1)
                    if u0 == U_WA:
                        pe.wait_ge(att_done, l + 1)
                    for k in range(n):
                        i = 2 * (u0 + k - U_GF)

                        def beside(i=i):
                            for kind, j in BESIDE[i]:
                                small(kind, j)

                        beside()
                        unit(u0 + k, lt, c0 + k, use, k == 0, k == n - 1, lambda i=i: beside(i + 1))
                turned_pass(M, X_MT, lambda k: pe.wait_ge(m_ready, l * 2 + k // 4 + 1) if k % 4 == 0 else None,
                            U_OUT, C_OUT, KC)
                turned_pass(XN, X_H2, xn(2), U_Q, C_Q, 2 * KC)

                def query(base, k):
                    b = bank(base + k % 8)
                    for t in range(TB):
                        mm = pe.transpose(b[:, t * P:(t + 1) * P], Z[:, t, k * P:(k + 1) * P], ident[:])
                    mm.then_inc(aux_done, 1)

                def score(base, m, n):
                    t, q = n // 2, 2 * m + n % 2
                    b = bank(base + n)
                    for j in range(4):
                        mm = pe.matmul(b[:, j * P:(j + 1) * P], PQT[:, 4 * q + j, t * P:(t + 1) * P], KEYT[:, 4 * q + j, :],
                                       start=True, stop=True)
                    mm.then_inc(aux_done, 1)

                for k in range(KC):
                    if k == 1:
                        pe.wait_ge(pq_ready, l * 2 + 1)
                    if 1 <= k < 5:
                        for n in range(2):
                            query(X_QA, 2 * (k - 1) + n)
                    if k == 5:
                        pe.wait_ge(pqt_ready, l * 2 + 1)
                        pe.wait_ge(keys_landed, l * 16 + 16)
                    if k >= 5:
                        for n in range(2):
                            score(X_SA, 0, 2 * (k - 5) + n)
                    unit(U_Q + KC + k, (LTh, LTl), k, C_Q + 6, k == 0, k == KC - 1)
                pe.wait_ge(pq_ready, l * 2 + 2)
                for k in range(8, 16):
                    query(X_QB, k)
                pe.wait_ge(pqt_ready, l * 2 + 2)
                for n in range(6):
                    score(X_SB, 1, n)
                for t in range(TB):
                    pe.wait_ge(index_ready, l * TB + t + 1)
                    pe.wait_ge(sel_ready, l * TB + t + 1)
                    b = bank(X_IT + t)
                    for q in range(3):
                        mm = pe.transpose(b[:, q * P:(q + 1) * P], SELf[:, t % 2, q, :], ident[:])
                    mm.then_inc(aux_done, 1)
                with pe.Fori(0, T // (2 * GT)) as g:
                    for j in range(2 * GT):
                        n = j // 4
                        use = X_G + n
                        if j % 4 == 0:
                            pe.wait_ge(aux_free, l * X_U + g * 8 + use + 1)
                            pe.wait_ge(hot1_ready, l * (T // 4) + g * 8 + n + 1)
                            if n in BY_POOL:
                                pe.wait_ge(hot2_ready, l * (T // (2 * GT) * len(BY_POOL)) + g * len(BY_POOL) + BY_POOL.index(n) + 1)
                        mm = pe.matmul(aux[use % 2][:, (j % 4) * P:(j % 4 + 1) * P], HOT1[:, j % 16, :], HOT2[:, j % 16, :],
                                       start=True, stop=True)
                        if j % 4 == 3:
                            mm.then_inc(aux_done, 1)
                for b in range(6):
                    pe.wait_ge(acc_free, l * ACCS + C_V + b + 1)

                def experts(k, first, last):
                    for j in range(2):
                        pe.wait_ge(lo_ready, l * UNITS + k * 4 + U_PEER + j + 1 + SLOTS)
                        if first:
                            pe.wait_ge(aux_free, l * X_U + X_U + j + 1)
                        else:
                            pe.wait_ge(act_ready, l * KEYS + k * 2 + j - 1)
                        b = aux[(X_U + j) % 2]
                        for c in range(KC):
                            for n, (w, x) in enumerate(((whi, LTh), (whi, LTl), (wlo, LTh))):
                                mm = pe.matmul(b[:, 0:T], w[:, j, c * P:(c + 1) * P], x[:, c, :],
                                               start=(c == 0 and n == 0), stop=(c == KC - 1 and n == 2))
                        mm.then_inc(aux_done, 1)
                    for j in range(2):
                        pe.wait_ge(lo_ready, l * UNITS + k * 4 + U_PEER + 2 + j + 1 + SLOTS)
                        pe.wait_ge(w_ready, l * KEYS + k * 2 + j + 1 + GN + 1)
                        for h in range(2):
                            for t in range(TB):
                                wh, wl = (x[:, j, t * P:(t + 1) * P] for x in (BTh, BTl))
                                for n, (x, w) in enumerate(((wh, whi), (wh, wlo), (wl, whi))):
                                    mm = pe.matmul(accum(C_V + TB * h + t)[:], x, w[:, 2 + j, h * HB:(h + 1) * HB],
                                                   start=(first and j == 0 and n == 0), stop=(last and j == 1 and n == 2),
                                                   skip_group_check=True)
                                if last and j == 1:
                                    mm.then_inc(acc_done, 1)
                        (pe.drain() if last and j == 1 else mm).then_inc(unit_used, 1)

                experts(0, True, False)
                with pe.Fori(1, KEYS // 2 - 1) as k:
                    experts(k, False, False)
                experts(KEYS // 2 - 1, False, True)

        @block.vector
        def _(dve):
            dve.memset(nhalf[:], -0.5)
            dve.memset(wpg[:], 0.0)
            dve.drain().then_inc(start_ready, 1)
            dve.sem_inc(acc_free, 6)
            dve.sem_inc(aux_free, 2)
            dve.sem_inc(layer_free, 1)
            dve.sem_inc(w_ready, GN + 1)
            dve.wait_ge(x_landed, 32)
            dve.wait_ge(silu_ready, 1)

            def mean_square():
                for t in range(TB):
                    dve.tensor_tensor_reduce(XN[:, t], X[:, t], X[:, t], 1.0, 0.0, ALU.mult, ALU.add, ms[:, t:t + 1])
                dve.drain()
                dve.tensor_scalar(ms[:], ms[:], 1.0 / D, EPS, ALU.mult, ALU.add).then_inc(ms_ready, 1)

            def normalise(n):
                dve.wait_ge(rstd_ready, n)
                for t in range(TB):
                    dve.tensor_scalar(XN[:, t], X[:, t], rstd[:, t:t + 1], None, ALU.mult)

            with dve.Fori(0, DEPTH) as l:
                def bank(use):
                    dve.wait_ge(aux_done, l * AUXS + use + 1)
                    return aux[use % 2]

                def accu(use):
                    dve.wait_ge(acc_done, l * ACCS + use + 1)
                    return accum(use)

                def split(h, lo, src):
                    dve.tensor_copy(h, src)
                    dve.drain()
                    return dve.tensor_tensor(lo, src, h.bitcast(F32), ALU.subtract)

                for s in range(2):
                    dve.tensor_copy(CB[:, :, 64 * s:64 * s + 64],
                                    cond[:, s, :].rearrange("p (k o) -> p k o", o=1).to_broadcast([P, KC, 64]))
                dve.drain().then_inc(cond_ready, 1)
                mean_square()
                dve.wait_ge(bada_landed, l * 16 + 16)
                for p in range(6):
                    for h in range(2):
                        at = p * D + h * HB
                        dve.tensor_tensor(MODR[:, at:at + HB], accu(C_ADA + 2 * p + h)[:], BADA[:, at:at + HB],
                                          ALU.add).then_inc(acc_free, 1)
                    dve.drain().then_inc(modr_ready, 1)
                normalise(l * 2 + 1)
                dve.drain().then_inc(xn_ready, 1)
                for n in range(4):
                    for q in range(2):
                        b = bank(X_MOD + 2 * n + q)
                        dve.tensor_copy(modc[:, n, :, 4 * q:4 * q + 4],
                                        b[:].rearrange("p (k s c) -> p s k c", k=4, s=2)[:, :, :, 0]).then_inc(aux_free, 1)
                dve.drain().then_inc(mods_done, 1)
                dve.wait_ge(cols_landed, l * 96 + 96)
                for n in range(2):
                    for s in range(2):
                        dve.scalar_tensor_tensor(modc[:, 2 * n + 1, s, :], modc[:, 2 * n + 1, s, :], 1.0, gcol[:, n, :],
                                                 ALU.add, ALU.mult)
                dve.drain()

                def columns(base, chunks, evacuate):
                    for k in range(KC + 2):
                        if k < KC:
                            evacuate(k, bank(base + k)).then_inc(aux_free, 1)
                        if 1 <= k <= KC:
                            dve.tensor_copy(LTh[:, k - 1], chunks[:, k - 1])
                        if k >= 2:
                            dve.tensor_tensor(LTl[:, k - 2], chunks[:, k - 2], LTh[:, k - 2].bitcast(F32), ALU.subtract)
                        x = dve.drain()
                        if k >= 2:
                            x.then_inc(ht_ready, 1)

                def modulate(n):
                    def step(k, b):
                        for s, (c0, c1) in enumerate(((0, P), (P, T))):
                            x = dve.tensor_scalar(HRAW[:, k, c0:c1], b[:, c0:c1], modc[:, 2 * n + 1, s, k:k + 1],
                                                  modc[:, 2 * n, s, k:k + 1], ALU.mult, ALU.add)
                        return x
                    return step

                def projected(use, n0):
                    for h in range(2):
                        for t in range(TB):
                            dve.tensor_copy(Z[:, t, n0 + h * HB:n0 + (h + 1) * HB], accu(use + TB * h + t)[:]).then_inc(acc_free, 1)

                columns(X_HT, HRAW, modulate(0))
                projected(C_IN, 0)
                projected(C_IN + 6, D)
                dve.drain().then_inc(z_ready, 1)
                dve.wait_ge(const_landed, 16 * 7)
                dve.wait_ge(att_landed, l * (16 * 6) + 16 * 6)
                bv = BIAS.rearrange("p b h (r n) -> p (b h r) n", r=4)
                dve.tensor_tensor(bv, bv, mask[:].rearrange("p (o n) -> p o n", o=1).to_broadcast([P, 2 * HEADS * 4, GRID]), ALU.add)
                dve.drain()

                def small(kind, i):
                    h, t = i // TB, i % TB
                    s, r = i % 2, 64 * (i // TB % 2)
                    b = bank(USE[kind, i])
                    if kind == "z":
                        if i < 2:
                            x = dve.tensor_copy(ZFT[:, i], b[:, 0:T])
                        elif i < 6:
                            x = dve.tensor_scalar(QT[:, i - 2], b[:, 0:T], DH ** -0.5, None, ALU.mult)
                        else:
                            x = dve.tensor_copy(KT[:, i - 6], b[:, 0:T])
                        x.then_inc(aux_free, 1)
                        if i in (1, 9):
                            dve.drain().then_inc(zf_ready if i == 1 else qk_ready, 1)
                    elif kind == "f":
                        dve.tensor_copy(ZCS[:, i].rearrange("p c n -> p (c n)"), b[:]).then_inc(aux_free, 1)
                        if i == 2:
                            dve.drain().then_inc(zcs_ready, 1)
                    elif kind == "p":
                        split(BTh[:, i], BTl[:, i], b[:, 0:T]).then_inc(aux_free, 1)
                    elif kind == "d":
                        dve.tensor_copy(DT[:, i], b[:, 0:T]).then_inc(aux_free, 1)
                        if i == 1:
                            dve.drain().then_inc(dt_ready, 1)
                    elif kind == "y":
                        dve.tensor_scalar(ZFT[:, i], b[:, 0:T], pscale[:, i:i + 1], None, ALU.mult).then_inc(aux_free, 1)
                        dve.drain()
                        split(BTh[:, 6 + i], BTl[:, 6 + i], ZFT[:, i])
                        if i == 1:
                            dve.drain().then_inc(four_done, 1)
                    elif kind == "s":
                        if t == 0:
                            dve.tensor_copy(S[:, s, 0:P], b[:, 0:P]).then_inc(aux_free, 1)
                        else:
                            dve.tensor_tensor(S[:, s, 0:256], b[:, 0:256], BIAS[:, t - 1, h, :], ALU.add)
                            dve.tensor_copy(S[:, s, 256:T], b[:, 256:T]).then_inc(aux_free, 1)
                        dve.drain()
                        dve.tensor_reduce(nmax[:, s:s + 1], S[:, s, 0:P if t == 0 else T], AX, ALU.max, negate=True).then_inc(s_ready, 1)
                    elif kind == "t":
                        n = 1 if t == 0 else 3
                        dve.tensor_copy(PT[:, s, 0:n, :].rearrange("p k q -> p (k q)"), b[:, 0:n * P]).then_inc(aux_free, 1)
                        dve.drain().then_inc(pt_ready, 1)
                    elif kind == "v":
                        at = (slice(r, r + 64), 2 + h // 2, slice(t * P, (t + 1) * P))
                        split(BTh[at], BTl[at], b[r:r + 64, 0:P]).then_inc(aux_free, 1)

                def probabilities(i):
                    s, n = i % 2, P if i % TB == 0 else T
                    dve.wait_ge(p_ready, l * STEPS + i + 1)
                    dve.reciprocal(rsum[:, s:s + 1], rsum[:, s:s + 1])
                    dve.drain()
                    dve.tensor_scalar(PR[:, s, 0:n], PR[:, s, 0:n], rsum[:, s:s + 1], None, ALU.mult).then_inc(pn_ready, 1)

                def gate(n, use):
                    dve.wait_ge(bgate_landed, l * 48 + 16 * (n + 1))
                    for h in range(2):
                        for t in range(TB):
                            g = GTB[:, t, h * HB:(h + 1) * HB]
                            dve.tensor_tensor(g, g, accu(use + TB * h + t)[:], ALU.add).then_inc(acc_free, 1)
                        dve.drain().then_inc(gate_sum, 1)

                def merge(n, use):
                    if n == 0:
                        dve.wait_ge(kv_stored, l * 32 + 32)
                    for h in range(2):
                        dve.wait_ge(gate_ready, l * 6 + 2 * n + h + 1)
                        for t in range(TB):
                            g, m = (x[:, t, h * HB:(h + 1) * HB] for x in (GTB, M))
                            dve.tensor_tensor(g if n else m, g, accu(use + TB * h + t)[:], ALU.mult).then_inc(acc_free, 1)
                        if n:
                            dve.drain()
                            g, m = (x[:, :, h * HB:(h + 1) * HB] for x in (GTB, M))
                            dve.tensor_tensor(m, m, g, ALU.add)
                        x = dve.drain()
                        if n == 2:
                            x.then_inc(m_ready, 1)
                    if n < 2:
                        x.then_inc(gtb_free, 1)

                for i in range(U_OUT - U_GF):
                    u = U_GF + i
                    for half in range(2):
                        for kind, j in BESIDE[2 * i + half]:
                            small(kind, j)
                        for kind, j in BESIDE[2 * i + half]:
                            if kind == "s":
                                probabilities(j)
                    if u == U_WA - 1:
                        dve.drain().then_inc(att_done, 1)
                    for u1, what, n, use in ((U_WF, gate, 0, C_GF), (U_GP, merge, 0, C_WF), (U_WP, gate, 1, C_GP),
                                             (U_GA, merge, 1, C_WP), (U_WA, gate, 2, C_GA), (U_OUT, merge, 2, C_WA)):
                        if u + 1 == u1:
                            what(n, use)
                columns(X_MT, MRAW, lambda k, b: dve.tensor_copy(MRAW[:, k], b[:, 0:T]))

                def residual(use, gates):
                    parts = [(h, t) for h in range(2) for t in range(TB)]
                    for n in range(7):
                        if n < 6:
                            h, t = parts[n]
                            dve.tensor_tensor(XTMP[:, n % 2], accu(use + n)[:], gates[:, min(t, 1), h * HB:(h + 1) * HB],
                                              ALU.mult).then_inc(acc_free, 1)
                        if n:
                            h, t = parts[n - 1]
                            at = slice(h * HB, (h + 1) * HB)
                            dve.tensor_tensor(X[:, t, at], X[:, t, at], XTMP[:, (n - 1) % 2], ALU.add)
                        dve.drain()

                dve.wait_ge(gate1_landed, l * 32 + 32)
                residual(C_OUT, Z[:, 0:2, D:2 * D])
                dve.sem_inc(out_done, 1)
                mean_square()
                normalise(l * 2 + 2)
                dve.drain().then_inc(xn_ready, 1)
                columns(X_H2, HRAW, modulate(1))
                projected(C_Q, 0)
                dve.drain().then_inc(pq_ready, 1)

                def retrieval(m, xq, xs):
                    for k in range(8):
                        dve.tensor_copy(PQT[:, 8 * m + k], bank(xq + k)[:, 0:T]).then_inc(aux_free, 1)
                    dve.drain().then_inc(pqt_ready, 1)
                    for n in range(6):
                        t, q = n // 2, 2 * m + n % 2
                        dve.tensor_copy(Z[:, t, q * HB:(q + 1) * HB], bank(xs + n)[:]).then_inc(aux_free, 1)
                    dve.drain()

                def top16(rows):
                    for r in range(2):
                        for v, m, i in rows:
                            dve.max(m[:, 8 * r:8 * r + 8], v)
                        dve.drain()
                        for v, m, i in rows:
                            dve.max_index(i[:, 8 * r:8 * r + 8], m[:, 8 * r:8 * r + 8], v)
                        if r == 0:
                            dve.drain()
                            for v, m, i in rows:
                                dve.match_replace(v, m[:, 0:8], v, -3.0e38)
                            dve.drain()

                def top_keys(t, m):
                    top16([(Z[:, t, k * P:(k + 1) * P], SV[:, t, k, :], SI[:, t, k, :]) for k in range(8 * m, 8 * m + 8)])
                    dve.drain()

                retrieval(0, X_QA, X_SA)
                for t in range(2):
                    top_keys(t, 0)
                projected(C_Q + 6, D)
                dve.drain().then_inc(pq_ready, 1)
                retrieval(1, X_QB, X_SB)
                top_keys(2, 0)

                def selected(t):
                    b = bank(X_IT + t)
                    dve.tensor_copy(SELT[:, :, t * P:(t + 1) * P], b[:, 0:3 * P].rearrange("p (q t) -> p q t", q=3)).then_inc(aux_free, 1)
                    dve.drain()

                for t in range(TB):
                    s = t % 2
                    top_keys(t, 1)
                    if t >= 2:
                        dve.wait_ge(index_ready, l * TB + t - 1)
                    dve.tensor_copy(SIF[:, s].rearrange("p h q k -> p (h q) k"), SI[:, t])
                    sv = SV[:, t].rearrange("p (h q) k -> p h q k", q=2)
                    dve.tensor_tensor(CAND, sv[:, :, 0].rearrange("p h (a o) -> p h a o", o=1).to_broadcast([P, HEADS, TOPK, TOPK]),
                                      sv[:, :, 1].rearrange("p h (o b) -> p h o b", o=1).to_broadcast([P, HEADS, TOPK, TOPK]), ALU.add)
                    dve.drain()
                    top16([(CAND[:, h].rearrange("p a b -> p (a b)"), TOP[:, h, :], POS[:, h, :]) for h in range(HEADS)])
                    dve.drain()
                    dve.tensor_scalar(PA, POS, 4, None, ALU.logical_shift_right)
                    dve.tensor_scalar(PB, POS, TOPK - 1, None, ALU.bitwise_and)
                    dve.tensor_tensor(SEL[:, s, 2], TOP, TOP[:, :, 0:1].to_broadcast([P, HEADS, TOPK]), ALU.subtract)
                    dve.drain().then_inc(top_ready, 1)
                    dve.tensor_copy(PAB[:, s, 0], PA)
                    dve.tensor_copy(PAB[:, s, 1], PB)
                    dve.drain()
                    if t:
                        dve.wait_ge(index_ready, l * TB + t)
                    for q in range(2):
                        place = PAB[:, s, q].rearrange("p h (k o) -> p h k o", o=1).to_broadcast([P, HEADS, TOPK, TOPK])
                        number = iota[:, 0:TOPK].rearrange("p (x y a) -> p x y a", x=1, y=1).to_broadcast([P, HEADS, TOPK, TOPK])
                        dve.tensor_tensor(OH[q], place, number, ALU.is_equal)
                    dve.drain().then_inc(place_ready, 1)
                    if t:
                        selected(t - 1)
                    dve.wait_ge(exp_ready, l * TB + t + 1)
                    dve.tensor_reduce(hsum[:], SEL[:, s, 2], AX, ALU.add)
                    dve.drain()
                    dve.reciprocal(hsum[:], hsum[:])
                    dve.drain()
                    dve.tensor_tensor(SEL[:, s, 2], SEL[:, s, 2], hsum[:].rearrange("p (h o) -> p h o", o=1).to_broadcast([P, HEADS, TOPK]), ALU.mult)
                    dve.drain().then_inc(sel_ready, 1)
                selected(TB - 1)
                with dve.Fori(0, T // (2 * GT)) as g:
                    for n in range(8):
                        s = n // 4
                        dve.wait_ge(aux_done, l * AUXS + g * 8 + X_G + n - 3)
                        if n % 4 == 0:
                            dve.tensor_copy(SELC[:, s], SELT[:, :, bass.ds(g * (2 * GT) + s * GT, GT)])
                            dve.drain().then_inc(selc_ready, 1)
                        for j in range(4 * n, 4 * n + 4):
                            i1, i2, gg = (SELC[:, s, q, j % GT:j % GT + 1] for q in range(3))
                            dve.tensor_scalar(HOT1[:, j % 16, :], iota[:], i1, gg, ALU.is_equal, ALU.mult)
                            if n not in BY_POOL:
                                dve.tensor_scalar(HOT2[:, j % 16, :], iota[:], i2, None, ALU.is_equal)
                        dve.drain().then_inc(hot1_ready, 1)
                with dve.Fori(0, KEYS // BODY) as i:
                    for n in range(BODY):
                        j, s = n % 2, n // GN
                        if n % GN == 0:
                            dve.wait_ge(group_landed[s], l * (8 * GGROUPS) + i * 16 + 16)
                        dve.wait_ge(act_ready, l * KEYS + i * BODY + n + 1)
                        dve.tensor_tensor(ACTB[:, j], ACTB[:, j], GCH[:, s, :, n % GN], ALU.mult)
                        dve.drain()
                        dve.wait_ge(unit_used, l * USED + i * BODY + U_PEER + n - 1 + SLOTS)
                        split(BTh[:, j], BTl[:, j], ACTB[:, j]).then_inc(w_ready, 1)
                dve.wait_ge(gate2_landed, l * 32 + 32)
                residual(C_V, GATE2)
                dve.drain().then_inc(layer_free, 1)
            mean_square()
            normalise(2 * DEPTH + 1)
            dve.drain()
            dve.wait_ge(gfin_landed, 16)
            for t in range(TB):
                dve.tensor_tensor(X[:, t], XN[:, t], GFIN, ALU.mult)
            dve.drain().then_inc(y_ready, 1)


def _constants():
    import numpy as np

    ident = np.eye(P, dtype=np.float32)
    iota = np.tile(np.arange(P, dtype=np.float32), (P, 1))
    qc = np.arange(P)[:, None] % GRID
    kc = np.arange(GRID)[None, :]
    start = np.clip(qc - 8, 0, GRID - 16)
    mask = np.where((kc >= start) & (kc < start + 16), 0.0, -1e30).astype(np.float32)

    def dft(n):
        angle = 2 * np.pi * (np.outer(np.arange(n), np.arange(n)) % n) / n
        return np.cos(angle) / np.sqrt(n), np.sin(angle) / np.sqrt(n)

    c64, s64 = dft(64)
    dft_c = np.zeros((P, 256))
    for g in range(2):
        dft_c[64 * g:64 * g + 64, 64 * g:64 * g + 64] = c64
        dft_c[64 * g:64 * g + 64, P + 64 * g:P + 64 * g + 64] = s64
    c, s = dft(128)
    dft_p = np.stack([c, -s], axis=1)
    c, s = dft(256)
    dft_s = np.stack([c, -s], axis=1).reshape(2, P, 2, 256).transpose(1, 0, 2, 3)

    def pool(n):
        out = np.zeros((n, 4, n))
        for g, w in enumerate((2, 4, 8, 16)):
            for t in range(n):
                a, b = max(t - w // 2, 0), min(t + w // 2, n)
                out[a:b, g, t] = 1.0 / (b - a)
                out[t, g, t] -= 1.0
        return out

    pool_p = pool(128)
    pool_s = pool(256).reshape(2, P, 4, 256).transpose(1, 0, 2, 3)
    tables = dict(ident=ident, iota=iota, mask=mask, dft_c=dft_c, dft_p=dft_p, dft_s=dft_s, pool_p=pool_p, pool_s=pool_s)
    return {k: np.ascontiguousarray(v, dtype=np.float32) for k, v in tables.items()}


_OUTS = {"y_prompt": (128, D), "y_sample": (256, D), "new_k": (DEPTH, HEADS, 128, DH), "new_v": (DEPTH, HEADS, 128, DH)}


def kernel(**inputs):
    import numpy as np
    import concourse.bacc as bacc
    from concourse.bass_utils import run_bass_kernel_spmd as run

    x = {k: np.asarray(v) for k, v in inputs.items()}
    arrays = dict(_constants())
    arrays["x_prompt"] = x["x_prompt"].reshape(128, D)
    arrays["x_sample"] = x["x_sample"].reshape(256, D)
    arrays["cond"] = np.stack([x["c_ctx"].reshape(KC, P), x["c"].reshape(KC, P)]).transpose(2, 0, 1)
    arrays["gcol"] = np.stack([x["g_attn"].reshape(DEPTH, KC, P), x["g_ffn"].reshape(DEPTH, KC, P)], axis=1).transpose(0, 3, 1, 2)
    arrays["pool_scale"] = x["pool_scale"].reshape(DEPTH, 2, P).transpose(0, 2, 1)
    arrays["b_gate"] = x["b_gate"].reshape(DEPTH, 3, D)
    for name in ("b_ada", "w_ada", "w_in", "w_fourier", "w_pool_grp", "w_pool", "w_attn", "w_gate", "w_out", "peer_wq", "rel_bias"):
        arrays[name] = x[name]
    arrays["cache_k"] = x["cache_k"][0].reshape(DEPTH, 4, 2, 128, DH).transpose(0, 2, 4, 1, 3).reshape(DEPTH, P, 4, 128)
    arrays["cache_v"] = x["cache_v"][0]
    arrays["keys"] = x["peer_keys"].transpose(0, 4, 1, 2, 3).reshape(DEPTH, P, 16, KEYS)
    arrays["ut"] = x["peer_u"].reshape(DEPTH, KEYS, KEYS, KC, P).transpose(0, 2, 4, 3, 1).reshape(DEPTH * KEYS, P, KC * KEYS)
    arrays["peer_v"] = x["peer_v"].reshape(DEPTH * KEYS, KEYS, D)
    arrays["g_final"] = x["g_final"].reshape(1, D)
    arrays = {k: np.ascontiguousarray(v) for k, v in arrays.items()}

    nc = bacc.Bacc("TRN2", target_bir_lowering=False, num_devices=1)
    a = {k: nc.dram_tensor("in_" + k, v.shape, F32, kind="ExternalInput").ap() for k, v in arrays.items()}
    o = {k: nc.dram_tensor("out_" + k, shape, F32, kind="ExternalOutput").ap() for k, shape in _OUTS.items()}
    build(nc, a, o)
    r = run(nc, [{"in_" + k: v for k, v in arrays.items()}], core_ids=[0]).results[0]
    return (r["out_y_prompt"].reshape(1, 128, D), r["out_y_sample"].reshape(1, 256, D),
            r["out_new_k"].reshape(1, DEPTH, HEADS, 128, DH), r["out_new_v"].reshape(1, DEPTH, HEADS, 128, DH))
```

```python
from contextlib import ExitStack

import concourse.bass as bass
from concourse import mybir
from concourse.alu_op_type import AluOpType as ALU

F32 = mybir.dt.float32
F32R = mybir.dt.float32r
U32 = mybir.dt.uint32
ACT = mybir.ActivationFunctionType
AX = mybir.AxisListType.X

P = 128
D = 1024
DEPTH = 2
TB = 3
T = TB * P
KC = D // P
HEADS = 8
DH = 64
GRID = 64
RB = 15 * 31
KEYS = 128
TOPK = 16
ROW_SPLIT = 4
CANDS = ROW_SPLIT * TOPK + (TOPK - ROW_SPLIT) * ROW_SPLIT
assert (ROW_SPLIT + 1) * (ROW_SPLIT + 1) > TOPK == ROW_SPLIT * ROW_SPLIT
EPS = 1e-6
UW = 1024
HB = 512
SLOTS = 4

U_IN = 0
U_GF = U_IN + 2 * KC
U_WF = U_GF + KC
U_GP = U_WF + 2
U_WP = U_GP + KC
U_GA = U_WP + 2
U_WA = U_GA + KC
U_OUT = U_WA + 4
U_Q = U_OUT + KC
U_PEER = U_Q + 2 * KC
UNITS = U_PEER + 2 * KEYS
PAIRS = UNITS // 2
USED = U_PEER + KEYS
assert UNITS % SLOTS == 0

C_ADA = 0
C_IN = C_ADA + 12
C_GF = C_IN + 12
C_WF = C_GF + 6
C_GP = C_WF + 6
C_WP = C_GP + 6
C_GA = C_WP + 6
C_WA = C_GA + 6
C_OUT = C_WA + 6
C_Q = C_OUT + 6
C_NEXT = C_Q + 12
C_V = C_NEXT + 12
ACCS = C_V + 6 - C_IN
FREES = ACCS - 12
assert ACCS % 6 == 0

STEPS = HEADS * TB
BESIDE = [[("z", 2), ("z", 3)], [], [("z", 4), ("z", 5), ("z", 0)], [], [("z", 1), ("z", 6), ("z", 7)], [],
          [("f", 0), ("f", 1), ("f", 2)], [], [("z", 8), ("p", 0), ("p", 1)], [], [("z", 9), ("d", 0), ("d", 1)], [],
          [("y", 0), ("y", 1)], []]
_step = 0
for _i in range(len(BESIDE), 2 * (U_WA - U_GF)):
    BESIDE.append([])
    if (_i % 2 == 0 and _i // 2 not in (8, 18)) or (_i % 2 and _i // 2 in (10, 12, 14, 16, 20, 22, 24)):
        BESIDE[-1] += [(_k, _j) for _k, _j in (("s", _step), ("t", _step - 1), ("v", _step - 2)) if 0 <= _j < STEPS]
        _step += 1
BESIDE += [[]] * (2 * (U_OUT - U_WA))
assert _step == STEPS + 2
X_MOD = 0
X_HT = X_MOD + 2
X_GATE = X_HT + KC
X_BES = X_GATE + 2
USE = {}
for _i in BESIDE:
    for _u in _i:
        USE[_u] = X_BES + len(USE)
X_MT = X_BES + len(USE)
X_H2 = X_MT + KC
X_QA = X_H2 + KC
X_SA = X_QA + 8
X_QB = X_SA + 6
X_SB = X_QB + 8
X_NEXT = X_SB + 6
X_IT = X_NEXT + 2
X_G = X_IT + TB
X_U = X_G + T // 4
AUXS = X_U + KEYS - X_HT
FREED = X_U - X_HT
assert X_U % 2 == AUXS % 2 == 0

GT = 16
BY_POOL = (0, 3, 4, 7)
BY_ACT = (2, 6)
GN = 8
GGROUPS = KEYS // GN
BODY = 2 * GN


def build(nc, a, o):
    with ExitStack() as ctx:
        def sb(name, shape, dt=F32):
            return ctx.enter_context(nc.sbuf_tensor(name, shape, dt))

        def sem(name):
            return ctx.enter_context(nc.semaphore(name))

        X = sb("x", [P, TB, D])
        Z = sb("z", [P, TB, 2 * D])
        Zf = Z[:].rearrange("p t n -> p (t n)")
        XN = Zf[:, 0:TB * D].rearrange("p (t n) -> p t n", t=TB)
        HRAW = Zf[:, TB * D:2 * TB * D].rearrange("p (k t) -> p k t", k=KC)
        M = Z[:, :, 0:D]
        GCH = Zf.rearrange("p (s t n) -> p s t n", s=2, n=GN)
        LTh = sb("lt_hi", [P, KC, T], F32R)
        LTl = sb("lt_lo", [P, KC, T], F32R)
        BTh = sb("bt_hi", [P, 8, T], F32R)
        BTl = sb("bt_lo", [P, 8, T], F32R)
        raw = sb("raw", [P, SLOTS, UW])
        whi = sb("whi", [P, SLOTS, UW], F32R)
        wlo = sb("wlo", [P, SLOTS, UW], F32R)
        U = sb("u", [P, 13568])

        def part(at, n, **k):
            v = U[:, at:at + n]
            return v.rearrange(*k["r"][:1], **k["r"][1]) if "r" in k else v

        MODR = part(0, 2 * D, r=("p (s n) -> p s n", dict(s=2)))
        GTB = part(0, TB * D, r=("p (t n) -> p t n", dict(t=TB)))
        ZFT = Z[:, 0:2, 256:256 + T]
        ZCS = part(10240, TB * 512, r=("p (t c n) -> p t c n", dict(t=TB, c=2)))
        DT = part(11776, 2 * T, r=("p (c t) -> p c t", dict(c=2)))
        XTMP = part(0, 1024, r=("p (s n) -> p s n", dict(s=2)))
        QT = part(3072, 4 * T, r=("p (c t) -> p c t", dict(c=4)))
        KT = part(4608, 4 * T, r=("p (c t) -> p c t", dict(c=4)))
        BIAS = part(6144, 4096, r=("p (b h n) -> p b h n", dict(b=2, h=HEADS)))
        MRAW = part(6144, KC * T, r=("p (k t) -> p k t", dict(k=KC)))
        S = part(10240, 768, r=("p (s n) -> p s n", dict(s=2)))
        PR = part(11008, 768, r=("p (s n) -> p s n", dict(s=2)))
        PT = part(11776, 768, r=("p (s k q) -> p s k q", dict(s=2, k=3)))
        KCT = part(12544, 512, r=("p (c n) -> p c n", dict(c=4)))
        VC = part(13056, 512)
        KEYT = part(0, 16 * KEYS, r=("p (h n) -> p h n", dict(h=16)))
        PQT = part(2048, 16 * T, r=("p (h t) -> p h t", dict(h=16)))
        CAND = part(2048, HEADS * CANDS, r=("p (h c) -> p h c", dict(h=HEADS)))
        FAR_ROW = part(3072, 128)
        OH = [part(at, 2048, r=("p (h k a) -> p h k a", dict(h=HEADS, k=TOPK))) for at in (4096, 11488)]
        STG = part(4096, 4096, r=("p (s g t n) -> p s g t n", dict(s=2, g=GGROUPS, t=GT)))
        GATE2 = part(2048, 2048, r=("p (c n) -> p c n", dict(c=2)))
        SV = part(8192, 768, r=("p (t h k) -> p t h k", dict(t=TB, h=16)))
        SI = part(8960, 768, r=("p (t h k) -> p t h k", dict(t=TB, h=16))).bitcast(U32)
        SIF = part(6144, 512, r=("p (s h q k) -> p s h q k", dict(s=2, h=HEADS, q=2)))
        TOP = part(9728, 128, r=("p (h k) -> p h k", dict(h=HEADS)))
        POS = part(9856, 128, r=("p (h k) -> p h k", dict(h=HEADS))).bitcast(U32)
        PLACE1 = part(9984, 256, r=("p (q m) -> p q m", dict(q=2))).bitcast(U32)
        PLACE2 = part(3328, 256, r=("p (q m) -> p q m", dict(q=2))).bitcast(U32)
        PAB = part(3584, 512, r=("p (s q h k) -> p s q h k", dict(s=2, q=2, h=HEADS)))
        PABf = part(3584, 512, r=("p (s q m) -> p s q m", dict(s=2, q=2)))
        SEL = part(6656, 3 * TB * P, r=("p (s q h k) -> p s q h k", dict(s=TB, q=3, h=HEADS)))
        SELf = part(6656, 3 * TB * P, r=("p (s q m) -> p s q m", dict(s=TB, q=3)))
        SELT = part(10336, 3 * T, r=("p (q t) -> p q t", dict(q=3)))
        SELC = part(10240, 96, r=("p (s q t) -> p s q t", dict(s=2, q=3)))
        HOT1 = part(0, 4096, r=("p (s n) -> p s n", dict(s=32)))
        HOT2 = part(11488, 2048, r=("p (s n) -> p s n", dict(s=16)))
        SQUARES = part(6144, D)
        FAR = part(8192, 512, r=("p (t n) -> p t n", dict(t=4)))
        ACTB = part(0, 768, r=("p (s t) -> p s t", dict(s=2)))
        GFIN = part(0, D)

        ident = sb("ident", [P, P])
        iota = sb("iota", [P, P])
        mask = sb("mask", [P, GRID])
        dft_c = sb("dft_c", [P, 256])
        dft_p = sb("dft_p", [P, 2, P])
        dft_s = sb("dft_s", [P, 2, 2, 256])
        pool_p = sb("pool_p", [P, 4, P])
        pool_s = sb("pool_s", [P, 2, 4, 256])
        wpg = sb("wpg", [P, 2, P])
        cond = sb("cond", [P, 2, KC])
        gcol = sb("gcol", [P, 2, KC])
        pscale = sb("pscale", [P, 2])
        bada = sb("bada", [P, 6, KC])
        modc = sb("modc", [P, 6, 2, KC])
        gate_r = sb("gate_r", [2 * KC, 2, P])
        one = sb("one", [P, 1])
        ms = sb("ms", [P, TB])
        rstd = sb("rstd", [P, TB])
        nhalf = sb("nhalf", [P, 1])
        eps = sb("eps", [P, 1])
        nmax = sb("nmax", [P, 2])
        rsum = sb("rsum", [P, 2])
        hsum = sb("hsum", [P, HEADS])
        acc = [ctx.enter_context(nc.psum_tensor(f"acc{i}", [P, HB], F32)) for i in range(6)]
        aux = [ctx.enter_context(nc.psum_tensor(f"aux{i}", [P, HB], F32)) for i in range(2)]

        gate_rows = nc.dram_tensor("gate_rows", (DEPTH, 2, 2, D), F32, kind="Internal").ap()
        gmat = nc.dram_tensor("gmat", (GGROUPS, P, T * GN), F32, kind="Internal").ap()

        bias_rows = nc.dram_tensor("bias_rows", (DEPTH * HEADS, GRID, RB), F32, kind="Internal").ap()
        toeplitz = nc.dram_tensor("toeplitz", (DEPTH, GRID, HEADS, 7 * GRID), F32, kind="Internal").ap()

        pair_landed = [sem("pair_landed0"), sem("pair_landed1")]
        hi_ready = sem("hi_ready")
        lo_ready = sem("lo_ready")
        unit_used = sem("unit_used")
        acc_done = sem("acc_done")
        acc_free = sem("acc_free")
        aux_done = sem("aux_done")
        aux_free = sem("aux_free")
        first_landed = sem("first_landed")
        const_landed = sem("const_landed")
        x_landed = sem("x_landed")
        start_ready = sem("start_ready")
        bias_rows_stored = sem("bias_rows_stored")
        toeplitz_stored = sem("toeplitz_stored")
        silu_ready = sem("silu_ready")
        layer_free = sem("layer_free")
        ada_landed = [sem(f"ada_landed{i}") for i in range(SLOTS)]
        ada_used = sem("ada_used")
        cols_landed = sem("cols_landed")
        modr_ready = sem("modr_ready")
        modr_used = sem("modr_used")
        mods_ready = sem("mods_ready")
        rows_ready = sem("rows_ready")
        rows_stored = sem("rows_stored")
        x_ready = sem("x_ready")
        ms_ready = sem("ms_ready")
        rstd_ready = sem("rstd_ready")
        xn_ready = sem("xn_ready")
        ht_ready = sem("ht_ready")
        z_ready = sem("z_ready")
        kv_stored = sem("kv_stored")
        att_landed = sem("att_landed")
        zf_ready = sem("zf_ready")
        qk_ready = sem("qk_ready")
        zcs_ready = sem("zcs_ready")
        dt_ready = sem("dt_ready")
        four_done = sem("four_done")
        bgate_landed = sem("bgate_landed")
        gate_sum = sem("gate_sum")
        gate_ready = sem("gate_ready")
        gtb_free = sem("gtb_free")
        s_ready = sem("s_ready")
        p_ready = sem("p_ready")
        pn_ready = sem("pn_ready")
        pt_ready = sem("pt_ready")
        att_done = sem("att_done")
        m_ready = sem("m_ready")
        gate1_landed = sem("gate1_landed")
        out_done = sem("out_done")
        keys_landed = sem("keys_landed")
        pq_ready = sem("pq_ready")
        pqt_ready = sem("pqt_ready")
        scores_ready = sem("scores_ready")
        top_ready = sem("top_ready")
        exp_ready = sem("exp_ready")
        place_ready = sem("place_ready")
        index_ready = sem("index_ready")
        sel_ready = sem("sel_ready")
        selc_ready = sem("selc_ready")
        hot1_ready = sem("hot1_ready")
        hot2_ready = sem("hot2_ready")
        hot2_open = sem("hot2_open")
        hot3_ready = sem("hot3_ready")
        stage_ready = sem("stage_ready")
        stage_stored = [sem("stage_stored0"), sem("stage_stored1")]
        gate2_landed = sem("gate2_landed")
        group_landed = [sem("group_landed0"), sem("group_landed1")]
        act_ready = sem("act_ready")
        w_ready = sem("w_ready")
        gfin_landed = sem("gfin_landed")
        y_ready = sem("y_ready")
        y_stored = sem("y_stored")

        NSTG = T // GT
        block = ctx.enter_context(nc.Block())

        def accum(use):
            return acc[use % 6]

        @block.sync
        def _(sp):
            def modulation(n, l):
                v = a["w_ada"][bass.ds(n, 1)].rearrange("o (k p) n -> p (o k) n", p=P)
                for i in range(6 * KC):
                    p, k = i // KC, i % KC
                    if i >= SLOTS:
                        sp.wait_ge(ada_used, n * (6 * KC) + i + 1 - SLOTS)
                    elif l is not None:
                        sp.wait_ge(lo_ready, l * UNITS + U_PEER + i + 1)
                    sp.dma_start(raw[:, i % SLOTS, :], v[:, k, p * D:(p + 1) * D]).then_inc(ada_landed[i % SLOTS], 16)

            def layer(l, last):
                def pairs(u0, u1, source):
                    for i, u in enumerate(range(u0, u1, 2)):
                        q = u // 2
                        sp.wait_ge(lo_ready, l * UNITS + u + 2)
                        sp.dma_start(raw[:, u % SLOTS:u % SLOTS + 2, :], source(i)).then_inc(pair_landed[q % 2], 16)

                def rows(w, n0):
                    v = w[bass.ds(l, 1)].rearrange("o (k s p) n -> p (o k) s n", p=P, s=2)
                    return lambda i: v[:, i, :, n0:n0 + UW]

                pairs(U_IN, U_IN + 4, rows(a["w_in"], 0))
                sp.wait_ge(mods_ready, l + 1)
                sp.dma_start(KCT, a["cache_k"][bass.ds(l, 1)].rearrange("o p c n -> (o p) c n")).then_inc(att_landed, 16)
                sp.wait_ge(layer_free, l + 1)
                sp.wait_ge(toeplitz_stored, 16 * DEPTH * HEADS)
                for b in range(2):
                    for r2 in range(2):
                        r = 2 * b + r2
                        sp.dma_start(BIAS[64 * r2:64 * r2 + 64, b],
                                     toeplitz[bass.ds(l, 1), :, :, (3 - r) * GRID:(7 - r) * GRID]
                                     .rearrange("o q h n -> (o q) h n")).then_inc(att_landed, 16)
                sp.dma_start(GTB, a["b_gate"][bass.ds(l, 1), 0:1, :].to_broadcast([P, TB, D])).then_inc(bgate_landed, 16)
                sp.dma_start(VC.rearrange("p (h d) -> p h d", h=HEADS),
                             a["cache_v"][bass.ds(l, 1)].rearrange("o h k d -> (o k) h d")).then_inc(att_landed, 16)
                v = a["w_in"][bass.ds(l, 1)].rearrange("o (k s p) n -> p (o k) s n", p=P, s=2)
                pairs(U_IN + 4, U_IN + 8, lambda i: v[:, i + 2, :, 0:UW])
                pairs(U_IN + 8, U_IN + 16, rows(a["w_in"], UW))
                pairs(U_GF, U_GF + 4, rows(a["w_gate"], 0))
                sp.wait_ge(rows_ready, l + 1)
                for g in range(2):
                    sp.dma_start(gate_rows[bass.ds(l, 1), g].rearrange("o s (k p) -> (o s k) p", p=P), gate_r[:, g, :]).then_inc(rows_stored, 16)
                sp.wait_ge(z_ready, l + 1)
                for n0, out in ((768, o["new_k"]), (1280, o["new_v"])):
                    sp.dma_start(out[bass.ds(l, 1)].rearrange("o h t d -> (o t) h d"),
                                 Z[:, 0, n0:n0 + 512].rearrange("p (h d) -> p h d", h=HEADS)).then_inc(kv_stored, 16)
                wg = a["w_gate"][bass.ds(l, 1)].rearrange("o (k s p) n -> p (o k) s n", p=P, s=2)
                pairs(U_GF + 4, U_WF, lambda i: wg[:, i + 2, :, 0:UW])
                pairs(U_WF, U_GP, rows(a["w_fourier"], 0))
                pairs(U_GP, U_GP + 4, rows(a["w_gate"], 2 * UW))
                sp.wait_ge(gtb_free, l * 2 + 1)
                sp.dma_start(GTB, a["b_gate"][bass.ds(l, 1), 2:3, :].to_broadcast([P, TB, D])).then_inc(bgate_landed, 16)
                pairs(U_GP + 4, U_WP, lambda i: wg[:, i + 2, :, 2 * UW:3 * UW])
                pairs(U_WP, U_GA, rows(a["w_pool"], 0))
                pairs(U_GA, U_GA + 4, rows(a["w_gate"], UW))
                sp.wait_ge(gtb_free, l * 2 + 2)
                sp.dma_start(GTB, a["b_gate"][bass.ds(l, 1), 1:2, :].to_broadcast([P, TB, D])).then_inc(bgate_landed, 16)
                pairs(U_GA + 4, U_WA, lambda i: wg[:, i + 2, :, UW:2 * UW])
                pairs(U_WA, U_OUT, rows(a["w_attn"], 0))
                sp.wait_ge(rows_stored, l * 32 + 32)
                sp.wait_ge(att_done, l + 1)
                for s in range(2):
                    sp.dma_start(Z[:, s, D:2 * D], gate_rows[bass.ds(l, 1), 0, s, :].to_broadcast([P, D])).then_inc(gate1_landed, 16)
                pairs(U_OUT, U_Q, rows(a["w_out"], 0))
                pairs(U_Q, U_Q + 4, rows(a["peer_wq"], 0))
                sp.wait_ge(out_done, l + 1)
                sp.dma_start(KEYT, a["keys"][bass.ds(l, 1)].rearrange("o p h n -> (o p) h n")).then_inc(keys_landed, 16)
                wq = a["peer_wq"][bass.ds(l, 1)].rearrange("o (k s p) n -> p (o k) s n", p=P, s=2)
                pairs(U_Q + 4, U_Q + 8, lambda i: wq[:, i + 2, :, 0:UW])
                pairs(U_Q + 8, U_PEER, rows(a["peer_wq"], UW))
                def group(g, s, used):
                    if used is not None:
                        sp.wait_ge(w_ready, l * KEYS + used + GN + 1)
                    sp.dma_start(GCH[:, s].rearrange("p t n -> p (t n)"),
                                 gmat[bass.ds(g, 1)].rearrange("o p n -> (o p) n")).then_inc(group_landed[s], 16)

                def expert_pair(i, n, after_ada=False):
                    def slots(m):
                        if after_ada:
                            sp.wait_ge(ada_used, l * (6 * KC) + 12 * KC - 4 + m)
                        else:
                            sp.wait_ge(lo_ready, l * UNITS + i * (2 * BODY) + 2 * n + (U_PEER + m))

                    slots(2)
                    sp.dma_start(raw[:, 0:2, :], a["ut"][bass.ds(l * KEYS + i * BODY + n, 2)].rearrange("s p n -> p s n")).then_inc(pair_landed[0], 16)
                    slots(4)
                    sp.dma_start(raw[:, 2:4, :], a["peer_v"][bass.ds(l * P, P), bass.ds(i * BODY + n, 2), :]).then_inc(pair_landed[1], 16)

                if not last:
                    modulation(l + 1, l)
                expert_pair(0, 0, not last)
                with sp.Fori(0, NSTG // 2) as g:
                    for s in range(2):
                        sp.wait_ge(stage_ready, l * NSTG + g * 2 + s + 1)
                        sp.dma_start(gmat.rearrange("g p (t n) -> p g t n", n=GN)[:, :, bass.ds(g * (2 * GT) + s * GT, GT), :]
                                     .rearrange("p g t n -> p g (t n)"),
                                     STG[:, s].rearrange("p g t n -> p g (t n)")).then_inc(stage_stored[s], 16)
                for s in range(2):
                    sp.wait_ge(stage_stored[s], l * (8 * NSTG) + 8 * NSTG)
                group(0, 0, None)
                for s in range(2):
                    sp.dma_start(GATE2[:, s, :], gate_rows[bass.ds(l, 1), 1, s, :].to_broadcast([P, D])).then_inc(gate2_landed, 16)
                def experts(i, last):
                    for k in range(BODY // 2):
                        n = 2 * k
                        if not (last and n == BODY - 2):
                            expert_pair(i, n + 2)
                        if n == GN // 2:
                            group(i * 2 + 1, 1, i * BODY)
                        if n == BODY - GN // 2 and not last:
                            group(i * 2 + 2, 0, i * BODY + GN)

                with sp.Fori(0, KEYS // BODY - 1) as i:
                    experts(i, False)
                experts(KEYS // BODY - 1, True)

            modulation(0, None)
            sp.wait_ge(ada_used, 6 * KC)
            with sp.Fori(0, DEPTH - 1) as l:
                layer(l, False)
            layer(DEPTH - 1, True)
            sp.wait_ge(layer_free, DEPTH + 1)
            sp.dma_start(GFIN, a["g_final"].to_broadcast([P, D])).then_inc(gfin_landed, 16)
            sp.wait_ge(y_ready, 1)
            sp.dma_start(o["y_prompt"], X[:, 0, :]).then_inc(y_stored, 16)
            sp.dma_start(o["y_sample"].rearrange("(b p) n -> p b n", p=P), X[:, 1:3, :]).then_inc(y_stored, 16)
            sp.wait_ge(kv_stored, 32 * DEPTH)
            sp.wait_ge(y_stored, 32)

        @block.gpsimd
        def _(pool):
            pool.sem_inc(lo_ready, SLOTS)
            pool.wait_ge(start_ready, 1)

            def root(n):
                for t in range(TB):
                    pool.wait_ge(ms_ready, n * TB - TB + t + 1)
                    pool.tensor_tensor(rstd[:, t:t + 1], ms[:, t:t + 1], eps[:], ALU.add)
                    pool.drain()
                    pool.tensor_tensor(rstd[:, t:t + 1], rstd[:, t:t + 1], nhalf[:], ALU.pow).then_inc(rstd_ready, 1)

            def lo(value, slot):
                pool.wait_ge(hi_ready, value)
                pool.tensor_tensor(wlo[:, slot], raw[:, slot], whi[:, slot].bitcast(F32), ALU.subtract).then_inc(lo_ready, 1)

            def layer(l):
                root(l * 2 + 1)
                with pool.Fori(0, (U_Q + 4) // 4) as i:
                    for s in range(SLOTS):
                        lo(l * UNITS + i * 4 + s + 1, s)
                root(l * 2 + 2)
                with pool.Fori(0, (U_PEER - U_Q - 4) // 4) as i:
                    for s in range(SLOTS):
                        lo(l * UNITS + i * 4 + U_Q + 4 + s + 1, s)
                for t in range(TB - 1):
                    s = t % 2
                    pool.wait_ge(place_ready, l * (TB - 1) + t + 1)
                    for q in range(2):
                        index = SIF[:, s, :, q, :].rearrange("p h (o a) -> p h o a", o=1).to_broadcast([P, HEADS, TOPK, TOPK])
                        pool.tensor_tensor(OH[q], OH[q], index, ALU.mult)
                    pool.drain()
                    for w in (8, 4, 2, 1):
                        for q in range(2):
                            out = OH[q][:, :, :, 0:w] if w > 1 else SEL[:, t, q].rearrange("p h (k o) -> p h k o", o=1)
                            pool.tensor_tensor(out, OH[q][:, :, :, 0:w], OH[q][:, :, :, w:2 * w], ALU.add)
                        x = pool.drain()
                    x.then_inc(index_ready, 1)
                with pool.Fori(0, T // (2 * GT)) as g:
                    for n in range(8):
                        if n not in BY_POOL:
                            continue
                        if n in (BY_POOL[0], min(x for x in BY_POOL if x > 3)):
                            pool.wait_ge(selc_ready, l * (T // GT) + g * 2 + n // 4 + 1)
                        pool.wait_ge(aux_done, l * AUXS + g * 8 + X_G + n - 3)
                        pool.sem_inc(hot2_open, 1)
                        for j in range(4 * n, 4 * n + 4):
                            i2 = SELC[:, n // 4, 1, j % GT:j % GT + 1]
                            x = pool.tensor_scalar(HOT2[:, j % 16, :], iota[:], i2, None, ALU.is_equal)
                        x.then_inc(hot2_ready, 1)
                with pool.Fori(0, 2 * KEYS // 4) as i:
                    for s in range(SLOTS):
                        lo(l * UNITS + i * 4 + U_PEER + s + 1, s)

            with pool.Fori(0, DEPTH - 1) as l:
                layer(l)
            layer(DEPTH - 1)
            root(2 * DEPTH + 1)

        @block.scalar
        def _(act):
            def columns(n):
                for t, src in ((bada, "bada"), (gcol, "gcol")):
                    act.dma_start(t[:], a[src][bass.ds(n, 1)].rearrange("o p s k -> (o p) s k")).then_inc(cols_landed, 16)
                act.dma_start(pscale[:], a["pool_scale"][bass.ds(n, 1)].rearrange("o p s -> (o p) s")).then_inc(cols_landed, 16)
                for g in range(4):
                    act.dma_start(wpg[64 * (g % 2):64 * (g % 2) + 64, g // 2, 64 * (g % 2):64 * (g % 2) + 64],
                                  a["w_pool_grp"][bass.ds(n, 1), g].rearrange("o c e -> (o c) e")).then_inc(cols_landed, 16)

            for t, src in ((cond, "cond"), (ident, "ident")):
                act.dma_start(t[:], a[src]).then_inc(first_landed, 16)
            act.wait_ge(first_landed, 32)
            act.activation(cond[:], cond[:], ACT.Silu).then_inc(silu_ready, 1)
            def squares(n):
                for t in range(TB):
                    if isinstance(n, int) and n == 1:
                        act.wait_ge(x_landed, 32)
                    else:
                        act.wait_ge(x_ready, n * TB - 2 * TB + t + 1)
                    act.activation(SQUARES, X[:, t], ACT.Square, scale=D ** -0.5, accum_out=ms[:, t:t + 1])
                    act.drain().then_inc(ms_ready, 1)

            def modulation(n, use, p):
                if not (isinstance(n, int) and p < 2):
                    act.wait_ge(modr_used, n * 6 + p - 1)
                for h in range(2):
                    act.wait_ge(acc_done, use + 2 * p + h + 1)
                    act.activation(MODR[0:2, p % 2, h * HB:(h + 1) * HB], acc[(2 * p + h) % 6][0:2, :], ACT.Copy).then_inc(modr_ready, 1)

            def layer(l, last):
                def hi(u):
                    q = u // 2
                    act.wait_ge(pair_landed[q % 2], l * (8 * PAIRS) + 16 * (q // 2 + 1))
                    act.wait_ge(unit_used, l * USED + max(u + 1, 3))
                    act.activation(whi[:, u % SLOTS], raw[:, u % SLOTS], ACT.Copy).then_inc(hi_ready, 1)

                for u in range(U_IN, U_GF + 2):
                    hi(u)

                def exps(i):
                    n = P if i % TB == 0 else T
                    act.wait_ge(s_ready, l * STEPS + i + 1)
                    if i >= 2:
                        act.wait_ge(pt_ready, l * STEPS + i - 1)
                    act.activation(PR[:, i % 2, 0:n], S[:, i % 2, 0:n], ACT.Exp, bias=nmax[:, i % 2:i % 2 + 1],
                                   accum_out=rsum[:, i % 2:i % 2 + 1]).then_inc(p_ready, 1)

                def sigmoid(g):
                    for h in range(2):
                        act.wait_ge(gate_sum, l * 6 + 2 * g + h + 1)
                        v = GTB[:, :, h * HB:(h + 1) * HB]
                        act.activation(v, v, ACT.Sigmoid).then_inc(gate_ready, 1)

                for u in range(U_GF, U_OUT):
                    i = 2 * (u - U_GF)
                    hi(u + 2)
                    for kind, j in BESIDE[i] + BESIDE[i + 1]:
                        if kind == "s":
                            exps(j)
                    if u in (U_WF, U_WP, U_WA):
                        sigmoid((U_WF, U_WP, U_WA).index(u))
                for u in range(U_OUT + 2, U_Q + KC + 2):
                    if u == U_Q + 4:
                        squares(l * 2 + 2)
                    hi(u)

                def evacuated(out, use, width):
                    act.wait_ge(aux_done, l * AUXS + use + 1)
                    return act.activation(out, aux[use % 2][:, 0:width], ACT.Copy).then_inc(aux_free, 1)

                def queries(m, x, k0, k1):
                    for k in range(k0, k1):
                        evacuated(PQT[:, 8 * m + k], x + k, T)
                    if k1 == 8:
                        act.drain().then_inc(pqt_ready, 1)

                def scores(m, x, t):
                    for n in range(2):
                        q = 2 * m + n
                        evacuated(Z[:, t, q * HB:(q + 1) * HB], x + 2 * t + n, HB)
                    act.drain().then_inc(scores_ready, 1)

                for k in range(KC):
                    if k + 2 < KC:
                        hi(U_Q + KC + k + 2)
                    if k in (1, 2):
                        queries(0, X_QA, 4 * k - 4, 4 * k)
                    elif 3 <= k < 6:
                        scores(0, X_SA, k - 3)
                queries(1, X_QB, 0, 8)
                for t in range(TB):
                    scores(1, X_SB, t)
                if not last:
                    act.wait_ge(pq_ready, l * 2 + 1)
                    columns(l + 1)
                for t in range(TB):
                    if not last:
                        for p in ((0, 1), (2, 3), (4, 5))[t]:
                            modulation(l + 1, l * ACCS + C_NEXT, p)
                    act.wait_ge(top_ready, l * TB + t + 1)
                    act.activation(SEL[:, t, 2], SEL[:, t, 2], ACT.Exp).then_inc(exp_ready, 1)
                for u in range(U_PEER, U_PEER + SLOTS):
                    hi(u)

                def stages(g, first):
                    for s in range(2):
                        if not first:
                            act.wait_ge(stage_stored[s], l * (8 * NSTG) + g * 16)
                        act.wait_ge(selc_ready, l * (T // GT) + g * 2 + s + 1)

                        def far(j):
                            act.activation(FAR[:, j], iota[:], ACT.Abs, bias=SELC[:, s, 1, 8 + j:9 + j], scale=-1.0)

                        far(0)
                        far(1)
                        for j in range(4):
                            if j == 1:
                                far(2)
                                far(3)
                                act.drain()
                                act.activation(HOT2[:, 8:12, :], FAR, ACT.Relu, bias=one[:], scale=-1.0).then_inc(hot3_ready, 1)
                            use = X_G + 4 * s + j
                            act.wait_ge(aux_done, l * AUXS + g * 8 + use + 1)
                            act.activation(STG[:, s, :, 4 * j:4 * j + 4, :].rearrange("p g t n -> p t g n"),
                                           aux[use % 2][:].rearrange("p (t g n) -> p t g n", t=4, n=GN), ACT.Copy)\
                               .then_inc(aux_free, 1)
                        act.drain().then_inc(stage_ready, 1)

                stages(0, True)
                with act.Fori(1, NSTG // 2) as g:
                    stages(g, False)

                def gelus(k):
                    for j in range(2):
                        use = X_U + j
                        act.wait_ge(aux_done, l * AUXS + k * 2 + use + 1)
                        act.wait_ge(w_ready, l * KEYS + k * 2 + j - 1 + GN + 1)
                        act.activation(ACTB[:, j], aux[use % 2][:, 0:T], ACT.Gelu_apprx_tanh).then_inc(act_ready, 1)

                with act.Fori(1, KEYS // 2) as k:
                    gelus(k - 1)
                    for j in range(4):
                        act.wait_ge(pair_landed[j // 2], l * (8 * PAIRS) + k * 16 + (4 * U_PEER + 16))
                        if j < 2:
                            act.wait_ge(aux_done, l * AUXS + k * 2 + X_U + j - 1)
                        else:
                            act.wait_ge(unit_used, l * USED + k * 2 + U_PEER + j - 3 + SLOTS)
                        act.activation(whi[:, j], raw[:, j], ACT.Copy).then_inc(hi_ready, 1)
                gelus(KEYS // 2 - 1)
                squares(l * 2 + 3)

            act.wait_ge(start_ready, 1)
            for p in range(6):
                modulation(0, C_ADA, p)
                if p == 0:
                    act.dma_start(X[:, 0, :], a["x_prompt"]).then_inc(x_landed, 16)
                    act.dma_start(X[:, 1:3, :], a["x_sample"].rearrange("(b p) n -> p b n", p=P)).then_inc(x_landed, 16)
                elif p == 1:
                    rb = a["rel_bias"].rearrange("l h r c -> (l h) (r c)")
                    act.dma_start(bias_rows, rb.rearrange("n (o c) -> n o c", o=1).to_broadcast([DEPTH * HEADS, GRID, RB]))\
                       .then_inc(bias_rows_stored, 16)
                elif p == 2:
                    columns(0)
                    act.wait_ge(bias_rows_stored, 16)
                    for n in range(DEPTH):
                        for h in range(HEADS):
                            src = bass.AP(tensor=bias_rows.tensor, offset=(n * HEADS + h) * GRID * RB + 4 * 31 + 15,
                                          ap=[[RB - 1, GRID], [31, 7], [1, GRID]])
                            act.dma_start(toeplitz[n, :, h, :].rearrange("q (r k) -> q r k", r=7), src).then_inc(toeplitz_stored, 16)
                elif p == 3:
                    squares(1)
                    for t, src in ((iota, "iota"), (mask, "mask"), (dft_c, "dft_c"), (dft_p, "dft_p"),
                                   (dft_s, "dft_s"), (pool_p, "pool_p"), (pool_s, "pool_s")):
                        act.dma_start(t[:], a[src]).then_inc(const_landed, 16)
            with act.Fori(0, DEPTH - 1) as l:
                layer(l, False)
            layer(DEPTH - 1, True)

        @block.tensor
        def _(pe):
            pe.sem_inc(unit_used, SLOTS)
            pe.wait_ge(first_landed, 32)
            def modulation(n, free, aux0, x):
                def turned(p):
                    pe.wait_ge(modr_ready, n * 12 + 2 * p + 2)
                    b = aux[(x + p // 3) % 2]
                    if p % 3 == 0:
                        pe.wait_ge(aux_free, aux0 + x + p // 3 + 1)
                    for j in range(KC):
                        at = (p % 3) * 2 * KC + 2 * j
                        mm = pe.transpose(b[:, at:at + 2], MODR[0:2, p % 2, j * P:(j + 1) * P], ident[0:2, 0:2])
                    mm.then_inc(modr_used, 1)
                    if p % 3 == 2:
                        pe.drain().then_inc(aux_done, 1)

                for p in range(6):
                    for k in range(KC):
                        i = p * KC + k
                        pe.wait_ge(ada_landed[i % SLOTS], n * (16 * 6 * KC // SLOTS) + 16 * (i // SLOTS + 1))
                        for h in range(2):
                            m = 2 * p + h
                            if k == 0 and m < 6:
                                pe.wait_ge(acc_free, free + m + 1)
                            elif k == 0:
                                pe.wait_ge(modr_ready, n * 12 + m - 5)
                            mm = pe.matmul(acc[m % 6][0:2, :], cond[:, :, k], raw[:, i % SLOTS, h * HB:(h + 1) * HB],
                                           start=(k == 0), stop=(k == KC - 1))
                            if k == KC - 1:
                                mm.then_inc(acc_done, 1)
                        (mm if k < KC - 1 else pe.drain()).then_inc(ada_used, 1)
                    if p:
                        turned(p - 1)
                turned(5)

            def layer(l, last):
                def unit(u, lt, chunk, use, first, last, beside=None):
                    pe.wait_ge(lo_ready, l * UNITS + u + 1 + SLOTS)
                    s = u % SLOTS
                    for h in range(2):
                        if beside and h:
                            beside()
                        for t in range(TB):
                            if first:
                                pe.wait_ge(acc_free, l * FREES + use - C_IN + TB * h + t + 1)
                            lh, ll = (x[:, chunk, t * P:(t + 1) * P] for x in lt)
                            for n, (x, w) in enumerate(((lh, whi), (lh, wlo), (ll, whi))):
                                mm = pe.matmul(accum(use + TB * h + t)[:], x, w[:, s, h * HB:(h + 1) * HB],
                                               start=first and n == 0, stop=last and n == 2)
                            if last:
                                mm.then_inc(acc_done, 1)
                    (pe.drain() if last else mm).then_inc(unit_used, 1)

                def bank(use):
                    pe.wait_ge(aux_free, l * FREED + use + 1)
                    return aux[use % 2]

                def turn(src, base, k):
                    b = bank(base + k)
                    for t in range(TB):
                        mm = pe.transpose(b[:, t * P:(t + 1) * P], src[:, t, k * P:(k + 1) * P], ident[:])
                    mm.then_inc(aux_done, 1)

                def turned_pass(src, base, ready, u0, use, ht0):
                    for k in range(KC + 3):
                        if k < KC:
                            ready(k)
                            turn(src, base, k)
                        if k >= 3:
                            pe.wait_ge(ht_ready, l * (3 * KC) + ht0 + k - 2)
                            unit(u0 + k - 3, (LTh, LTl), k - 3, use, k == 3, k == KC + 2)

                def xn(n):
                    return lambda k: pe.wait_ge(xn_ready, l * 2 + n) if k == 0 else None

                turned_pass(XN, X_HT, xn(1), U_IN, C_IN, 0)
                pe.wait_ge(mods_ready, l + 1)
                for g in range(2):
                    pe.transpose(bank(X_GATE + g)[0:2 * KC, 0:P], modc[:, 3 * g + 2].rearrange("p s k -> p (s k)"), ident[:])\
                      .then_inc(aux_done, 1)
                for k in range(KC):
                    unit(U_IN + KC + k, (LTh, LTl), k, C_IN + 6, k == 0, k == KC - 1)

                def small(kind, i):
                    if (kind, i) == ("z", 2):
                        pe.wait_ge(z_ready, l + 1)
                    if (kind, i) == ("f", 0):
                        pe.wait_ge(zf_ready, l + 1)
                        pe.wait_ge(const_landed, 16 * 7)
                    if (kind, i) == ("p", 0):
                        pe.wait_ge(zcs_ready, l + 1)
                    if (kind, i) == ("y", 0):
                        pe.wait_ge(dt_ready, l + 1)
                        pe.wait_ge(cols_landed, l * 96 + 96)
                    if (kind, i) == ("s", 0):
                        pe.wait_ge(qk_ready, l + 1)
                        pe.wait_ge(att_landed, l * (16 * 6) + 16 * 6)
                    b = bank(USE[kind, i])
                    h, t = i // TB, i % TB
                    r = 64 * (h % 2)
                    if kind == "z":
                        for t in range(TB):
                            mm = pe.transpose(b[:, t * P:(t + 1) * P], Z[:, t, i * P:(i + 1) * P], ident[:])
                    elif kind == "f":
                        for c in range(2):
                            mm = pe.matmul(b[:, c * 256:(c + 1) * 256], ZFT[:, c, i * P:(i + 1) * P], dft_c[:], start=True, stop=True)
                    elif kind == "p":
                        for q in range(2):
                            pe.matmul(b[:, 0:P], ZCS[:, 0, i, q * P:(q + 1) * P], dft_p[:, q, :], start=(q == 0), stop=(q == 1))
                        for n in range(4):
                            t, q = n // 2, n % 2
                            mm = pe.matmul(b[:, P:T], ZCS[:, 1 + t, i, q * P:(q + 1) * P], dft_s[:, t, q, :], start=(n == 0), stop=(n == 3))
                    elif kind == "d":
                        for g2 in range(2):
                            g = 2 * i + g2
                            out = b[64 * g2:64 * g2 + 64, :]
                            pe.matmul(out[:, 0:P], Z[:, 0, 1792 + 64 * g:1856 + 64 * g], pool_p[:, g, :], start=True, stop=True)
                            for t in range(2):
                                mm = pe.matmul(out[:, P:T], Z[:, 1 + t, 1792 + 64 * g:1856 + 64 * g], pool_s[:, t, g, :],
                                               start=(t == 0), stop=(t == 1))
                    elif kind == "y":
                        mm = pe.matmul(b[:, 0:T], wpg[:, i, :], DT[:, i, :], start=True, stop=True)
                    elif kind == "s":
                        q = QT[r:r + 64, h // 2, t * P:(t + 1) * P]
                        if t == 0:
                            mm = pe.matmul(b[:, 0:P], q, KT[r:r + 64, h // 2, 0:P], start=True, stop=True)
                        else:
                            pe.matmul(b[:, 0:256], q, KT[r:r + 64, h // 2, P:T], start=True, stop=True)
                            mm = pe.matmul(b[:, 256:T], q, KCT[r:r + 64, h // 2, :], start=True, stop=True)
                    elif kind == "t":
                        pe.wait_ge(pn_ready, l * STEPS + i + 1)
                        for n in range(1 if t == 0 else 3):
                            mm = pe.transpose(b[:, n * P:(n + 1) * P], PR[:, i % 2, n * P:(n + 1) * P], ident[:])
                    else:
                        pe.wait_ge(pt_ready, l * STEPS + i + 1)
                        v = 1280 + DH * h
                        vs = [Z[:, 0, v:v + DH]] if t == 0 else [Z[:, 1, v:v + DH], Z[:, 2, v:v + DH], VC[:, DH * h:DH * h + DH]]
                        for n, x in enumerate(vs):
                            mm = pe.matmul(b[r:r + 64, 0:P], x, PT[:, i % 2, n, :], start=(n == 0), stop=(n == len(vs) - 1))
                    mm.then_inc(aux_done, 1)

                passes = [(U_GF, KC, (LTh, LTl), 0, C_GF), (U_WF, 2, (BTh, BTl), 0, C_WF),
                          (U_GP, KC, (LTh, LTl), 0, C_GP), (U_WP, 2, (BTh, BTl), 6, C_WP),
                          (U_GA, KC, (LTh, LTl), 0, C_GA), (U_WA, 4, (BTh, BTl), 2, C_WA)]
                for u0, n, lt, c0, use in passes:
                    if u0 == U_WF:
                        pe.wait_ge(four_done, l + 1)
                    if u0 == U_WA:
                        pe.wait_ge(att_done, l + 1)
                    for k in range(n):
                        i = 2 * (u0 + k - U_GF)

                        def beside(i=i):
                            for kind, j in BESIDE[i]:
                                small(kind, j)

                        beside()
                        unit(u0 + k, lt, c0 + k, use, k == 0, k == n - 1, lambda i=i: beside(i + 1))
                turned_pass(M, X_MT, lambda k: pe.wait_ge(m_ready, l * 2 + k // 4 + 1) if k % 4 == 0 else None,
                            U_OUT, C_OUT, KC)
                turned_pass(XN, X_H2, xn(2), U_Q, C_Q, 2 * KC)

                def query(base, k):
                    b = bank(base + k % 8)
                    for t in range(TB):
                        mm = pe.transpose(b[:, t * P:(t + 1) * P], Z[:, t, k * P:(k + 1) * P], ident[:])
                    mm.then_inc(aux_done, 1)

                def score(base, m, n):
                    t, q = n // 2, 2 * m + n % 2
                    b = bank(base + n)
                    for j in range(4):
                        mm = pe.matmul(b[:, j * P:(j + 1) * P], PQT[:, 4 * q + j, t * P:(t + 1) * P], KEYT[:, 4 * q + j, :],
                                       start=True, stop=True)
                    mm.then_inc(aux_done, 1)

                for k in range(KC):
                    if k == 1:
                        pe.wait_ge(pq_ready, l * 2 + 1)
                    if k in (1, 2):
                        for n in range(4):
                            query(X_QA, 4 * (k - 1) + n)
                    if k == 3:
                        pe.wait_ge(pqt_ready, l * 2 + 1)
                        pe.wait_ge(keys_landed, l * 16 + 16)
                    if 3 <= k < 6:
                        for n in range(2):
                            score(X_SA, 0, 2 * (k - 3) + n)
                    unit(U_Q + KC + k, (LTh, LTl), k, C_Q + 6, k == 0, k == KC - 1)
                pe.wait_ge(pq_ready, l * 2 + 2)
                for k in range(8, 16):
                    query(X_QB, k)
                pe.wait_ge(pqt_ready, l * 2 + 2)
                for n in range(6):
                    score(X_SB, 1, n)
                if not last:
                    modulation(l + 1, l * FREES + C_NEXT - C_IN, l * FREED, X_NEXT)
                else:
                    pe.drain().then_inc(acc_done, 12)
                    pe.drain().then_inc(aux_done, 2)
                for t in range(TB):
                    if t < TB - 1:
                        pe.wait_ge(index_ready, l * (TB - 1) + t + 1)
                    pe.wait_ge(sel_ready, l * TB + t + 1)
                    b = bank(X_IT + t)
                    for q in range(3):
                        mm = pe.transpose(b[:, q * P:(q + 1) * P], SELf[:, t, q, :], ident[:])
                    mm.then_inc(aux_done, 1)
                with pe.Fori(0, T // (2 * GT)) as g:
                    for j in range(2 * GT):
                        n = j // 4
                        use = X_G + n
                        if j % 4 == 0:
                            pe.wait_ge(aux_free, l * FREED + g * 8 + use + 1)
                            if n % 2 == 0:
                                pe.wait_ge(hot1_ready, l * (T // 8) + g * 4 + n // 2 + 1)
                            if n in BY_ACT:
                                pe.wait_ge(hot3_ready, l * (T // GT) + g * 2 + BY_ACT.index(n) + 1)
                            if n in BY_POOL:
                                pe.wait_ge(hot2_ready, l * (T // (2 * GT) * len(BY_POOL)) + g * len(BY_POOL) + BY_POOL.index(n) + 1)
                        mm = pe.matmul(aux[use % 2][:, (j % 4) * P:(j % 4 + 1) * P], HOT1[:, j % 32, :], HOT2[:, j % 16, :],
                                       start=True, stop=True)
                        if j % 4 == 3:
                            mm.then_inc(aux_done, 1)
                if not last:
                    pe.wait_ge(modr_ready, l * 12 + 24)
                for b in range(6):
                    pe.wait_ge(acc_free, l * FREES + C_NEXT - C_IN + b + 1)

                def experts(k, first, last):
                    for j in range(2):
                        pe.wait_ge(lo_ready, l * UNITS + k * 4 + U_PEER + j + 1 + SLOTS)
                        if first:
                            pe.wait_ge(aux_free, l * FREED + X_U + j + 1)
                        else:
                            pe.wait_ge(act_ready, l * KEYS + k * 2 + j - 1)
                        b = aux[(X_U + j) % 2]
                        for c in range(KC):
                            for n, (w, x) in enumerate(((whi, LTh), (whi, LTl), (wlo, LTh))):
                                mm = pe.matmul(b[:, 0:T], w[:, j, c * P:(c + 1) * P], x[:, c, :],
                                               start=(c == 0 and n == 0), stop=(c == KC - 1 and n == 2))
                        mm.then_inc(aux_done, 1)
                    for j in range(2):
                        pe.wait_ge(lo_ready, l * UNITS + k * 4 + U_PEER + 2 + j + 1 + SLOTS)
                        pe.wait_ge(w_ready, l * KEYS + k * 2 + j + 1 + GN + 1)
                        for h in range(2):
                            for t in range(TB):
                                wh, wl = (x[:, j, t * P:(t + 1) * P] for x in (BTh, BTl))
                                for n, (x, w) in enumerate(((wh, whi), (wh, wlo), (wl, whi))):
                                    mm = pe.matmul(accum(C_V + TB * h + t)[:], x, w[:, 2 + j, h * HB:(h + 1) * HB],
                                                   start=(first and j == 0 and n == 0), stop=(last and j == 1 and n == 2),
                                                   skip_group_check=True)
                                if last and j == 1:
                                    mm.then_inc(acc_done, 1)
                        (pe.drain() if last and j == 1 else mm).then_inc(unit_used, 1)

                experts(0, True, False)
                with pe.Fori(1, KEYS // 2 - 1) as k:
                    experts(k, False, False)
                experts(KEYS // 2 - 1, False, True)

            pe.wait_ge(silu_ready, 1)
            modulation(0, 0, 0, X_MOD)
            with pe.Fori(0, DEPTH - 1) as l:
                layer(l, False)
            layer(DEPTH - 1, True)

        @block.vector
        def _(dve):
            dve.memset(nhalf[:], -0.5)
            dve.memset(eps[:], EPS)
            dve.memset(one[:], 1.0)
            dve.memset(wpg[:], 0.0)
            dve.drain().then_inc(start_ready, 1)
            dve.sem_inc(acc_free, 6)
            dve.sem_inc(aux_free, 2)
            dve.sem_inc(layer_free, 1)
            dve.sem_inc(w_ready, GN + 1)
            dve.wait_ge(x_landed, 32)
            dve.wait_ge(silu_ready, 1)

            def normalise(n):
                for t in range(TB):
                    dve.wait_ge(rstd_ready, n * TB - TB + t + 1)
                    dve.tensor_scalar(XN[:, t], X[:, t], rstd[:, t:t + 1], None, ALU.mult)

            def modulation(n, aux0, x):
                dve.wait_ge(cols_landed, n * (16 * 7) + 16 * 7)
                for h in range(2):
                    dve.wait_ge(aux_done, aux0 + x + h + 1)
                    at = slice(3 * h, 3 * h + 3)
                    dve.tensor_tensor(modc[:, at], aux[(x + h) % 2][:, 0:6 * KC].rearrange("p (q k s) -> p q s k", q=3, s=2),
                                      bada[:, at, :].rearrange("p q (o k) -> p q o k", o=1).to_broadcast([P, 3, 2, KC]),
                                      ALU.add).then_inc(aux_free, 1)
                dve.drain()
                for m in range(2):
                    for s in range(2):
                        dve.scalar_tensor_tensor(modc[:, 3 * m + 1, s, :], modc[:, 3 * m + 1, s, :], 1.0, gcol[:, m, :],
                                                 ALU.add, ALU.mult)
                dve.drain().then_inc(mods_ready, 1)

            def layer(l, last):
                def bank(use):
                    dve.wait_ge(aux_done, l * AUXS + use + 1)
                    return aux[use % 2]

                def accu(use):
                    dve.wait_ge(acc_done, l * ACCS + use + 1)
                    return accum(use)

                def split(h, lo, src):
                    dve.tensor_copy(h, src)
                    dve.drain()
                    return dve.tensor_tensor(lo, src, h.bitcast(F32), ALU.subtract)

                def columns(base, chunks, evacuate):
                    for k in range(KC + 2):
                        if k < KC:
                            evacuate(k, bank(base + k)).then_inc(aux_free, 1)
                        if 1 <= k <= KC:
                            dve.tensor_copy(LTh[:, k - 1], chunks[:, k - 1])
                        if k >= 2:
                            dve.tensor_tensor(LTl[:, k - 2], chunks[:, k - 2], LTh[:, k - 2].bitcast(F32), ALU.subtract)
                        x = dve.drain()
                        if k >= 2:
                            x.then_inc(ht_ready, 1)

                def modulate(n):
                    def step(k, b):
                        for s, (c0, c1) in enumerate(((0, P), (P, T))):
                            x = dve.tensor_scalar(HRAW[:, k, c0:c1], b[:, c0:c1], modc[:, 3 * n + 1, s, k:k + 1],
                                                  modc[:, 3 * n, s, k:k + 1], ALU.mult, ALU.add)
                        return x
                    return step

                def projected(use, n0):
                    for h in range(2):
                        for t in range(TB):
                            dve.tensor_copy(Z[:, t, n0 + h * HB:n0 + (h + 1) * HB], accu(use + TB * h + t)[:]).then_inc(acc_free, 1)

                columns(X_HT, HRAW, modulate(0))
                for g in range(2):
                    dve.tensor_copy(gate_r[:, g, :], bank(X_GATE + g)[0:2 * KC, 0:P]).then_inc(aux_free, 1)
                dve.drain().then_inc(rows_ready, 1)
                projected(C_IN, 0)
                projected(C_IN + 6, D)
                dve.drain().then_inc(z_ready, 1)
                dve.wait_ge(const_landed, 16 * 7)
                dve.wait_ge(att_landed, l * (16 * 6) + 16 * 6)
                bv = BIAS.rearrange("p b h (r n) -> p (b h r) n", r=4)
                dve.tensor_tensor(bv, bv, mask[:].rearrange("p (o n) -> p o n", o=1).to_broadcast([P, 2 * HEADS * 4, GRID]), ALU.add)
                dve.drain()

                def small(kind, i):
                    h, t = i // TB, i % TB
                    s, r = i % 2, 64 * (i // TB % 2)
                    b = bank(USE[kind, i])
                    if kind == "z":
                        if i < 2:
                            x = dve.tensor_copy(ZFT[:, i], b[:, 0:T])
                        elif i < 6:
                            x = dve.tensor_scalar(QT[:, i - 2], b[:, 0:T], DH ** -0.5, None, ALU.mult)
                        else:
                            x = dve.tensor_copy(KT[:, i - 6], b[:, 0:T])
                        x.then_inc(aux_free, 1)
                        if i in (1, 9):
                            dve.drain().then_inc(zf_ready if i == 1 else qk_ready, 1)
                    elif kind == "f":
                        dve.tensor_copy(ZCS[:, i].rearrange("p c n -> p (c n)"), b[:]).then_inc(aux_free, 1)
                        if i == 2:
                            dve.drain().then_inc(zcs_ready, 1)
                    elif kind == "p":
                        split(BTh[:, i], BTl[:, i], b[:, 0:T]).then_inc(aux_free, 1)
                    elif kind == "d":
                        dve.tensor_copy(DT[:, i], b[:, 0:T]).then_inc(aux_free, 1)
                        if i == 1:
                            dve.drain().then_inc(dt_ready, 1)
                    elif kind == "y":
                        dve.tensor_scalar(ZFT[:, i], b[:, 0:T], pscale[:, i:i + 1], None, ALU.mult).then_inc(aux_free, 1)
                        dve.drain()
                        split(BTh[:, 6 + i], BTl[:, 6 + i], ZFT[:, i])
                        if i == 1:
                            dve.drain().then_inc(four_done, 1)
                    elif kind == "s":
                        if t == 0:
                            dve.tensor_copy(S[:, s, 0:P], b[:, 0:P]).then_inc(aux_free, 1)
                        else:
                            dve.tensor_tensor(S[:, s, 0:256], b[:, 0:256], BIAS[:, t - 1, h, :], ALU.add)
                            dve.tensor_copy(S[:, s, 256:T], b[:, 256:T]).then_inc(aux_free, 1)
                        dve.drain()
                        dve.tensor_reduce(nmax[:, s:s + 1], S[:, s, 0:P if t == 0 else T], AX, ALU.max, negate=True).then_inc(s_ready, 1)
                    elif kind == "t":
                        n = 1 if t == 0 else 3
                        dve.tensor_copy(PT[:, s, 0:n, :].rearrange("p k q -> p (k q)"), b[:, 0:n * P]).then_inc(aux_free, 1)
                        dve.drain().then_inc(pt_ready, 1)
                    elif kind == "v":
                        at = (slice(r, r + 64), 2 + h // 2, slice(t * P, (t + 1) * P))
                        split(BTh[at], BTl[at], b[r:r + 64, 0:P]).then_inc(aux_free, 1)

                def probabilities(i):
                    s, n = i % 2, P if i % TB == 0 else T
                    dve.wait_ge(p_ready, l * STEPS + i + 1)
                    dve.reciprocal(rsum[:, s:s + 1], rsum[:, s:s + 1])
                    dve.drain()
                    dve.tensor_scalar(PR[:, s, 0:n], PR[:, s, 0:n], rsum[:, s:s + 1], None, ALU.mult).then_inc(pn_ready, 1)

                def gate(n, use):
                    dve.wait_ge(bgate_landed, l * 48 + 16 * (n + 1))
                    for h in range(2):
                        for t in range(TB):
                            g = GTB[:, t, h * HB:(h + 1) * HB]
                            dve.tensor_tensor(g, g, accu(use + TB * h + t)[:], ALU.add).then_inc(acc_free, 1)
                        dve.drain().then_inc(gate_sum, 1)

                def merge(n, use):
                    if n == 0:
                        dve.wait_ge(kv_stored, l * 32 + 32)
                    for h in range(2):
                        dve.wait_ge(gate_ready, l * 6 + 2 * n + h + 1)
                        for t in range(TB):
                            g, m = (x[:, t, h * HB:(h + 1) * HB] for x in (GTB, M))
                            dve.tensor_tensor(g if n else m, g, accu(use + TB * h + t)[:], ALU.mult).then_inc(acc_free, 1)
                        if n:
                            dve.drain()
                            g, m = (x[:, :, h * HB:(h + 1) * HB] for x in (GTB, M))
                            dve.tensor_tensor(m, m, g, ALU.add)
                        x = dve.drain()
                        if n == 2:
                            x.then_inc(m_ready, 1)
                    if n < 2:
                        x.then_inc(gtb_free, 1)

                for i in range(U_OUT - U_GF):
                    u = U_GF + i
                    for half in range(2):
                        for kind, j in BESIDE[2 * i + half]:
                            small(kind, j)
                        for kind, j in BESIDE[2 * i + half]:
                            if kind == "s":
                                probabilities(j)
                    if u == U_WA - 1:
                        dve.drain().then_inc(att_done, 1)
                    for u1, what, n, use in ((U_WF, gate, 0, C_GF), (U_GP, merge, 0, C_WF), (U_WP, gate, 1, C_GP),
                                             (U_GA, merge, 1, C_WP), (U_WA, gate, 2, C_GA), (U_OUT, merge, 2, C_WA)):
                        if u + 1 == u1:
                            what(n, use)
                columns(X_MT, MRAW, lambda k, b: dve.tensor_copy(MRAW[:, k], b[:, 0:T]))

                def residual(use, gates):
                    parts = [(h, t) for t in range(TB) for h in range(2)]
                    for n in range(7):
                        if n < 6:
                            h, t = parts[n]
                            dve.tensor_tensor(XTMP[:, n % 2], accu(use + TB * h + t)[:], gates[:, min(t, 1), h * HB:(h + 1) * HB],
                                              ALU.mult).then_inc(acc_free, 1)
                        if n:
                            h, t = parts[n - 1]
                            at = slice(h * HB, (h + 1) * HB)
                            dve.tensor_tensor(X[:, t, at], X[:, t, at], XTMP[:, (n - 1) % 2], ALU.add)
                        x = dve.drain()
                        if n in (2, 4, 6):
                            x.then_inc(x_ready, 1)

                dve.wait_ge(gate1_landed, l * 32 + 32)
                residual(C_OUT, Z[:, 0:2, D:2 * D])
                dve.sem_inc(out_done, 1)
                normalise(l * 2 + 2)
                dve.drain().then_inc(xn_ready, 1)
                columns(X_H2, HRAW, modulate(1))
                projected(C_Q, 0)
                dve.drain().then_inc(pq_ready, 1)

                def top16(rows):
                    for r in range(2):
                        for v, m, i in rows:
                            dve.max(m[:, 8 * r:8 * r + 8], v)
                        dve.drain()
                        for v, m, i in rows:
                            dve.max_index(i[:, 8 * r:8 * r + 8], m[:, 8 * r:8 * r + 8], v)
                        if r == 0:
                            dve.drain()
                            for v, m, i in rows:
                                dve.match_replace(v, m[:, 0:8], v, -3.0e38)
                            dve.drain()

                def top_keys(t, m):
                    dve.wait_ge(scores_ready, l * (2 * TB) + m * TB + t + 1)
                    top16([(Z[:, t, k * P:(k + 1) * P], SV[:, t, k, :], SI[:, t, k, :]) for k in range(8 * m, 8 * m + 8)])
                    dve.drain()

                for t in range(2):
                    top_keys(t, 0)
                projected(C_Q + 6, D)
                dve.drain().then_inc(pq_ready, 1)
                top_keys(2, 0)

                def gates(t):
                    g = SEL[:, t, 2]
                    dve.wait_ge(exp_ready, l * TB + t + 1)
                    dve.tensor_reduce(hsum[:], g, AX, ALU.add)
                    dve.drain()
                    dve.reciprocal(hsum[:], hsum[:])
                    dve.drain()
                    dve.tensor_tensor(g, g, hsum[:].rearrange("p (h o) -> p h o", o=1).to_broadcast([P, HEADS, TOPK]), ALU.mult)
                    dve.drain().then_inc(sel_ready, 1)

                def selected(t):
                    b = bank(X_IT + t)
                    dve.tensor_copy(SELT[:, :, t * P:(t + 1) * P], b[:, 0:3 * P].rearrange("p (q t) -> p q t", q=3)).then_inc(aux_free, 1)
                    dve.drain()

                for t in range(TB):
                    s = t % 2
                    top_keys(t, 1)
                    if t == 0:
                        dve.wait_ge(scores_ready, l * (2 * TB) + 2 * TB)
                    if t >= 2:
                        dve.wait_ge(index_ready, l * (TB - 1) + t - 1)
                    dve.tensor_copy(SIF[:, s].rearrange("p h q k -> p (h q) k"), SI[:, t])
                    sv = SV[:, t].rearrange("p (h q) k -> p h q k", q=2)
                    for a0, a1, at, width in ((0, ROW_SPLIT, 0, TOPK), (ROW_SPLIT, TOPK, ROW_SPLIT * TOPK, ROW_SPLIT)):
                        n = (a1 - a0) * width
                        dve.tensor_tensor(CAND[:, :, at:at + n].rearrange("p h (a b) -> p h a b", b=width),
                                          sv[:, :, 0, a0:a1].rearrange("p h (a o) -> p h a o", o=1).to_broadcast([P, HEADS, a1 - a0, width]),
                                          sv[:, :, 1, 0:width].rearrange("p h (o b) -> p h o b", o=1).to_broadcast([P, HEADS, a1 - a0, width]),
                                          ALU.add)
                    dve.drain()
                    top16([(CAND[:, h], TOP[:, h, :], POS[:, h, :]) for h in range(HEADS)])
                    dve.drain()
                    pos = POS.rearrange("p h k -> p (h k)")
                    dve.tensor_scalar(PLACE1[:, 0], pos, 4, None, ALU.logical_shift_right)
                    dve.tensor_scalar(PLACE1[:, 1], pos, TOPK - 1, None, ALU.bitwise_and)
                    dve.tensor_scalar(PLACE2[:, 0], pos, 2, None, ALU.logical_shift_right)
                    dve.tensor_scalar(PLACE2[:, 1], pos, ROW_SPLIT - 1, None, ALU.bitwise_and)
                    dve.tensor_tensor(SEL[:, t, 2], TOP, TOP[:, :, 0:1].to_broadcast([P, HEADS, TOPK]), ALU.subtract)
                    dve.drain().then_inc(top_ready, 1)
                    dve.tensor_scalar(FAR_ROW, PLACE1[:, 0], float(ROW_SPLIT), None, ALU.is_ge)
                    dve.scalar_tensor_tensor(PABf[:, s, 0], PLACE2[:, 0], float(ROW_SPLIT - TOPK),
                                             PLACE1[:, 0], ALU.add, ALU.subtract)
                    dve.tensor_tensor(PABf[:, s, 1], PLACE2[:, 1], PLACE1[:, 1], ALU.subtract)
                    dve.drain()
                    dve.tensor_tensor(PABf[:, s], PABf[:, s], FAR_ROW.rearrange("p (o m) -> p o m", o=1).to_broadcast([P, 2, P]), ALU.mult)
                    dve.drain()
                    dve.tensor_tensor(PABf[:, s], PABf[:, s], PLACE1, ALU.add)
                    dve.drain()
                    if t:
                        dve.wait_ge(index_ready, l * (TB - 1) + t)
                    for q in range(2):
                        place = PAB[:, s, q].rearrange("p h (k o) -> p h k o", o=1).to_broadcast([P, HEADS, TOPK, TOPK])
                        number = iota[:, 0:TOPK].rearrange("p (x y a) -> p x y a", x=1, y=1).to_broadcast([P, HEADS, TOPK, TOPK])
                        dve.tensor_tensor(OH[q], place, number, ALU.is_equal)
                    if t < TB - 1:
                        dve.drain().then_inc(place_ready, 1)
                    else:
                        dve.drain()
                        for q in range(2):
                            index = SIF[:, s, :, q, :].rearrange("p h (o a) -> p h o a", o=1).to_broadcast([P, HEADS, TOPK, TOPK])
                            dve.tensor_tensor(OH[q], OH[q], index, ALU.mult)
                        dve.drain()
                        for q in range(2):
                            dve.tensor_reduce(SEL[:, t, q], OH[q], AX, ALU.add)
                    if t:
                        gates(t - 1)
                if not last:
                    modulation(l + 1, l * AUXS, X_NEXT)
                else:
                    dve.sem_inc(aux_free, 2)
                selected(0)
                gates(TB - 1)
                for t in range(1, TB):
                    selected(t)
                with dve.Fori(0, T // (2 * GT)) as g:
                    for m in range(4):
                        s = m // 2
                        mine = [n for n in (2 * m, 2 * m + 1) if n not in BY_POOL + BY_ACT]
                        if m % 2 == 0:
                            dve.wait_ge(aux_done, l * AUXS + g * 8 + X_G + 4 * s - 3)
                            dve.tensor_copy(SELC[:, s], SELT[:, :, bass.ds(g * (2 * GT) + s * GT, GT)])
                            dve.drain().then_inc(selc_ready, 1)
                        dve.wait_ge(aux_done, l * AUXS + g * 8 + X_G + (mine[-1] - 3 if mine else 2 * m - 6))
                        for j in range(8 * m, 8 * m + 8):
                            i1, gg = (SELC[:, s, q, j % GT:j % GT + 1] for q in (0, 2))
                            dve.tensor_scalar(HOT1[:, j, :], iota[:], i1, gg, ALU.is_equal, ALU.mult)
                        for n in mine:
                            at = 4 * (n % 4)
                            dve.tensor_tensor(HOT2[:, at:at + 4, :], iota[:].rearrange("p (o n) -> p o n", o=1).to_broadcast([P, 4, P]),
                                              SELC[:, s, 1, at:at + 4].rearrange("p (t o) -> p t o", o=1).to_broadcast([P, 4, P]),
                                              ALU.is_equal)
                        dve.drain().then_inc(hot1_ready, 1)
                with dve.Fori(0, KEYS // BODY) as i:
                    for n in range(BODY):
                        j, s = n % 2, n // GN
                        if n % GN == 0:
                            dve.wait_ge(group_landed[s], l * (8 * GGROUPS) + i * 16 + 16)
                        dve.wait_ge(act_ready, l * KEYS + i * BODY + n + 1)
                        dve.tensor_tensor(ACTB[:, j], ACTB[:, j], GCH[:, s, :, n % GN], ALU.mult)
                        dve.drain()
                        dve.wait_ge(unit_used, l * USED + i * BODY + U_PEER + n - 1 + SLOTS)
                        split(BTh[:, j], BTl[:, j], ACTB[:, j]).then_inc(w_ready, 1)
                dve.wait_ge(gate2_landed, l * 32 + 32)
                residual(C_V, GATE2)
                normalise(l * 2 + 3)
                dve.drain().then_inc(xn_ready, 1)
                dve.sem_inc(layer_free, 1)

            normalise(1)
            dve.drain().then_inc(xn_ready, 1)
            modulation(0, 0, X_MOD)
            with dve.Fori(0, DEPTH - 1) as l:
                layer(l, False)
            layer(DEPTH - 1, True)
            dve.wait_ge(gfin_landed, 16)
            for t in range(TB):
                dve.tensor_tensor(X[:, t], XN[:, t], GFIN, ALU.mult)
            dve.drain().then_inc(y_ready, 1)


def _constants():
    import numpy as np

    ident = np.eye(P, dtype=np.float32)
    iota = np.tile(np.arange(P, dtype=np.float32), (P, 1))
    qc = np.arange(P)[:, None] % GRID
    kc = np.arange(GRID)[None, :]
    start = np.clip(qc - 8, 0, GRID - 16)
    mask = np.where((kc >= start) & (kc < start + 16), 0.0, -1e30).astype(np.float32)

    def dft(n):
        angle = 2 * np.pi * (np.outer(np.arange(n), np.arange(n)) % n) / n
        return np.cos(angle) / np.sqrt(n), np.sin(angle) / np.sqrt(n)

    c64, s64 = dft(64)
    dft_c = np.zeros((P, 256))
    for g in range(2):
        dft_c[64 * g:64 * g + 64, 64 * g:64 * g + 64] = c64
        dft_c[64 * g:64 * g + 64, P + 64 * g:P + 64 * g + 64] = s64
    c, s = dft(128)
    dft_p = np.stack([c, -s], axis=1)
    c, s = dft(256)
    dft_s = np.stack([c, -s], axis=1).reshape(2, P, 2, 256).transpose(1, 0, 2, 3)

    def pool(n):
        out = np.zeros((n, 4, n))
        for g, w in enumerate((2, 4, 8, 16)):
            for t in range(n):
                a, b = max(t - w // 2, 0), min(t + w // 2, n)
                out[a:b, g, t] = 1.0 / (b - a)
                out[t, g, t] -= 1.0
        return out

    pool_p = pool(128)
    pool_s = pool(256).reshape(2, P, 4, 256).transpose(1, 0, 2, 3)
    tables = dict(ident=ident, iota=iota, mask=mask, dft_c=dft_c, dft_p=dft_p, dft_s=dft_s, pool_p=pool_p, pool_s=pool_s)
    return {k: np.ascontiguousarray(v, dtype=np.float32) for k, v in tables.items()}


_OUTS = {"y_prompt": (128, D), "y_sample": (256, D), "new_k": (DEPTH, HEADS, 128, DH), "new_v": (DEPTH, HEADS, 128, DH)}


def kernel(**inputs):
    import numpy as np
    import concourse.bacc as bacc
    from concourse.bass_utils import run_bass_kernel_spmd as run

    x = {k: np.asarray(v) for k, v in inputs.items()}
    arrays = dict(_constants())
    arrays["x_prompt"] = x["x_prompt"].reshape(128, D)
    arrays["x_sample"] = x["x_sample"].reshape(256, D)
    arrays["cond"] = np.stack([x["c_ctx"].reshape(KC, P), x["c"].reshape(KC, P)]).transpose(2, 0, 1)
    arrays["bada"] = x["b_ada"].reshape(DEPTH, 6, KC, P).transpose(0, 3, 1, 2)
    arrays["gcol"] = np.stack([x["g_attn"].reshape(DEPTH, KC, P), x["g_ffn"].reshape(DEPTH, KC, P)], axis=1).transpose(0, 3, 1, 2)
    arrays["pool_scale"] = x["pool_scale"].reshape(DEPTH, 2, P).transpose(0, 2, 1)
    arrays["b_gate"] = x["b_gate"].reshape(DEPTH, 3, D)
    for name in ("w_ada", "w_in", "w_fourier", "w_pool_grp", "w_pool", "w_attn", "w_gate", "w_out", "peer_wq", "rel_bias"):
        arrays[name] = x[name]
    arrays["cache_k"] = x["cache_k"][0].reshape(DEPTH, 4, 2, 128, DH).transpose(0, 2, 4, 1, 3).reshape(DEPTH, P, 4, 128)
    arrays["cache_v"] = x["cache_v"][0]
    arrays["keys"] = x["peer_keys"].transpose(0, 4, 1, 2, 3).reshape(DEPTH, P, 16, KEYS)
    arrays["ut"] = x["peer_u"].reshape(DEPTH, KEYS, KEYS, KC, P).transpose(0, 2, 4, 3, 1).reshape(DEPTH * KEYS, P, KC * KEYS)
    arrays["peer_v"] = x["peer_v"].reshape(DEPTH * KEYS, KEYS, D)
    arrays["g_final"] = x["g_final"].reshape(1, D)
    arrays = {k: np.ascontiguousarray(v) for k, v in arrays.items()}

    nc = bacc.Bacc("TRN2", target_bir_lowering=False, num_devices=1)
    a = {k: nc.dram_tensor("in_" + k, v.shape, F32, kind="ExternalInput").ap() for k, v in arrays.items()}
    o = {k: nc.dram_tensor("out_" + k, shape, F32, kind="ExternalOutput").ap() for k, shape in _OUTS.items()}
    build(nc, a, o)
    r = run(nc, [{"in_" + k: v for k, v in arrays.items()}], core_ids=[0]).results[0]
    return (r["out_y_prompt"].reshape(1, 128, D), r["out_y_sample"].reshape(1, 256, D),
            r["out_new_k"].reshape(1, DEPTH, HEADS, 128, DH), r["out_new_v"].reshape(1, DEPTH, HEADS, 128, DH))
```
